# Optimizing a Trainium2 kernel written in Bass

```python
import math
import jax
import jax.numpy as jnp
from jax import lax
import numpy as np

D_MODEL = 1024
BATCH = 1
SEQ = 256
DEPTH = 1
DEC_BATCH = 8
DEC_SEQ = 4
PAST_LEN = 2048
PAGE_SIZE = 128

GDN_HEADS = 4
GDN_DK = 128
GDN_DV = 128
GDN_CONV = 4
GDN_CHUNK = 64
GDN_QK = GDN_HEADS * GDN_DK
GDN_V = GDN_HEADS * GDN_DV
GDN_CONV_CH = 2 * GDN_QK + GDN_V
MOBA_HEADS = 8
MOBA_HD = 64
MOBA_BLOCK = 256
MOBA_TOPK = 3
Q_BLOCK = 32
MOBA_W = MOBA_HEADS * MOBA_HD
MIX_W = GDN_V + MOBA_W
IN_W = GDN_CONV_CH + 2 * GDN_HEADS + GDN_V + 3 * MOBA_W
D_FF = ((8 * D_MODEL // 3) + 127) // 128 * 128
N_MOD = 9
EPS = 1e-6

kernel_name = "hymba_gdn_moba_macaron_adaln_step"

def rmsnorm(x, w):
    xf = x.astype(jnp.float32)
    y = xf * lax.rsqrt(jnp.mean(xf * xf, axis=-1, keepdims=True) + EPS)
    return (y * w.astype(jnp.float32)).astype(x.dtype)

def l2norm(x):
    xf = x.astype(jnp.float32)
    return xf * lax.rsqrt(jnp.sum(xf * xf, axis=-1, keepdims=True) + EPS)

def swiglu(x, w_up, w_down):
    gate, up = jnp.split(x @ w_up, 2, axis=-1)
    return (jax.nn.silu(gate) * up) @ w_down

def alibi_slopes():
    return jnp.exp2(-8.0 * jnp.arange(1, MOBA_HEADS + 1, dtype=jnp.float32) / MOBA_HEADS)

def causal_dwconv(xc, w):
    return lax.conv_general_dilated(
        xc, w[:, None, :].astype(xc.dtype), window_strides=(1,), padding="VALID",
        dimension_numbers=("NWC", "WIO", "NWC"), feature_group_count=xc.shape[-1])

def gated_delta_rule(q, k, v, g, beta, s0):
    b, t_len, h, _ = q.shape
    dv = v.shape[-1]
    c = GDN_CHUNK
    pad = (-t_len) % c

    def prep(a):
        a = a.astype(jnp.float32)
        a = jnp.pad(a, [(0, 0), (0, pad)] + [(0, 0)] * (a.ndim - 2))
        a = a.reshape((b, a.shape[1] // c, c) + a.shape[2:])
        return jnp.moveaxis(a, (1, 3), (0, 2))

    qc, kc, vc, gc, bc = prep(q), prep(k), prep(v), prep(g), prep(beta)
    gcum = jnp.cumsum(gc, axis=-1)
    pos = jnp.arange(c)
    causal = pos[:, None] >= pos[None, :]
    strict = pos[:, None] > pos[None, :]
    decay = jnp.exp(jnp.where(causal, gcum[..., :, None] - gcum[..., None, :], -jnp.inf))
    kb = kc * bc[..., None]
    m = jnp.where(strict, jnp.einsum("nbhtd,nbhsd->nbhts", kb, kc) * decay, 0.0)
    a_mat = m + jnp.eye(c, dtype=jnp.float32)
    rhs = jnp.concatenate([vc * bc[..., None], kb * jnp.exp(gcum)[..., None]], axis=-1)
    sol = lax.linalg.triangular_solve(a_mat, rhs, left_side=True, lower=True, unit_diagonal=True)
    u, w = sol[..., :dv], sol[..., dv:]
    attn = jnp.einsum("nbhtd,nbhsd->nbhts", qc, kc) * decay
    q_dec = qc * jnp.exp(gcum)[..., None]
    g_last = gcum[..., -1]
    k_dec = kc * jnp.exp(g_last[..., None] - gcum)[..., None]

    def step(s, inp):
        u_i, w_i, attn_i, qd_i, kd_i, gl_i = inp
        v_new = u_i - jnp.einsum("bhcd,bhde->bhce", w_i, s)
        o = jnp.einsum("bhcd,bhde->bhce", qd_i, s) + jnp.einsum("bhts,bhse->bhte", attn_i, v_new)
        s = s * jnp.exp(gl_i)[..., None, None] + jnp.einsum("bhcd,bhce->bhde", kd_i, v_new)
        return s, o

    s_fin, o = lax.scan(step, s0.astype(jnp.float32), (u, w, attn, q_dec, k_dec, g_last))
    o = jnp.moveaxis(o, (0, 2), (1, 3)).reshape(b, -1, h, dv)[:, :t_len]
    return o, s_fin

def own_block_logits(q, k_own, t, s, slopes):
    dist = (t[:, None] - s[None, :]).astype(jnp.float32)
    lg = jnp.einsum("bqhd,bkhd->bqhk", q, k_own.astype(q.dtype), preferred_element_type=jnp.float32)
    lg = lg - slopes[None, None, :, None] * dist[None, :, None, :]
    return jnp.where(dist[None, :, None, :] >= 0, lg, -jnp.inf)

def selected_logits(q, k_sel, t, idx, slopes):
    s = idx[..., None] * MOBA_BLOCK + jnp.arange(MOBA_BLOCK)
    dist = (t[None, :, None, None, None] - s).astype(jnp.float32)
    lg = jnp.einsum("bqhd,bqhnkd->bqhnk", q, k_sel.astype(q.dtype), preferred_element_type=jnp.float32)
    return lg - slopes[None, None, :, None, None] * dist

def attend_merged(l_sel, v_sel, l_own, v_own):
    if l_sel is None:
        p = jax.nn.softmax(l_own, axis=-1).astype(v_own.dtype)
        return jnp.einsum("bqhk,bkhd->bqhd", p, v_own)
    b, q, h, n, k1 = l_sel.shape
    p = jax.nn.softmax(jnp.concatenate([l_sel.reshape(b, q, h, n * k1), l_own], axis=-1), axis=-1)
    p_sel = p[..., : n * k1].reshape(b, q, h, n, k1).astype(v_sel.dtype)
    p_own = p[..., n * k1:].astype(v_own.dtype)
    return (jnp.einsum("bqhnk,bqhnkd->bqhd", p_sel, v_sel)
            + jnp.einsum("bqhk,bkhd->bqhd", p_own, v_own.astype(v_sel.dtype)))

def moba_prompt(q, k, v):
    b, t_len, h, hd = q.shape
    nb = -(-t_len // MOBA_BLOCK)
    pad = nb * MOBA_BLOCK - t_len
    kp = jnp.pad(k, ((0, 0), (0, pad), (0, 0), (0, 0)))
    vp = jnp.pad(v, ((0, 0), (0, pad), (0, 0), (0, 0)))
    kblk = kp.reshape(b, nb, MOBA_BLOCK, h, hd)
    vblk = vp.reshape(b, nb, MOBA_BLOCK, h, hd)
    kmean = jnp.mean(kblk.astype(jnp.float32), axis=2)
    n_sel = min(MOBA_TOPK, (t_len - 1) // MOBA_BLOCK)
    slopes = alibi_slopes()
    bi = jnp.arange(b)[:, None, None, None]
    hi = jnp.arange(h)[None, None, :, None]
    nq = t_len // Q_BLOCK
    qb = q.reshape(b, nq, Q_BLOCK, h, hd).transpose(1, 0, 2, 3, 4)

    def one_block(args):
        i, qi = args
        q0 = i * Q_BLOCK
        j = q0 // MOBA_BLOCK
        t = q0 + jnp.arange(Q_BLOCK)
        k_own = lax.dynamic_slice_in_dim(kp, j * MOBA_BLOCK, MOBA_BLOCK, axis=1)
        v_own = lax.dynamic_slice_in_dim(vp, j * MOBA_BLOCK, MOBA_BLOCK, axis=1)
        l_own = own_block_logits(qi, k_own, t, j * MOBA_BLOCK + jnp.arange(MOBA_BLOCK), slopes)
        if n_sel == 0:
            return attend_merged(None, None, l_own, v_own)
        gate = jnp.einsum("bqhd,bnhd->bqhn", qi.astype(jnp.float32), kmean)
        gate = jnp.where(jnp.arange(nb) < j, gate, -jnp.inf)
        _, idx = lax.top_k(gate, n_sel)
        k_sel = kblk[bi, idx, :, hi, :]
        v_sel = vblk[bi, idx, :, hi, :]
        l_sel = selected_logits(qi, k_sel, t, idx, slopes)
        l_sel = jnp.where((idx < j)[..., None], l_sel, -jnp.inf)
        return attend_merged(l_sel, v_sel, l_own, v_own)

    out = lax.map(one_block, (jnp.arange(nq), qb))
    return out.transpose(1, 0, 2, 3, 4).reshape(b, t_len, h, hd)

def moba_sample(q, k, v, cache_k, cache_v, page_table):
    b, ds, h, hd = q.shape
    past = page_table.shape[1] * PAGE_SIZE
    ppb = MOBA_BLOCK // PAGE_SIZE
    j = past // MOBA_BLOCK
    own_start = j * MOBA_BLOCK
    slopes = alibi_slopes()
    t = past + jnp.arange(ds)
    k_own, v_own = k, v
    if past > own_start:
        own_pages = page_table[:, own_start // PAGE_SIZE:]
        k_own = jnp.concatenate([cache_k[own_pages].reshape(b, -1, h, hd).astype(k.dtype), k], axis=1)
        v_own = jnp.concatenate([cache_v[own_pages].reshape(b, -1, h, hd).astype(v.dtype), v], axis=1)
    l_own = own_block_logits(q, k_own, t, own_start + jnp.arange(k_own.shape[1]), slopes)
    n_sel = min(MOBA_TOPK, j)
    if n_sel == 0:
        return attend_merged(None, None, l_own, v_own)
    k_full = cache_k[page_table[:, : j * ppb]].reshape(b, j, MOBA_BLOCK, h, hd)
    kmean = jnp.mean(k_full.astype(jnp.float32), axis=2)
    gate = jnp.einsum("bqhd,bnhd->bqhn", q.astype(jnp.float32), kmean)
    _, idx = lax.top_k(gate, n_sel)
    lpage = idx[..., None] * ppb + jnp.arange(ppb)
    phys = page_table[jnp.arange(b)[:, None, None, None, None], lpage]
    hi = jnp.arange(h)[None, None, :, None, None]
    k_sel = cache_k[phys, :, hi, :].reshape(b, ds, h, n_sel, MOBA_BLOCK, hd)
    v_sel = cache_v[phys, :, hi, :].reshape(b, ds, h, n_sel, MOBA_BLOCK, hd).astype(v.dtype)
    l_sel = selected_logits(q, k_sel, t, idx, slopes)
    return attend_merged(l_sel, v_sel, l_own, v_own)

def token_mixing(hn, conv_state, s0, attend, w_in, conv_w, a_log, dt_bias, gdn_norm_w, w_out):
    b, t_len, _ = hn.shape
    proj = hn @ w_in
    o1 = GDN_CONV_CH
    o2 = o1 + GDN_HEADS
    o3 = o2 + GDN_HEADS
    o4 = o3 + GDN_V
    qkv_pre, a, bb, z = proj[..., :o1], proj[..., o1:o2], proj[..., o2:o3], proj[..., o3:o4]
    mq, mk, mv = jnp.split(proj[..., o4:], 3, axis=-1)
    xc = jnp.concatenate([conv_state.astype(qkv_pre.dtype), qkv_pre], axis=1)
    new_conv = xc[:, -(GDN_CONV - 1):]
    qkv = jax.nn.silu(causal_dwconv(xc, conv_w))
    gq, gk, gv = jnp.split(qkv, [GDN_QK, 2 * GDN_QK], axis=-1)
    gq = l2norm(gq.reshape(b, t_len, GDN_HEADS, GDN_DK)) * (GDN_DK ** -0.5)
    gk = l2norm(gk.reshape(b, t_len, GDN_HEADS, GDN_DK))
    gv = gv.reshape(b, t_len, GDN_HEADS, GDN_DV)
    g_log = -jnp.exp(a_log.astype(jnp.float32)) * jax.nn.softplus(a.astype(jnp.float32) + dt_bias.astype(jnp.float32))
    beta = jax.nn.sigmoid(bb.astype(jnp.float32))
    go, s_new = gated_delta_rule(gq, gk, gv, g_log, beta, s0)
    go = rmsnorm(go, gdn_norm_w) * jax.nn.silu(z.reshape(b, t_len, GDN_HEADS, GDN_DV).astype(jnp.float32))
    go = go.astype(hn.dtype).reshape(b, t_len, GDN_V)
    mq = mq.reshape(b, t_len, MOBA_HEADS, MOBA_HD) * (MOBA_HD ** -0.5)
    mk = mk.reshape(b, t_len, MOBA_HEADS, MOBA_HD)
    mv = mv.reshape(b, t_len, MOBA_HEADS, MOBA_HD)
    mo = attend(mq, mk, mv).astype(hn.dtype).reshape(b, t_len, MOBA_W)
    out = jnp.concatenate([go, mo], axis=-1) @ w_out
    return out, s_new, new_conv, mk, mv

def trunk_layer(x, c, mixing, w_ada, b_ada, norm_w, ffn_up, ffn_down):
    mod = (jax.nn.silu(c) @ w_ada + b_ada).reshape(c.shape[0], N_MOD, 1, D_MODEL)
    sh1, sc1, g1, sh2, sc2, g2, sh3, sc3, g3 = [mod[:, i] for i in range(N_MOD)]
    h = x + 0.5 * g1 * swiglu(rmsnorm(x, norm_w[0]) * (1 + sc1) + sh1, ffn_up[0], ffn_down[0])
    mix_out, *state = mixing(rmsnorm(h, norm_w[1]) * (1 + sc2) + sh2)
    h = h + g2 * mix_out
    h = h + 0.5 * g3 * swiglu(rmsnorm(h, norm_w[2]) * (1 + sc3) + sh3, ffn_up[1], ffn_down[1])
    return h, state

def setup_inputs(seed: int = 0) -> dict:
    key = jax.random.key(seed)
    ks = jax.random.split(key, 24)
    f32 = jnp.float32

    def nrm(k, shape, s=1.0):
        return jax.random.normal(k, shape, f32) * s

    n_pages = PAST_LEN // PAGE_SIZE
    n_phys = (5 * DEC_BATCH * n_pages + 3) // 4
    perm = jax.random.permutation(ks[6], n_phys)
    page_table = perm[: DEC_BATCH * n_pages].reshape(DEC_BATCH, n_pages).astype(jnp.int32)
    dt = jnp.exp(jax.random.uniform(ks[16], (DEPTH, GDN_HEADS), f32, math.log(1e-3), math.log(1e-1)))
    return {
        "x_prompt": nrm(ks[0], (BATCH, SEQ, D_MODEL)),
        "x_sample": nrm(ks[1], (DEC_BATCH, DEC_SEQ, D_MODEL)),
        "c_prompt": nrm(ks[2], (BATCH, D_MODEL)),
        "c_sample": nrm(ks[3], (DEC_BATCH, D_MODEL)),
        "cache_k": nrm(ks[4], (DEPTH, n_phys, PAGE_SIZE, MOBA_HEADS, MOBA_HD)),
        "cache_v": nrm(ks[5], (DEPTH, n_phys, PAGE_SIZE, MOBA_HEADS, MOBA_HD)),
        "page_table": page_table,
        "state_gdn": nrm(ks[7], (DEPTH, DEC_BATCH, GDN_HEADS, GDN_DK, GDN_DV), 0.5),
        "state_conv": nrm(ks[8], (DEPTH, DEC_BATCH, GDN_CONV - 1, GDN_CONV_CH)),
        "w_ada": nrm(ks[9], (DEPTH, D_MODEL, N_MOD * D_MODEL), 0.5 * D_MODEL ** -0.5),
        "b_ada": nrm(ks[10], (DEPTH, N_MOD * D_MODEL), 0.1),
        "norm_w": 1.0 + nrm(ks[11], (DEPTH, 3, D_MODEL), 0.05),
        "ffn_up": nrm(ks[12], (DEPTH, 2, D_MODEL, 2 * D_FF), D_MODEL ** -0.5),
        "ffn_down": nrm(ks[13], (DEPTH, 2, D_FF, D_MODEL), D_FF ** -0.5),
        "w_in": nrm(ks[14], (DEPTH, D_MODEL, IN_W), D_MODEL ** -0.5),
        "conv_w": nrm(ks[17], (DEPTH, GDN_CONV, GDN_CONV_CH), GDN_CONV ** -0.5),
        "a_log": jnp.log(jax.random.uniform(ks[15], (DEPTH, GDN_HEADS), f32, 1.0, 16.0)),
        "dt_bias": dt + jnp.log(-jnp.expm1(-dt)),
        "gdn_norm_w": 1.0 + nrm(ks[18], (DEPTH, GDN_DV), 0.05),
        "w_out": nrm(ks[19], (DEPTH, MIX_W, D_MODEL), MIX_W ** -0.5),
        "final_norm_w": 1.0 + nrm(ks[20], (D_MODEL,), 0.05),
    }

def reference(x_prompt, x_sample, c_prompt, c_sample, cache_k, cache_v, page_table, state_gdn,
              state_conv, w_ada, b_ada, norm_w, ffn_up, ffn_down, w_in, conv_w, a_log, dt_bias,
              gdn_norm_w, w_out, final_norm_w):
    hp, hs = x_prompt, x_sample
    kp_l, vp_l, sp_l, cp_l, ks_l, vs_l, ss_l, cs_l = [], [], [], [], [], [], [], []
    for l in range(DEPTH):
        mix_w = (w_in[l], conv_w[l], a_log[l], dt_bias[l], gdn_norm_w[l], w_out[l])
        layer_w = (w_ada[l], b_ada[l], norm_w[l], ffn_up[l], ffn_down[l])
        conv0 = jnp.zeros((hp.shape[0], GDN_CONV - 1, GDN_CONV_CH), hp.dtype)
        s0 = jnp.zeros((hp.shape[0], GDN_HEADS, GDN_DK, GDN_DV), jnp.float32)
        hp, (s_p, c_p, k_p, v_p) = trunk_layer(
            hp, c_prompt, lambda hn: token_mixing(hn, conv0, s0, moba_prompt, *mix_w), *layer_w)
        ck, cv = cache_k[l], cache_v[l]
        sample_attend = lambda q, k, v: moba_sample(q, k, v, ck, cv, page_table)
        hs, (s_s, c_s, k_s, v_s) = trunk_layer(
            hs, c_sample, lambda hn: token_mixing(hn, state_conv[l], state_gdn[l], sample_attend, *mix_w), *layer_w)
        kp_l.append(k_p); vp_l.append(v_p); sp_l.append(s_p); cp_l.append(c_p)
        ks_l.append(k_s); vs_l.append(v_s); ss_l.append(s_s); cs_l.append(c_s)
    y_prompt = rmsnorm(hp, final_norm_w)
    y_sample = rmsnorm(hs, final_norm_w)
    k_prompt = jnp.stack(kp_l)
    v_prompt = jnp.stack(vp_l)
    gdn_prompt = jnp.stack(sp_l)
    conv_prompt = jnp.stack(cp_l)
    k_sample = jnp.stack(ks_l)
    v_sample = jnp.stack(vs_l)
    gdn_sample = jnp.stack(ss_l)
    conv_sample = jnp.stack(cs_l)
    return (y_prompt, y_sample, k_prompt, v_prompt, gdn_prompt, conv_prompt, k_sample, v_sample, gdn_sample, conv_sample)


_drawn_inputs = setup_inputs


def setup_inputs(seed=0):
    import zlib

    import numpy as np

    out = dict(_drawn_inputs(seed))
    spreads = {}
    factors = {'gdn_norm_w': 7.336}
    for name, (base, spread) in spreads.items():
        noise = np.random.default_rng([zlib.crc32(name.encode()), seed]).standard_normal(out[name].shape)
        drawn = base * np.exp(spread * noise) if base else spread * noise
        out[name] = jnp.asarray(drawn.astype(out[name].dtype))
    for name, factor in factors.items():
        out[name] = (out[name] * factor).astype(out[name].dtype)
    return out
```

```python
from contextlib import ExitStack

import numpy as np

import concourse.bass as bass
from concourse import mybir

F32 = mybir.dt.float32
I32 = mybir.dt.int32
ALU = mybir.AluOpType
ACT = mybir.ActivationFunctionType
AX_X = mybir.AxisListType.X

P = 128
D = 1024
KD = D // P
SEQ = 256
NB = 8
NT = 4
NS = NB * NT
TOK = SEQ + NS
F = 2816
FC = F // P
NMOD = 9
NR = 1 + NB
HG = 4
HM = 8
HD = 64
CONV = 4
CC = 12
XW = 3 + SEQ + NB * 7
YW = XW - 3
NPROB = 9
PAGE = 128
NPAGE = 16
NPHYS = 160
PAST = 2048
BLK = 256
NBLK = PAST // BLK
TOPK = 3
EPS = 1e-6
NEG = -1e30
RING = 4
KVR = 8
PHASE = NB * NBLK

UP_TILES = FC // 2
ADA_FIRST = 6
ADA_TILES = NMOD * D // 512


def const_layout():
    names = [("ident", P), ("ones", P), ("tri", P), ("later", P), ("triS", P), ("laterS", P),
             ("lev", 7 * P), ("mh8", P), ("lower8", 64), ("biasS", PAST), ("biasO", 64),
             ("dist", 3 * P), ("hmask", 512), ("selbt", 16), ("bdm", NB)]
    at, out = 0, {}
    for n, w in names:
        out[n] = (at, at + w)
        at += w
    return out, at


def make_consts():
    lay, width = const_layout()
    c = np.zeros((P, width), np.float32)
    i = np.arange(P)

    def put(name, value):
        a, b = lay[name]
        c[:, a:b] = value

    put("ident", np.eye(P))
    put("ones", 1.0)
    put("tri", i[:, None] <= i[None, :])
    put("later", i[:, None] > i[None, :])
    same = i[:, None] // NT == i[None, :] // NT
    put("triS", same & (i[:, None] <= i[None, :]))
    put("laterS", same & (i[:, None] > i[None, :]))
    lev = np.zeros((P, 7, P))
    for l in range(7):
        s, t = i[:, None], i[None, :]
        lev[:, l, :] = (s >> (l + 1) == t >> (l + 1)) & ((s >> l) % 2 == 0) & ((t >> l) % 2 == 1)
    put("lev", lev.reshape(P, -1))
    put("mh8", (i[:, None] % 4 == i[None, :] // NS) & (i[:, None] < 8))
    n, m = np.arange(64) // 8, np.arange(64) % 8
    put("lower8", np.broadcast_to(m < n, (P, 64)))
    h, t = (i % 32) // NT, i % NT
    slope = 2.0 ** -(h + 1.0)
    put("biasS", slope[:, None] * (np.arange(PAST)[None, :] - PAST - t[:, None]))
    own = np.zeros((P, 2, 32))
    for g in range(2):
        j = np.arange(32)
        ok = (j[None, :] // NT == 4 * g + i[:, None] // 32) & (j[None, :] % NT <= t[:, None])
        own[:, g, :] = np.where(ok, slope[:, None] * (j[None, :] % NT - t[:, None]), NEG)
    put("biasO", own.reshape(P, -1))
    d0 = np.where(i[None, :] <= i[:, None], i[None, :] - i[:, None], NEG)
    k = np.arange(SEQ)
    d1 = np.where(k[None, :] <= P + i[:, None], k[None, :] - P - i[:, None], NEG)
    put("dist", np.concatenate([d0, d1], 1))
    put("hmask", h[:, None] == np.arange(512)[None, :] // HD)
    put("selbt", (i[:, None] // 32) * NT + t[:, None] == np.arange(16)[None, :])
    put("bdm", ((i % NS) // NT)[:, None] == np.arange(NB)[None, :])
    return c


def build_program(nc, a, o):
    lay, cwidth = const_layout()
    with ExitStack() as ctx:
        def sb(name, shape, dt=F32):
            return ctx.enter_context(nc.sbuf_tensor(name, shape, dt))

        def sem(name):
            return ctx.enter_context(nc.semaphore(name))

        ps = [ctx.enter_context(nc.psum_tensor(f"bank{i}", [P, 512], F32)) for i in range(8)]

        const = sb("const", [P, cwidth])

        def cst(name):
            return const[:, lay[name][0]:lay[name][1]]

        def shaped(v, *shape):
            n = int(np.prod(shape))
            v = v[:, 0:n]
            if len(shape) == 2:
                v = v.rearrange("p (a b) -> p a b", a=shape[0])
            if len(shape) == 3:
                v = v.rearrange("p (a b c) -> p a b c", a=shape[0], b=shape[1])
            return v

        def carver(flat):
            at = [0]

            def take(*shape):
                n = int(np.prod(shape))
                assert at[0] + n <= flat.shape[1], (at, n)
                v = shaped(flat[:, at[0]:at[0] + n], *shape)
                at[0] += n
                return v
            return take

        wflat = sb("wring", [P, RING * 4096])
        wring = wflat[:, :].rearrange("p (s k n) -> p s k n", s=RING, k=8)
        kv = sb("kv", [P, KVR, 2, 512])
        h = sb("h", [P, KD, TOK])
        hn = sb("hn", [P, KD, TOK])
        mix = hn
        xsf = sb("xs", [P, KD * TOK])
        xs = shaped(xsf, KD, TOK)
        rstd = sb("rstd", [P, TOK])
        modT = sb("modT", [P, NMOD * KD, NR])
        coef = sb("coef", [P, KD, NR])
        gate = sb("gate", [P, KD, NR])
        samp = sb("samp", [P, 2, NB, NT])
        pvec = sb("pvec", [P, 153])
        eps = sb("eps", [P, 1])
        cT = sb("cT", [P, KD, 32])
        adaf = sb("adasb", [P, 1024])
        adasb = shaped(adaf, 2, 512)
        sgate = sb("sgate", [P, 2, TOK])
        region = sb("region", [P, 11952])
        ytok = shaped(region, 3, D)
        hid = shaped(region, FC, TOK)
        vown = sb("vown", [NS, 512])
        ptab = sb("ptab", [1, 2 * PHASE], I32)

        pro = carver(region)
        xin = pro(3, D)
        cin = pro(D)
        csil = pro(D)
        prow = pro(P)
        crow = pro(P)
        srow = pro(CC * P)

        reg = carver(region)
        XC = reg(CC, XW)
        Yb = reg(4, XW)
        Cv = reg(CC, TOK)
        mqT = reg(4, TOK)
        mkT = reg(4, TOK)
        mvT = reg(4, TOK)
        cst3 = sb("cst3", [P, CC, 24])
        z4 = carver(xsf)
        zs = z4(HG, TOK)
        goT = z4(HG, TOK)
        pa = carver(wflat)
        ktok = pa(3, 512)
        vtok = pa(3, 512)
        psS = pa(2, 384)
        psP = pa(2, 384)
        psT = pa(2, 384)
        cgat = pa(CC, 27)
        cout = pa(CC * P)
        patt = pa(32)
        gE = pa(2, P)
        sc8 = pa(5, TOK)
        gd = carver(wflat)
        SQ_AT = 3 * NPROB * P + 8 * TOK + 2 * NPROB * P
        RS_AT = SQ_AT + 3 * NPROB * P
        gR = gd(NPROB, P)
        EG = gd(NPROB, P)
        DT = gd(NPROB, P)
        QK = gd(8, TOK)
        AN = gd(NPROB, 2, P)
        KB = gd(NPROB, P)
        KDc = gd(NPROB, P)
        VB = gd(NPROB, P)
        X = gd(NPROB, P)
        XT = gd(NPROB, P)
        Pv = gd(NPROB, P)
        S1 = gd(HG, P)
        smp = gd(3, P)
        sq8 = shaped(wflat[:, SQ_AT:SQ_AT + 8 * TOK], 8, TOK)
        RS = shaped(wflat[:, RS_AT:RS_AT + 8 * TOK], 8, TOK)
        WQ = gd(HG * NB, 8)
        VN, WT, VX, NTl = X, Pv, gR, gR
        QD = shaped(DT.rearrange("p a b -> p (a b)"), NPROB, P)
        sqg = shaped(QK.rearrange("p a b -> p (a b)"), 8, TOK)
        st = shaped(region, HG, NB, P)
        gb = sb("gb", [P, 400])
        gsm = carver(gb)
        abT = sb("abT", [8, TOK])
        wab = sb("wab", [P, KD, 8])
        pab = sb("pab", [8, 4])
        GB = gsm(6, 8)
        G9 = gsm(NPROB)
        B9 = gsm(NPROB)
        cum = gsm(18)
        ecum = gsm(18)
        bek = gsm(NPROB)
        at_ = carver(region)
        S = at_(2, PAST)
        ktb = at_(2, 2, 512)
        pT = at_(2, 2, P)
        pex = at_(2, BLK)
        Om = at_(512)
        Qbd = shaped(adaf, 4, NB, 32)
        gts = at_(2, NBLK)
        bmx = at_(2, NBLK + 1)
        pen = at_(2, NBLK + 1)
        cmpA = at_(64)
        cmpB = at_(64)
        cnt = at_(NBLK)
        negm = at_(2)
        sown = at_(2, 32)
        pown = at_(2, 32)
        rsum = at_(2, NBLK + 1)
        rin = at_(8)
        ownT = at_(2, P)

        ident, ones, tri, later = cst("ident"), cst("ones"), cst("tri"), cst("later")
        triS, laterS = cst("triS"), cst("laterS")
        lev = shaped(cst("lev"), 7, P)
        bw = pvec[:, 0:NMOD * KD]
        nw = pvec[:, 72:104]
        gnw = pvec[:, 104:105]
        cw = pvec[:, 105:153]

        s_cst = sem("s_first_consts_landed")
        s_cst2 = sem("s_consts_landed")
        s_x = sem("s_x_landed")
        s_c = sem("s_c_landed")
        s_par = sem("s_params_landed")
        s_pab = sem("s_decay_params_landed")
        s_ini = sem("s_memsets")
        s_cs = sem("s_csilu")
        s_xT = sem("s_xT_psum")
        s_pT0 = sem("s_params_psum")
        s_cT = sem("s_cT_ready")
        s_w = [sem(f"s_w{i}_landed") for i in range(RING)]
        s_adamm = sem("s_ada_psum")
        s_adaev = sem("s_ada_copied")
        s_adaT = sem("s_ada_transposed")
        s_modr = sem("s_mod_reduced")
        s_mod = sem("s_mod_ready")
        s_h = sem("s_h_chunks")
        s_sq = sem("s_squares")
        s_ss = sem("s_sumsq_psum")
        s_ln = sem("s_ln")
        s_rstd = sem("s_rstd")
        s_hn = sem("s_hn_ready")
        s_gate = sem("s_gate_psum")
        s_up = sem("s_up_psum")
        s_silu = sem("s_silu")
        s_hid = sem("s_hidden")
        s_dpart = sem("s_down_tile_read")
        s_sub = sem("s_sublayer_psum")
        s_dve = sem("s_dve_chain")
        s_act = sem("s_act_chain")
        s_wab = sem("s_wab_landed")
        s_win = sem("s_win_psum")
        s_xc = sem("s_xc_copied")
        s_zm = sem("s_zqkv_copied")
        s_ab = sem("s_ab_copied")
        s_conv = sem("s_conv_taps")
        s_csil = sem("s_conv_silu")
        s_cg = sem("s_conv_rows")
        s_kvT = sem("s_kv_transposed")
        s_kvt = sem("s_kv_tokens")
        s_cvT = sem("s_convrows_transposed")
        s_cvo = sem("s_convrows_copied")
        s_sc = sem("s_scores_psum")
        s_paS = sem("s_scores_biased")
        s_nm = sem("s_row_max")
        s_pexp = sem("s_probs")
        s_pn = sem("s_probs_scaled")
        s_paT = sem("s_probsT_psum")
        s_pTe = sem("s_probsT_copied")
        s_pav = sem("s_attn_psum")
        s_pao = sem("s_attn_copied")
        s_out = sem("s_outputs")
        s_okv = sem("s_kv_outputs_done")
        s_g8 = sem("s_decay_rows")
        s_gT = sem("s_decay_psum")
        s_gp = sem("s_delta_psum")
        s_ge = sem("s_delta_copied")
        s_gbc = sem("s_decay_spread")
        s_ecum = sem("s_exp_cum")
        s_eg = sem("s_exp_rows")
        s_df = sem("s_decay_diff")
        s_dt = sem("s_decay_exp")
        s_qks = sem("s_qk_squares")
        s_rse = sem("s_qk_rstd")
        s_qkn = sem("s_qk_normalised")
        s_ntl = sem("s_level_masked")
        s_vx = sem("s_vnew_spread")
        s_st = sem("s_states_landed")
        s_go = sem("s_go_sq")
        s_gr = sem("s_go_rstd")
        s_gdn = sem("s_gdn_done")
        s_absx = sem("s_softplus_input")
        s_sp = sem("s_softplus_log")
        s_bmx = sem("s_block_max")
        s_qz = sem("s_qbd_zero")
        s_qbd = sem("s_qbd_ready")
        s_kv = [sem(f"s_kv{i}_landed") for i in range(KVR)]
        s_pt = sem("s_page_table")
        s_own = sem("s_own_psum")
        s_kt = sem("s_kt_psum")
        s_ktA = sem("s_kt_copied_act")
        s_ktD = sem("s_kt_copied_dve")
        s_qk = sem("s_logits_psum")
        s_lev = sem("s_logits_copied")
        s_pen = sem("s_selection")
        s_po = sem("s_own_probs")
        s_pe = sem("s_sel_probs")
        s_PT = sem("s_sel_probsT_psum")
        s_oT = sem("s_own_probsT_psum")
        s_pTs = sem("s_sel_probsT_copied")
        s_oTs = sem("s_own_probsT_copied")
        s_PV = sem("s_values_read")
        s_O = sem("s_sel_attn_psum")
        s_om = sem("s_sel_attn_scaled")
        s_AT = sem("s_sel_attnT_psum")
        s_mixa = sem("s_sel_attn_ready")
        s_yT = sem("s_y_transposed")
        s_y = sem("s_y_copied")
        block = ctx.enter_context(nc.Block())

        XCs = XC[:, :, 3 + SEQ:XW].rearrange("p c (b j) -> p c b j", b=NB)

        wada = a["w_ada"][0].rearrange("(k p) n -> p k n", p=P)
        wup = [a["ffn_up"][0, l].rearrange("(k p) (g n) -> p k g n", p=P, g=2) for l in range(2)]
        wdown = [a["ffn_down"][0, l].rearrange("(f p) n -> p f n", p=P) for l in range(2)]
        win = a["w_in"][0].rearrange("(k p) n -> p k n", p=P)
        wout = a["w_out"][0].rearrange("(k p) n -> p k n", p=P)
        WIN_COL = [0, 512, 1024, 1544, 2056, 2568, 3080]

        tiles = [("ada", j) for j in range(ADA_FIRST)] + [("up", 0, 0), ("ada", 6), ("ada", 7)]
        for i in range(5):
            tiles += [("up", 0, 1 + 2 * i), ("ada", 8 + 2 * i), ("up", 0, 2 + 2 * i), ("ada", 9 + 2 * i)]
        tiles += [("down", 0, g, t) for g in range(2) for t in range(3)]
        tiles += [("in", j) for j in range(7)]
        tiles += [("out", g) for g in range(2)]
        tiles += [("up", 1, j) for j in range(UP_TILES)]
        tiles += [("down", 1, g, t) for g in range(2) for t in range(3)]
        number = {t: n for n, t in enumerate(tiles)}

        def released(t):
            if t[0] == "ada":
                return s_adamm, t[1] + 1
            if t[0] == "up":
                return s_up, FC * t[1] + 2 * t[2] + 2
            if t[0] == "down":
                if t[3] < 2:
                    return s_dpart, 4 * t[1] + 2 * t[2] + t[3] + 1
                return s_sub, 16 * t[1] + 4 * t[2] + 4
            if t[0] == "in":
                return s_win, 4 * t[1] + 4
            return s_sub, 8 + 4 * t[1] + 4

        def halves(t, slot, j=None):
            w = wring[:, slot]
            if t[0] == "up":
                j = t[2] if j is None else j
                return [(w[:, :, 256 * g:256 * g + 256], wup[t[1]][:, :, g, bass.ds(j * 256, 256)]) for g in range(2)]
            if t[0] == "ada":
                j = t[1] if j is None else j
                return [(w[:, 4 * k:4 * k + 4, :], wada[:, 4 * k:4 * k + 4, bass.ds(j * 512, 512)]) for k in range(2)]
            if t[0] == "down":
                n = min(8, FC - 8 * t[3]) // 2
                return [(w[:, n * k:n * k + n, :], wdown[t[1]][:, 8 * t[3] + n * k:8 * t[3] + n * k + n, 512 * t[2]:512 * t[2] + 512]) for k in range(2)]
            c0 = WIN_COL[t[1]] if t[0] == "in" else 512 * t[1]
            src = win if t[0] == "in" else wout
            return [(w[:, 4 * k:4 * k + 4, :], src[:, 4 * k:4 * k + 4, c0:c0 + 512]) for k in range(2)]

        cache = [a["cache_k"][0].rearrange("n p h d -> n p (h d)"), a["cache_v"][0].rearrange("n p h d -> n p (h d)")]

        def steps():
            out = [("cum",)] + [("row", j) for j in range(3)] + [("l2", c) for c in range(8)]
            out += [("kt", j) for j in range(3)] + [("vt", j) for j in range(3)] + [("gram", j) for j in range(5)]
            for l in range(7):
                groups = range(3 if l < 2 else 2)
                out += [("P", l, g) for g in groups]
                for g in groups:
                    out += ([("XP", l, g)] if 0 < l < 6 else []) + [("PX", l, g)]
            out += [("W", 1), ("W", 2), ("U0",), ("S1",), ("V1",), ("o0",), ("o1",), ("S2",)]
            out += [("us",), ("ws",), ("vs",), ("os",)] + [("up", k) for k in range(8)] + [("rms", hh) for hh in range(HG)]
            return out

        STEPS = {t: k for k, t in enumerate(steps())}

        def copied(step):
            return s_ge, STEPS[step] + 1

        @block.sync
        def _(sp):
            sp.dma_start(const[:, 0:lay["mh8"][0]], a["consts"][:, 0:lay["mh8"][0]]).then_inc(s_cst, 16)

            def load(n):
                t = tiles[n]
                if n >= RING:
                    sp.wait_ge(*released(tiles[n - RING]))
                for dst, src in halves(t, n % RING):
                    sp.dma_start(dst, src).then_inc(s_w[n % RING], 16)

            def load_unit(v, table, which, sync):
                sp.wait_ge(*sync) if sync else None
                for y in range(2):
                    page = sp.value_load(ptab[0:1, bass.ds(table + y, 1)], min_val=0, max_val=NPHYS - 1)
                    sp.dma_start(kv[:, v, y, :], cache[which][bass.ds(page, 1), :, :].rearrange("a p n -> (a p) n"))\
                        .then_inc(s_kv[v], 16)

            for n in range(9 + 4):
                load(n)
                if n == 3:
                    sp.dma_start(const[:, lay["mh8"][0]:cwidth], a["consts"][:, lay["mh8"][0]:cwidth]).then_inc(s_cst2, 16)
            with sp.Fori(1, 5) as i:
                for k in range(4):
                    kind, slot = ("up", "ada", "up", "ada")[k], (9 + k) % RING
                    if kind == "up":
                        j = i * 2 + 1 + k // 2
                        sp.wait_ge(s_up, j * 2 - 2)
                        t = ("up", 0, 0)
                    else:
                        j = i * 2 + 8 + k // 2
                        sp.wait_ge(s_adamm, j - 1)
                        t = ("ada", 0)
                    for dst, src in halves(t, slot, j):
                        sp.dma_start(dst, src).then_inc(s_w[slot], 16)
            for n in range(29, 35):
                load(n)
            sp.wait_ge(s_pt, 16)
            for v in range(KVR):
                load_unit(v, 2 * v, 0, None)
            for n in range(35, 42):
                load(n)
            with sp.Fori(1, PHASE // KVR) as i:
                for v in range(KVR):
                    load_unit(v, i * (2 * KVR) + 2 * v, 0, (s_kt, i * 16 - 8 + 8 * (v // 4)) )
            sp.wait_ge(s_gdn, 1)
            sp.wait_ge(s_okv, 16 * 7)
            for n in range(42, 46):
                load(n)
            for v in range(KVR):
                load_unit(v, 2 * v, 1, (s_kt, 8 * (15 + v // 4)))
            with sp.Fori(1, PHASE // KVR) as i:
                for v in range(KVR):
                    load_unit(v, i * (2 * KVR) + 2 * v, 1, (s_PV, i * 2 - 1 + v // 4))
            for n in range(46, len(tiles)):
                load(n)

        @block.gpsimd
        def _(pool):
            pool.memset(cT[:], 0.0).then_inc(s_ini, 1)
            pool.memset(pab[:], 0.0).then_inc(s_ini, 1)
            pool.memset(eps[:], EPS).then_inc(s_ini, 1)
            pool.wait_ge(s_adaT, ADA_TILES)
            pool.memset(adaf[:], 0.0).then_inc(s_qz, 1)
            pool.wait_ge(s_kvt, 6)
            for name, buf in (("k", ktok), ("v", vtok)):
                pool.dma_start(o[name + "_prompt"][0, 0].rearrange("(t p) h d -> p t (h d)", p=P), buf[:, 0:2, :]).then_inc(s_okv, 16)
                pool.dma_start(o[name + "_sample"][0].rearrange("b t h d -> (b t) (h d)"), buf[0:NS, 2, :]).then_inc(s_okv, 16)
            pool.wait_ge(s_cvo, 3)
            pool.dma_start(o["conv_prompt"][0, 0], cout[0:3, :]).then_inc(s_okv, 16)
            pool.dma_start(o["conv_sample"][0].rearrange("b i n -> (b i) n"), cout[3:27, :]).then_inc(s_okv, 16)
            pool.wait_ge(*copied(("S2",)))
            pool.dma_start(o["gdn_prompt"][0, 0].rearrange("h k v -> k h v"), S1).then_inc(s_okv, 16)
            pool.wait_ge(*copied(("up", 7)))
            for hh in range(HG):
                pool.dma_start(o["gdn_sample"][0, :, hh].rearrange("b k v -> k b v"), st[:, hh]).then_inc(s_out, 16)
            pool.wait_ge(s_y, 6)
            pool.dma_start(o["y_prompt"][0].rearrange("(t p) n -> p t n", p=P), ytok[:, 0:2, :]).then_inc(s_out, 16)
            pool.dma_start(o["y_sample"].rearrange("b t n -> (b t) n"), ytok[0:NS, 2, :]).then_inc(s_out, 16)
            pool.wait_ge(s_out, 16 * 6)
            pool.wait_ge(s_okv, 16 * 7)



        def probs(g):
            return [range(0, 4), range(4, 8), range(8, 9)][g]

        @block.tensor
        def _(pe):
            def T(out, in_, n):
                return nc.tensor.transpose(out, in_, ident[0:n, 0:n])

            def landed(n):
                pe.wait_ge(s_w[n % RING], 32 * (n // RING + 1))

            pe.wait_ge(s_cst, 16)
            pe.wait_ge(s_cs, 1)
            for k in range(KD):
                m = T(ps[4][:, 16 * k:16 * k + NR], csil[0:NR, k * P:(k + 1) * P], NR)
            m.then_inc(s_pT0, 1)
            pe.wait_ge(s_par, 16 * 6)
            T(ps[5][:, 0:105], prow[0:105, :], 105)
            T(ps[5][:, 105:153], crow[0:48, :], 48)
            for c in range(CC):
                m = T(ps[6][:, 24 * c:24 * c + 24], srow[0:24, c * P:(c + 1) * P], 24)
            m.then_inc(s_pT0, 1)
            pe.wait_ge(s_x, 32)
            for c in range(KD):
                if c >= 4:
                    pe.wait_ge(s_h, c - 3)
                for t in range(3):
                    n = P if t < 2 else NS
                    m = T(ps[c % 4][:, t * P:t * P + n], xin[0:n, t, c * P:(c + 1) * P], n)
                m.then_inc(s_xT, 1)

            def ada_mm(j, slot, wait):
                pe.wait_ge(*wait)
                if not isinstance(j, int) or j >= 2:
                    pe.wait_ge(s_adaev, j - 1)
                for k in range(KD):
                    q = 32 * (k % 4)
                    m = nc.tensor.matmul(ps[ada_bank(j)][q:q + 32, :], cT[:, k, :], wring[:, slot, k, :],
                                         start=(k < 4), stop=(k >= 4), tile_position=(0, q))
                m.then_inc(s_adamm, 1)

            par = [0]

            def ada_bank(j):
                return 4 + (j if isinstance(j, int) else par[0]) % 2

            def ada_T(j, odd):
                pe.wait_ge(s_adaev, j + 1)
                if not isinstance(j, int) or j >= 2:
                    pe.wait_ge(s_modr, j - 1)
                for i in range(4):
                    m = T(ps[6 + odd][:, i * P:(i + 1) * P], adasb[:, odd, i * P:(i + 1) * P], P)
                m.then_inc(s_adaT, 1)

            def up_tile(l, j, slot, wait, first=False):
                pe.wait_ge(*wait)
                for s in range(2):
                    if not (first and l == 0):
                        pe.wait_ge(s_hid, j * 2 + (FC * l + s - 1))
                    for half, done in ((0, s_gate), (1, s_up)):
                        for k in range(KD):
                            m = nc.tensor.matmul(ps[2 * s + half][:, 0:TOK], wring[:, slot, k, 256 * half + P * s:256 * half + P * s + P],
                                                 hn[:, k, :], start=(k == 0), stop=(k == KD - 1))
                        m.then_inc(done, 1)

            def sumsq(ni):
                pe.wait_ge(s_sq, ni + 1)
                for k in range(KD):
                    m = nc.tensor.matmul(ps[0][:, 0:TOK], ones, xs[:, k, :], start=(k == 0), stop=(k == KD - 1))
                m.then_inc(s_ss, 1)

            def down(l):
                pe.wait_ge(s_hid, FC * (l + 1))
                for g in range(2):
                    for t in range(3):
                        landed(number[("down", l, g, t)])
                        slot = number[("down", l, g, t)] % RING
                        n = min(8, FC - 8 * t)
                        for i in range(4):
                            for f in range(n):
                                m = nc.tensor.matmul(ps[4 * (1 - g) + i][:, 0:TOK], wring[:, slot, f, i * P:(i + 1) * P],
                                                     hid[:, 8 * t + f, :], start=(t == 0 and f == 0), stop=(t == 2 and f == n - 1))
                            if t == 2:
                                m.then_inc(s_sub, 1)
                        if t < 2:
                            m.then_inc(s_dpart, 1)

            def tile(t):
                n = number[t]
                return n % RING, (s_w[n % RING], 32 * (n // RING + 1))

            pe.wait_ge(s_cT, 1)
            for j in range(ADA_FIRST):
                ada_mm(j, *tile(("ada", j)))
                if j:
                    ada_T(j - 1, (j - 1) % 2)
            sumsq(0)
            ada_T(5, 1)
            pe.wait_ge(s_hn, 1)
            up_tile(0, 0, *tile(("up", 0, 0)), first=True)
            ada_mm(6, *tile(("ada", 6)))
            ada_mm(7, *tile(("ada", 7)))
            ada_T(6, 0)
            with pe.Fori(0, 5) as i:
                for k in range(2):
                    slot = (9 + 2 * k) % RING
                    up_tile(0, i * 2 + 1 + k, slot, (s_w[slot], i * 32 + 32 * ((9 + 2 * k) // RING + 1)))
                    ada_T(i * 2 + 7 + k, (7 + k) % 2)
                    slot = (10 + 2 * k) % RING
                    par[0] = 8 + k
                    ada_mm(i * 2 + 8 + k, slot, (s_w[slot], i * 32 + 32 * ((10 + 2 * k) // RING + 1)))
            ada_T(17, 1)
            pe.wait_ge(s_modr, ADA_TILES)
            down(0)

            sumsq(1)
            pe.wait_ge(s_hn, 2)
            for q in range(28):
                if q % 4 == 0:
                    landed(number[("in", q // 4)])
                slot = number[("in", q // 4)] % RING
                if 8 <= q < 20:
                    pe.wait_ge(s_xc, q - 7)
                elif q >= 20:
                    pe.wait_ge(s_zm, q - 19)
                for k in range(KD):
                    m = nc.tensor.matmul(ps[q % 8][:, 0:TOK], wring[:, slot, k, (q % 4) * P:(q % 4 + 1) * P], hn[:, k, :],
                                         start=(k == 0), stop=(k == KD - 1))
                m.then_inc(s_win, 1)
            pe.wait_ge(s_wab, 16)
            pe.wait_ge(s_zm, 9)
            for k in range(KD):
                m = nc.tensor.matmul(ps[4][0:8, 0:TOK], wab[:, k, :], hn[:, k, :], start=(k == 0), stop=(k == KD - 1))
            m.then_inc(s_win, 1)

            pe.wait_ge(s_zm, 16)
            pe.wait_ge(s_ab, 1)
            for q in range(6):
                src, t = (mkT, mvT)[q % 2], q // 2
                n = P if t < 2 else NS
                for c in range(4):
                    m = T(ps[q][0:n, c * P:(c + 1) * P], src[:, c, t * P:t * P + n], P)
                m.then_inc(s_kvT, 1)
            pe.wait_ge(s_cg, 1)
            for r in range(3):
                if r == 2:
                    pe.wait_ge(s_kvt, 1)
                bank = ps[(6, 7, 0)[r]]
                for c in range(4):
                    m = T(bank[0:27, c * P:(c + 1) * P], cgat[:, 4 * r + c, :], P)
                m.then_inc(s_cvT, 1)

            pe.wait_ge(s_kvt, 6)
            pe.wait_ge(s_cvo, 3)
            for s in range(HM + 2):
                if s < HM:
                    c, r = s // 2, HD * (s % 2)
                    if s >= 2:
                        pe.wait_ge(s_paS, s - 1)
                    bank = ps[1 + s % 2]
                    nc.tensor.matmul(bank[:, 0:P], mqT[r:r + HD, c, 0:P], mkT[r:r + HD, c, 0:P], start=True, stop=True)
                    nc.tensor.matmul(bank[:, P:3 * P], mqT[r:r + HD, c, P:SEQ], mkT[r:r + HD, c, 0:SEQ],
                                     start=True, stop=True).then_inc(s_sc, 1)
                if 1 <= s <= HM:
                    x = s - 1
                    pe.wait_ge(s_pn, x + 1)
                    if x >= 2:
                        pe.wait_ge(s_pTe, x - 1)
                    for i in range(3):
                        m = T(ps[3 + x % 2][:, i * P:(i + 1) * P], psP[:, x % 2, i * P:(i + 1) * P], P)
                    m.then_inc(s_paT, 1)
                if s >= 2:
                    x = s - 2
                    c, r = x // 2, HD * (x % 2)
                    pe.wait_ge(s_pTe, x + 1)
                    if x % 2 == 0 and c >= 2:
                        pe.wait_ge(s_pao, c - 1)
                    bank = ps[5 + c % 2]
                    nc.tensor.matmul(bank[r:r + HD, 0:SEQ], vtok[:, 0, x * HD:(x + 1) * HD], psT[:, x % 2, 0:SEQ], start=True, stop=False)
                    nc.tensor.matmul(bank[r:r + HD, P:SEQ], vtok[:, 1, x * HD:(x + 1) * HD], psT[:, x % 2, SEQ:3 * P],
                                     start=False, stop=True).then_inc(s_pav, 1)

            pe.wait_ge(s_g8, 1)
            for i in range(6):
                src = (sc8[0:8, 3, :], sc8[0:8, 4, :])[i // 3]
                spread = gE[0:8, i // 3, :]
                m = T(ps[7][:, 8 * i:8 * i + 8], src[:, (i % 3) * P:(i % 3) * P + P] if i % 3 < 2 else spread, 8)
            m.then_inc(s_gT, 1)

            def bank(step):
                k = STEPS[step]
                if k >= 8:
                    pe.wait_ge(s_ge, k - 7)
                return ps[k % 8]

            mm = nc.tensor.matmul
            pe.wait_ge(s_gbc, 1)
            pe.wait_ge(s_pao, 4)
            b = bank(("cum",))
            mm(b[:, 0:8], tri, G9[:, 0:8], start=True, stop=True)
            mm(b[:, 8:9], triS, G9[:, 8:9], start=True, stop=True)
            mm(b[:, 9:17], later, G9[:, 0:8], start=True, stop=True)
            mm(b[:, 17:18], laterS, G9[:, 8:9], start=True, stop=True).then_inc(s_gp, 1)
            for j in range(3):
                b = bank(("row", j))
                for x, p in enumerate(probs(j)):
                    m = mm(b[:, x * P:(x + 1) * P], Pv[:, p, :], tri if p < 8 else triS, start=True, stop=True)
                m.then_inc(s_gp, 1)
            pe.wait_ge(s_qks, 1)
            for c in range(8):
                mm(bank(("l2", c))[:, 0:TOK], ones, sq8[:, c, :], start=True, stop=True).then_inc(s_gp, 1)
            pe.wait_ge(s_qkn, 1)
            for kind, base in (("kt", 4), ("vt", 8)):
                for j in range(3):
                    b = bank((kind, j))
                    for x, p in enumerate(probs(j)):
                        if p == 8:
                            src = smp[:, 1 if kind == "kt" else 2, :]
                        else:
                            src = (QK if kind == "kt" else Cv)[:, base + p % 4, (p // 4) * P:(p // 4 + 1) * P]
                        m = T(b[:, x * P:(x + 1) * P], src, P)
                    m.then_inc(s_gp, 1)
            QKh = QK.rearrange("p (two hh) n -> p hh two n", two=2)
            for j in range(5):
                b = bank(("gram", j))
                for x, p in enumerate(range(2 * j, min(2 * j + 2, NPROB))):
                    if p == 8:
                        k_, qk_ = smp[:, 1, :], smp[:, 0:2, :]
                    else:
                        cols = slice((p // 4) * P, (p // 4 + 1) * P)
                        k_, qk_ = QK[:, 4 + p % 4, cols], QKh[:, p % 4, :, cols]
                    m = mm(b[:, 2 * P * x:2 * P * (x + 1)], k_, qk_, start=True, stop=True)
                m.then_inc(s_gp, 1)
            nt = 0
            for l in range(7):
                groups = range(3 if l < 2 else 2)
                for g in groups:
                    b = bank(("P", l, g))
                    nt += 1
                    pe.wait_ge(s_ntl, nt)
                    if l:
                        pe.wait_ge(*copied(("PX", l - 1, g)))
                    for x, p in enumerate(probs(g)):
                        m = mm(b[:, x * P:(x + 1) * P], NTl[:, p, :], X[:, p, :] if l else ident, start=True, stop=True)
                    m.then_inc(s_gp, 1)
                for g in groups:
                    pe.wait_ge(*copied(("P", l, g)))
                    if 0 < l < 6:
                        b = bank(("XP", l, g))
                        for x, p in enumerate(probs(g)):
                            m = mm(b[:, x * P:(x + 1) * P], XT[:, p, :], Pv[:, p, :], start=True, stop=True)
                        m.then_inc(s_gp, 1)
                    b = bank(("PX", l, g))
                    for x, p in enumerate(probs(g)):
                        m = mm(b[:, x * P:(x + 1) * P], Pv[:, p, :], XT[:, p, :] if l else ident, start=True, stop=True)
                    m.then_inc(s_gp, 1)
            pe.wait_ge(*copied(("PX", 6, 1)))
            for g in (1, 2):
                b = bank(("W", g))
                for x, p in enumerate(probs(g)):
                    m = mm(b[:, x * P:(x + 1) * P], KB[:, p, :], XT[:, p, :], start=True, stop=True)
                m.then_inc(s_gp, 1)
            b = bank(("U0",))
            for x in range(4):
                m = mm(b[:, x * P:(x + 1) * P], XT[:, x, :], VB[:, x, :], start=True, stop=True)
            m.then_inc(s_gp, 1)
            pe.wait_ge(*copied(("U0",)))
            b = bank(("S1",))
            for x in range(4):
                m = mm(b[:, x * P:(x + 1) * P], KDc[:, x, :], VN[:, x, :], start=True, stop=True)
            m.then_inc(s_gp, 1)
            pe.wait_ge(*copied(("S1",)))
            b = bank(("V1",))
            for x in range(4):
                mm(b[:, x * P:(x + 1) * P], XT[:, 4 + x, :], VB[:, 4 + x, :], start=True, stop=False)
                m = mm(b[:, x * P:(x + 1) * P], WT[:, 4 + x, :], S1[:, x, :], start=False, stop=True)
            m.then_inc(s_gp, 1)
            b = bank(("o0",))
            for x in range(4):
                m = mm(b[:, x * P:(x + 1) * P], VN[:, x, :], AN[:, x, 0, :], start=True, stop=True)
            m.then_inc(s_gp, 1)
            pe.wait_ge(*copied(("V1",)))
            b = bank(("o1",))
            for x in range(4):
                mm(b[:, x * P:(x + 1) * P], VN[:, 4 + x, :], AN[:, 4 + x, 0, :], start=True, stop=False)
                m = mm(b[:, x * P:(x + 1) * P], S1[:, x, :], QD[:, 4 + x, :], start=False, stop=True)
            m.then_inc(s_gp, 1)
            b = bank(("S2",))
            for x in range(4):
                m = mm(b[:, x * P:(x + 1) * P], KDc[:, 4 + x, :], VN[:, 4 + x, :], start=True, stop=True)
            m.then_inc(s_gp, 1)
            mm(bank(("us",))[:, 0:P], VB[:, 8, :], XT[:, 8, :], start=True, stop=True).then_inc(s_gp, 1)
            pe.wait_ge(*copied(("W", 2)))
            pe.wait_ge(s_st, 64)
            b = bank(("ws",))
            for x in range(HG * NB):
                m = mm(b[:, 8 * x:8 * x + 8], st[:, x // NB, x % NB, :], WQ[:, x, :], start=True, stop=True)
            m.then_inc(s_gp, 1)
            pe.wait_ge(*copied(("ws",)))
            T(bank(("vs",))[:, 0:P], VX[:, 0, :], P).then_inc(s_gp, 1)
            pe.wait_ge(*copied(("vs",)))
            mm(bank(("os",))[:, 0:P], VN[:, 8, :], AN[:, 8, 0, :], start=True, stop=True).then_inc(s_gp, 1)
            pe.wait_ge(s_vx, 1)
            for x in range(8):
                hh, half = x // 2, x % 2
                rows = slice(NS * hh, NS * hh + NS)
                mm(bank(("up", x))[:, :], KDc[rows, 8, :], VX[rows, 4 * half:4 * half + 4, :].rearrange("p a b -> p (a b)"),
                   start=True, stop=True).then_inc(s_gp, 1)
            pe.wait_ge(s_go, 1)
            for hh in range(HG):
                mm(bank(("rms", hh))[:, 0:TOK], ones, sqg[:, hh, :], start=True, stop=True).then_inc(s_gp, 1)

            pe.wait_ge(s_ge, len(STEPS))
            pe.wait_ge(s_qbd, 8)
            for g in range(2):
                for b4 in range(4):
                    for c in range(4):
                        m = mm(ps[6][32 * b4:32 * b4 + 32, 32 * g:32 * g + 32], Qbd[:, c, 4 * g + b4, :], mkT[:, c, SEQ:TOK],
                               start=(c == 0), stop=(c == 3), tile_position=(0, 32 * b4))
                m.then_inc((s_qk, s_own)[g], 2 - g)

            def logits(g, n, mm0, odd, c):
                pe.wait_ge(s_ktA, mm0 + c + 3)
                pe.wait_ge(s_ktD, mm0 + c + 3)
                if c == 0:
                    pe.wait_ge(s_lev, n + 1)
                for b4 in range(4):
                    m = mm(ps[4 + odd][32 * b4:32 * b4 + 32, 0:BLK], Qbd[:, c, 4 * g + b4, :],
                           ktb[:, c % 2, b4 // 2, (b4 % 2) * BLK:(b4 % 2 + 1) * BLK],
                           start=(c == 0), stop=(c == 3), tile_position=(0, 32 * b4))
                m.then_inc(s_qk, 1)

            for g in range(2):
                with pe.Fori(0, 4) as i:
                    for odd in range(2):
                        n = i * 2 + (8 * g + odd)
                        mm0 = i * 8 + (32 * g + 4 * odd)
                        for c in range(4):
                            for pair in range(2):
                                pe.wait_ge((s_ktA, s_ktD)[pair], mm0 + c + 1)
                                for x in range(2):
                                    v = 4 * odd + 2 * pair + x
                                    if c == 0:
                                        pe.wait_ge(s_kv[v], i * 32 + 32 * (4 * g + 1))
                                    for y in range(2):
                                        m = T(ps[2 * (c % 2) + pair][:, x * BLK + y * PAGE:x * BLK + (y + 1) * PAGE],
                                              kv[:, v, y, c * P:(c + 1) * P], P)
                                m.then_inc(s_kt, 1)
                            if c:
                                logits(g, n, mm0, odd, c - 1)
                        logits(g, n, mm0, odd, 3)

            for n in range(16):
                g, blk = n // 8, n % 8
                if blk == 0:
                    pe.wait_ge(s_po, g + 1)
                    T(ps[g][0:32, 0:P], pown[:, g, :], P).then_inc(s_oT, 1)
                pe.wait_ge(s_pe, n + 1)
                if n >= 2:
                    pe.wait_ge(s_pTs, n - 1)
                for y in range(2):
                    m = T(ps[4 + n % 2][:, y * P:(y + 1) * P], pex[:, n % 2, y * P:(y + 1) * P], P)
                m.then_inc(s_PT, 1)
                pe.wait_ge(s_pTs, n + 1)
                if n == 8:
                    pe.wait_ge(s_om, 1)
                for b4 in range(4):
                    pe.wait_ge(s_kv[4 * (n % 2) + b4], 32 * (8 + n // 2 + 1))
                for y in range(2):
                    for b4 in range(4):
                        m = mm(ps[7][32 * b4:32 * b4 + 32, :], pT[:, n % 2, y, 32 * b4:32 * b4 + 32], kv[:, 4 * (n % 2) + b4, y, :],
                               start=(blk == 0 and y == 0), stop=False, tile_position=(0, 32 * b4))
                m.then_inc(s_PV, 1)
                if blk == 7:
                    pe.wait_ge(s_oTs, g + 1)
                    for b4 in range(4):
                        m = mm(ps[7][32 * b4:32 * b4 + 32, :], ownT[0:32, g, 32 * b4:32 * b4 + 32], vown[0:32, :],
                               start=False, stop=True, tile_position=(0, 32 * b4))
                    m.then_inc(s_O, 1)
                    pe.wait_ge(s_om, g + 1)
                    for c in range(4):
                        m = mm(ps[6][:, 64 * g + 16 * c:64 * g + 16 * c + 16], Om[:, c * P:(c + 1) * P], cst("selbt"), start=True, stop=True)
                    m.then_inc(s_AT, 1)

            pe.wait_ge(s_gdn, 1)
            pe.wait_ge(s_mixa, 2)
            for g in range(2):
                landed(number[("out", g)])
                slot = number[("out", g)] % RING
                for i in range(4):
                    for k in range(8):
                        m = mm(ps[4 * (1 - g) + i][:, 0:TOK], wring[:, slot, k, i * P:(i + 1) * P], mix[:, k, :],
                               start=(k == 0), stop=(k == 7))
                    m.then_inc(s_sub, 1)

            sumsq(2)
            pe.wait_ge(s_hn, 3)
            for j in range(3):
                up_tile(1, j, *tile(("up", 1, j)))
            with pe.Fori(0, 2) as i:
                for k in range(4):
                    n = number[("up", 1, 3)] + k
                    up_tile(1, i * 4 + 3 + k, n % RING, (s_w[n % RING], i * 32 + 32 * (n // RING + 1)))
            down(1)

            sumsq(3)
            pe.wait_ge(s_hn, 4)
            for q in range(6):
                t, half = q // 2, q % 2
                n = P if t < 2 else NS
                for c in range(4):
                    m = T(ps[1 + q][0:n, c * P:(c + 1) * P], hn[:, 4 * half + c, t * P:t * P + n], P)
                m.then_inc(s_yT, 1)

        @block.scalar
        def _(act):
            def fn(out, in_, func, **kw):
                return nc.scalar.activation(out, in_, func, **kw)

            def own(ins, s=s_act, count=[0]):
                count[0] += 1
                ins.then_inc(s, 1)
                act.wait_ge(s, count[0])

            act.dma_start(cin[0:1, :], a["c_prompt"]).then_inc(s_c, 16)
            act.dma_start(cin[1:NR, :], a["c_sample"]).then_inc(s_c, 16)
            act.dma_start(xin[:, 0:2, :], a["x_prompt"][0].rearrange("(t p) d -> p t d", p=P)).then_inc(s_x, 16)
            act.dma_start(xin[0:NS, 2, :], a["x_sample"].rearrange("b t d -> (b t) d")).then_inc(s_x, 16)
            act.dma_start(prow[0:72, :], a["b_ada"][0].rearrange("(r p) -> r p", p=P)).then_inc(s_par, 16)
            act.dma_start(prow[72:96, :], a["norm_w"][0].rearrange("i (r p) -> (i r) p", p=P)).then_inc(s_par, 16)
            act.dma_start(prow[96:104, :], a["final_norm_w"].rearrange("(r p) -> r p", p=P)).then_inc(s_par, 16)
            act.dma_start(prow[104:105, :], a["gdn_norm_w"]).then_inc(s_par, 16)
            act.dma_start(crow[0:48, :], a["conv_w"][0].rearrange("i (c p) -> (i c) p", p=P)).then_inc(s_par, 16)
            act.dma_start(srow[0:24, :], a["state_conv"][0].rearrange("b i n -> (b i) n")).then_inc(s_par, 16)
            act.wait_ge(s_c, 32)
            fn(csil[0:NR, :], cin[0:NR, :], ACT.Silu).then_inc(s_cs, 1)
            act.dma_start(wab[:, :, :], win[:, :, 1536:1544]).then_inc(s_wab, 16)
            act.dma_start(ptab[:, :], a["ptab"]).then_inc(s_pt, 16)
            act.wait_ge(s_ini, 3)
            act.dma_start(pab[0:HG, 0:1], a["dt_bias"].rearrange("o h -> h o")).then_inc(s_pab, 16)
            act.dma_start(pab[0:HG, 1:2], a["a_log"].rearrange("o h -> h o")).then_inc(s_pab, 16)

            def square(ni):
                act.wait_ge(s_h, KD * (ni + 1))
                fn(xs, h[:, :, :], ACT.Square).then_inc(s_sq, 1)

            def norm(ni):
                act.wait_ge(s_ss, ni + 1)
                fn(rstd[:, :], ps[0][:, 0:TOK], ACT.Ln, scale=1.0 / D, bias=eps[:, 0:1]).then_inc(s_ln, 1)
                act.wait_ge(s_ln, ni + 1)
                fn(rstd[:, :], rstd[:, :], ACT.Exp, scale=-0.5).then_inc(s_rstd, 1)

            def ada_copy(j, odd):
                act.wait_ge(s_adamm, j + 1)
                if not isinstance(j, int) or j >= 2:
                    act.wait_ge(s_adaT, j - 1)
                nc.scalar.copy(adasb[:, odd, :], ps[4 + odd][:, :]).then_inc(s_adaev, 1)

            def gate_silu(l, f, odd):
                act.wait_ge(s_gate, f + (FC * l + 1))
                if l or not isinstance(f, int) or f >= 2:
                    act.wait_ge(s_hid, f + (FC * l - 1))
                fn(sgate[:, odd, :], ps[2 * odd][:, 0:TOK], ACT.Silu).then_inc(s_silu, 1)

            square(0)
            for j in range(ADA_FIRST):
                ada_copy(j, j % 2)
            norm(0)
            gate_silu(0, 0, 0)
            gate_silu(0, 1, 1)
            ada_copy(6, 0)
            ada_copy(7, 1)
            with act.Fori(0, 5) as i:
                for k in range(2):
                    gate_silu(0, i * 4 + (2 + 2 * k), 0)
                    gate_silu(0, i * 4 + (3 + 2 * k), 1)
                    ada_copy(i * 2 + (8 + k), k)

            square(1)
            norm(1)

            def zqkv(q):
                act.wait_ge(s_win, q + 1)
                src, kind, c = ps[q % 8][:, 0:TOK], (q - 12) // 4, q % 4
                if kind == 0:
                    ins = fn(zs[:, c, :], src, ACT.Silu)
                elif kind == 1:
                    ins = nc.scalar.mul(mqT[:, c, :], src, HD ** -0.5)
                else:
                    ins = nc.scalar.copy((mkT, mvT)[kind - 2][:, c, :], src)
                ins.then_inc(s_zm, 1)

            def conv_silu(grp):
                for j in range(4):
                    cc = 4 * grp + j
                    act.wait_ge(s_conv, 16 * grp + 12 + j + 1)
                    fn(Cv[:, cc, 0:SEQ], Yb[:, j, 0:SEQ], ACT.Silu)
                    fn(Cv[:, cc, SEQ:TOK].rearrange("p (b t) -> p b t", b=NB),
                       Yb[:, j, 3 + SEQ:XW].rearrange("p (b s) -> p b s", b=NB)[:, :, 0:NT], ACT.Silu).then_inc(s_csil, 1)

            for grp in range(3):
                for q in range(12 + 4 * grp, 16 + 4 * grp):
                    zqkv(q)
                if grp < 2:
                    conv_silu(grp)
            for q in range(24, 28):
                zqkv(q)
            act.wait_ge(s_win, 29)
            nc.scalar.copy(abT[:, :], ps[4][0:8, 0:TOK]).then_inc(s_ab, 1)
            for q in range(6):
                act.wait_ge(s_kvT, q + 1)
                n = P if q < 4 else NS
                if q == 5:
                    nc.scalar.copy(vown[:, :], ps[q][0:n, :])
                nc.scalar.copy((ktok, vtok)[q % 2][0:n, q // 2, :], ps[q][0:n, :]).then_inc(s_kvt, 1)
            conv_silu(2)
            for r in range(3):
                act.wait_ge(s_cvT, r + 1)
                nc.scalar.copy(cout[0:27, 512 * r:512 * r + 512], ps[(6, 7, 0)[r]][0:27, :]).then_inc(s_cvo, 1)
            act.wait_ge(s_cg, 1)
            act.wait_ge(s_csil, CC)
            for hh in range(HG):
                act.dma_start(st[:, hh], a["state_gdn"][0, :, hh].rearrange("b k v -> k b v")).then_inc(s_st, 16)
            act.wait_ge(s_absx, 1)
            act.wait_ge(s_pab, 32)
            fn(sc8[0:8, 4, :], abT[:, :], ACT.Sigmoid)
            fn(pab[:, 2:3], pab[:, 1:2], ACT.Exp)
            own(fn(sc8[0:8, 1, :], sc8[0:8, 1, :], ACT.Exp))
            fn(sc8[0:8, 2, :], sc8[0:8, 1, :], ACT.Ln, bias=1.0).then_inc(s_sp, 1)
            for s in range(HM + 1):
                if s < HM:
                    act.wait_ge(s_nm, s + 1)
                    if s >= 2:
                        act.wait_ge(s_paT, s - 1)
                    fn(psP[:, s % 2, 0:P], psS[:, s % 2, 0:P], ACT.Exp, bias=patt[:, 2 * s:2 * s + 1],
                       accum_out=patt[:, 16 + 2 * s:17 + 2 * s])
                    fn(psP[:, s % 2, P:3 * P], psS[:, s % 2, P:3 * P], ACT.Exp, bias=patt[:, 2 * s + 1:2 * s + 2],
                       accum_out=patt[:, 17 + 2 * s:18 + 2 * s]).then_inc(s_pexp, 1)
                if s >= 1:
                    x = s - 1
                    act.wait_ge(s_paT, x + 1)
                    if x >= 2:
                        act.wait_ge(s_pav, x - 1)
                    nc.scalar.copy(psT[:, x % 2, :], ps[3 + x % 2][:, 0:3 * P]).then_inc(s_pTe, 1)

            act.wait_ge(s_gT, 1)
            fn(sq8, Cv[:, 0:8, :], ACT.Square).then_inc(s_qks, 1)
            act.wait_ge(*copied(("cum",)))
            fn(ecum, cum, ACT.Exp).then_inc(s_ecum, 1)
            for j in range(3):
                act.wait_ge(*copied(("row", j)))
                pr = probs(j)
                fn(EG[:, pr[0]:pr[-1] + 1, :], gR[:, pr[0]:pr[-1] + 1, :], ACT.Exp).then_inc(s_eg, 1)
            act.wait_ge(s_df, 1)
            fn(DT, DT, ACT.Exp).then_inc(s_dt, 1)
            act.wait_ge(*copied(("l2", 7)))
            own(fn(RS, RS, ACT.Ln))
            fn(RS, RS, ACT.Exp, scale=-0.5).then_inc(s_rse, 1)
            act.wait_ge(*copied(("os",)))
            fn(sqg[:, 0:HG, :], goT, ACT.Square).then_inc(s_go, 1)
            act.wait_ge(*copied(("rms", HG - 1)))
            own(fn(sqg[:, HG:8, :], sqg[:, HG:8, :], ACT.Ln))
            fn(sqg[:, HG:8, :], sqg[:, HG:8, :], ACT.Exp, scale=-0.5).then_inc(s_gr, 1)

            act.wait_ge(s_qz, 1)
            act.wait_ge(s_zm, 16)
            for c in range(4):
                for hh in range(2):
                    rows, head = slice(HD * hh, HD * hh + HD), 2 * c + hh
                    nc.scalar.copy(Qbd[rows, c, :, NT * head:NT * head + NT],
                                   mqT[rows, c, SEQ:TOK].rearrange("p (b t) -> p b t", b=NB)).then_inc(s_qbd, 1)
            act.sem_inc(s_ktA, 2)
            for g in range(2):
                with act.Fori(0, 4) as i:
                    for m in range(8):
                        count = i * 8 + (32 * g + m)
                        act.wait_ge(s_kt, i * 16 + (64 * g + 2 * m + 1))
                        act.wait_ge(s_qk, count + 1)
                        nc.scalar.copy(ktb[:, m % 2, 0, :], ps[2 * (m % 2)][:, :]).then_inc(s_ktA, 1)

            for n in range(2 * NBLK):
                g, blk = n // NBLK, n % NBLK
                act.wait_ge(s_pen, g + 1)
                if blk == 0:
                    fn(pown[:, g, :], sown[:, g, :], ACT.Exp, bias=pen[:, g, NBLK:NBLK + 1],
                       accum_out=rsum[:, g, NBLK:NBLK + 1]).then_inc(s_po, 1)
                if n >= 2:
                    act.wait_ge(s_PT, n - 1)
                fn(pex[:, n % 2, :], S[:, g, blk * BLK:(blk + 1) * BLK], ACT.Exp, bias=pen[:, g, blk:blk + 1],
                   accum_out=rsum[:, g, blk:blk + 1]).then_inc(s_pe, 1)

            square(2)
            norm(2)
            for f in range(6):
                gate_silu(1, f, f % 2)
            with act.Fori(0, 2) as i:
                for k in range(8):
                    gate_silu(1, i * 8 + (6 + k), k % 2)
            square(3)
            norm(3)
            for q in range(0, 6, 2):
                act.wait_ge(s_yT, q + 1)
                n = P if q < 4 else NS
                nc.scalar.copy(ytok[0:n, q // 2, 0:512], ps[1 + q][0:n, :]).then_inc(s_y, 1)

        @block.vector
        def _(dve):
            v = nc.vector

            def own(ins, count=[0]):
                count[0] += 1
                ins.then_inc(s_dve, 1)
                dve.wait_ge(s_dve, count[0])

            def bt(x):
                return x.rearrange("p (b t) -> p b t", b=NB)

            dve.wait_ge(s_ini, 3)
            dve.wait_ge(s_pT0, 1)
            v.tensor_copy(cT[:, :, 0:NR], ps[4][:, 0:P].rearrange("p (k r) -> p k r", k=KD)[:, :, 0:NR]).then_inc(s_cT, 1)
            dve.wait_ge(s_pT0, 2)
            v.tensor_copy(pvec[:, :], ps[5][:, 0:153])
            own(v.tensor_copy(cst3[:, :, :], ps[6][:, 0:CC * 24].rearrange("p (c x) -> p c x", c=CC)))
            for c in range(KD):
                dve.wait_ge(s_xT, c + 1)
                v.tensor_copy(h[:, c, :], ps[c % 4][:, 0:TOK]).then_inc(s_h, 1)

            def mod_tile(j, odd):
                dve.wait_ge(s_adaT, j + 1)
                part = ps[6 + odd][:, :].rearrange("p (c g r) -> p c r g", c=4, g=4)[:, :, 0:NR, :]
                at = bass.ds(j * 4, 4)
                v.tensor_reduce(modT[:, at, :], part, AX_X, ALU.add).then_inc(s_modr, 1)
                dve.wait_ge(s_modr, j + 1)
                v.tensor_tensor(modT[:, at, :], modT[:, at, :], bw[:, at].unsqueeze(2).to_broadcast([P, 4, NR]),
                                ALU.add).then_inc(s_mod, 1)

            def norm(ni):
                if ni < 3:
                    dve.wait_ge(s_mod, ADA_FIRST if ni == 0 else ADA_TILES)
                    sh = modT[:, 3 * ni * KD:(3 * ni + 1) * KD, :]
                    v.scalar_tensor_tensor(coef[:, :, :], modT[:, (3 * ni + 1) * KD:(3 * ni + 2) * KD, :], 1.0,
                                           nw[:, KD * ni:KD * ni + KD].unsqueeze(2).to_broadcast([P, KD, NR]), ALU.add, ALU.mult)
                dve.wait_ge(s_rstd, ni + 1)
                own(v.tensor_tensor(xs, h[:, :, :], rstd[:, :].unsqueeze(1).to_broadcast([P, KD, TOK]), ALU.mult))
                if ni == 3:
                    for c in range(KD):
                        ins = v.tensor_scalar(hn[:, c, :], xs[:, c, :], nw[:, 24 + c:25 + c], None, ALU.mult)
                    ins.then_inc(s_hn, 1)
                    return

                def smp4(x):
                    return x[:, :, SEQ:TOK].rearrange("p c (b t) -> p c b t", b=NB)

                def spread(x):
                    return x[:, :, 1:NR].unsqueeze(3).to_broadcast([P, KD, NB, NT])

                own(v.tensor_tensor(smp4(hn), smp4(xs), spread(coef), ALU.mult))
                v.tensor_tensor(smp4(hn), smp4(hn), spread(sh), ALU.add)
                for c in range(KD):
                    ins = v.tensor_scalar(hn[:, c, 0:SEQ], xs[:, c, 0:SEQ], coef[:, c, 0:1], sh[:, c, 0:1], ALU.mult, ALU.add)
                ins.then_inc(s_hn, 1)

            def hidden(l, f, odd):
                dve.wait_ge(s_silu, f + (FC * l + 1))
                dve.wait_ge(s_up, f + (FC * l + 1))
                at = bass.ds(f, 1)
                v.tensor_tensor(hid[:, at, :].rearrange("p o n -> p (o n)"), sgate[:, odd, :], ps[2 * odd + 1][:, 0:TOK],
                                ALU.mult).then_inc(s_hid, 1)

            def residual(si):
                mod = modT[:, (3 * si + 2) * KD:(3 * si + 3) * KD, :]
                gt = mod
                if si != 1:
                    own(v.tensor_scalar(gate[:, :, :], mod, 0.5, None, ALU.mult))
                    gt = gate
                for m in range(KD):
                    dve.wait_ge(s_sub, KD * si + m + 1)
                    b = ps[4 + m] if m < 4 else ps[m - 4]
                    own(v.tensor_tensor(samp[:, m % 2], bt(b[:, SEQ:TOK]), gt[:, m, 1:NR].unsqueeze(2).to_broadcast([P, NB, NT]), ALU.mult))
                    v.scalar_tensor_tensor(h[:, m, 0:SEQ], b[:, 0:SEQ], gt[:, m, 0:1], h[:, m, 0:SEQ], ALU.mult, ALU.add)
                    v.tensor_tensor(bt(h[:, m, SEQ:TOK]), bt(h[:, m, SEQ:TOK]), samp[:, m % 2], ALU.add).then_inc(s_h, 1)

            for j in range(ADA_FIRST):
                mod_tile(j, j % 2)
            norm(0)
            hidden(0, 0, 0)
            hidden(0, 1, 1)
            mod_tile(6, 0)
            with dve.Fori(0, 5) as i:
                for k in range(2):
                    hidden(0, i * 4 + (2 + 2 * k), 0)
                    hidden(0, i * 4 + (3 + 2 * k), 1)
                    mod_tile(i * 2 + (7 + k), 1 - k)
            mod_tile(17, 1)
            dve.wait_ge(s_mod, ADA_TILES)
            residual(0)

            norm(1)
            v.memset(XC[:, :, 0:3], 0.0)
            v.tensor_copy(XCs[:, :, :, 0:3], cst3[:, :, :].rearrange("p c (b i) -> p c b i", b=NB))
            for q in range(CC):
                dve.wait_ge(s_win, q + 1)
                v.tensor_copy(XC[:, q, 3:3 + SEQ], ps[q % 8][:, 0:SEQ])
                v.tensor_copy(XCs[:, q, :, 3:7], bt(ps[q % 8][:, SEQ:TOK])).then_inc(s_xc, 1)
            for grp in range(3):
                dve.wait_ge(s_xc, 4 * grp + 4)
                for tap in range(CONV):
                    for j in range(4):
                        cc, op = 4 * grp + j, 16 * grp + 4 * tap + j
                        src, w = XC[:, cc, tap:tap + YW], cw[:, CC * tap + cc:CC * tap + cc + 1]
                        if tap == 0:
                            if grp:
                                dve.wait_ge(s_csil, cc - 3)
                            ins = v.tensor_scalar(Yb[:, j, 0:YW], src, w, None, ALU.mult)
                        else:
                            dve.wait_ge(s_conv, op - 3)
                            ins = v.scalar_tensor_tensor(Yb[:, j, 0:YW], src, w, Yb[:, j, 0:YW], ALU.mult, ALU.add)
                        ins.then_inc(s_conv, 1)
            dve.wait_ge(s_win, 28)
            v.tensor_copy(cgat[:, :, 0:3], XC[:, :, SEQ:SEQ + 3])
            v.tensor_copy(cgat[:, :, 3:27].rearrange("p c (b i) -> p c b i", b=NB), XCs[:, :, :, 4:7]).then_inc(s_cg, 1)

            dve.wait_ge(s_cst2, 16)
            dve.wait_ge(s_ab, 1)
            dve.wait_ge(s_pab, 32)
            own(v.tensor_scalar(sc8[0:8, 0, :], abT[:, :], pab[:, 0:1], None, ALU.add))
            v.scalar_tensor_tensor(sc8[0:8, 1, :], sc8[0:8, 0, :], -1.0, sc8[0:8, 0, :], ALU.mult, ALU.min).then_inc(s_absx, 1)

            for s in range(HM + 2):
                if s < HM:
                    dve.wait_ge(s_sc, s + 1)
                    if s >= 2:
                        dve.wait_ge(s_pexp, s - 1)
                    v.scalar_tensor_tensor(psS[:, s % 2, :], cst("dist"), 2.0 ** -(s + 1), ps[1 + s % 2][:, 0:3 * P],
                                           ALU.mult, ALU.add).then_inc(s_paS, 1)
                    dve.wait_ge(s_paS, s + 1)
                    v.tensor_reduce(patt[:, 2 * s:2 * s + 1], psS[:, s % 2, 0:P], AX_X, ALU.max, negate=True)
                    v.tensor_reduce(patt[:, 2 * s + 1:2 * s + 2], psS[:, s % 2, P:3 * P], AX_X, ALU.max, negate=True).then_inc(s_nm, 1)
                if 1 <= s <= HM:
                    x = s - 1
                    dve.wait_ge(s_pexp, x + 1)
                    sums = patt[:, 16 + 2 * x:18 + 2 * x]
                    own(v.reciprocal(sums, sums))
                    v.tensor_scalar(psP[:, x % 2, 0:P], psP[:, x % 2, 0:P], sums[:, 0:1], None, ALU.mult)
                    v.tensor_scalar(psP[:, x % 2, P:3 * P], psP[:, x % 2, P:3 * P], sums[:, 1:2], None, ALU.mult).then_inc(s_pn, 1)
                if s >= 2 and s % 2:
                    c = (s - 2) // 2
                    dve.wait_ge(s_pav, 2 * c + 2)
                    v.tensor_copy(mix[:, 4 + c, 0:SEQ], ps[5 + c % 2][:, 0:SEQ]).then_inc(s_pao, 1)

            dve.wait_ge(s_sp, 1)
            own(v.scalar_tensor_tensor(sc8[0:8, 3, :], sc8[0:8, 0, :], 0.0, sc8[0:8, 2, :], ALU.max, ALU.add))
            own(v.tensor_scalar(sc8[0:8, 3, :], sc8[0:8, 3, :], pab[:, 2:3], -1.0, ALU.mult, ALU.mult))
            for i in range(2):
                ins = v.tensor_tensor(gE[0:8, i, :].rearrange("p (h n) -> p h n", h=HG),
                                      sc8[0:8, 3 + i, SEQ:TOK].unsqueeze(1).to_broadcast([8, HG, NS]),
                                      cst("mh8")[0:8, :].rearrange("p (h n) -> p h n", h=HG), ALU.mult)
            ins.then_inc(s_g8, 1)
            dve.wait_ge(s_gT, 1)
            own(v.tensor_copy(GB, ps[7][:, 0:48].rearrange("p (a b) -> p a b", a=6)))
            for dst, i, r in ((G9, 0, 0), (B9, 3, 4)):
                v.tensor_copy(dst[:, 0:4], GB[:, i, r:r + 4])
                v.tensor_copy(dst[:, 4:8], GB[:, i + 1, r:r + 4])
                own(v.tensor_reduce(dst[:, 8:9], GB[:, i + 2, r:r + 4], AX_X, ALU.add))
            v.tensor_copy(Pv, G9.unsqueeze(2).to_broadcast([P, NPROB, P])).then_inc(s_gbc, 1)

            def filled(step):
                k = STEPS[step]
                dve.wait_ge(s_gp, k + 1)
                return ps[k % 8]

            def grp3(b, g):
                n = len(probs(g))
                return b[:, 0:n * P].rearrange("p (a b) -> p a b", a=n)

            def sel(x, g):
                return x[:, probs(g)[0]:probs(g)[-1] + 1]

            v.tensor_copy(cum, filled(("cum",))[:, 0:18]).then_inc(s_ge, 1)
            dve.wait_ge(s_okv, 96)
            for g in range(3):
                v.tensor_copy(sel(gR, g), grp3(filled(("row", g)), g)).then_inc(s_ge, 1)
            dve.wait_ge(*copied(("row", 2)))
            for p in range(NPROB):
                ins = v.tensor_scalar(DT[:, p, :], gR[:, p, :], cum[:, p:p + 1], 0.0, ALU.subtract, ALU.min)
            ins.then_inc(s_df, 1)
            dve.wait_ge(s_ecum, 1)
            v.tensor_tensor(bek, B9, ecum[:, 0:NPROB], ALU.mult)
            for c in range(8):
                v.tensor_scalar(RS[:, c, :], filled(("l2", c))[:, 0:TOK], EPS, None, ALU.add).then_inc(s_ge, 1)
            dve.wait_ge(s_dt, 1)
            v.tensor_tensor(DT[:, 0:8, :], DT[:, 0:8, :], tri.unsqueeze(1).to_broadcast([P, 8, P]), ALU.mult)
            v.tensor_tensor(DT[:, 8, :], DT[:, 8, :], triS, ALU.mult)
            dve.wait_ge(s_rse, 1)
            v.scalar_tensor_tensor(QK[:, 0:4, :], Cv[:, 0:4, :], P ** -0.5, RS[:, 0:4, :], ALU.mult, ALU.mult)
            own(v.tensor_tensor(QK[:, 4:8, :], Cv[:, 4:8, :], RS[:, 4:8, :], ALU.mult))
            for i, src in enumerate((QK[:, 0:4], QK[:, 4:8], Cv[:, 8:12])):
                ins = v.tensor_copy(smp[:, i, :].rearrange("p (h n) -> p h n", h=HG), src[:, :, SEQ:TOK])
            ins.then_inc(s_qkn, 1)
            dve.wait_ge(s_qkn, 1)
            for j in range(3):
                b = filled(("kt", j))
                for x, p in enumerate(probs(j)):
                    v.tensor_scalar(KB[:, p, :], b[:, x * P:(x + 1) * P], bek[:, p:p + 1], None, ALU.mult)
                    ins = v.tensor_scalar(KDc[:, p, :], b[:, x * P:(x + 1) * P], ecum[:, 9 + p:10 + p], None, ALU.mult)
                ins.then_inc(s_ge, 1)
            for j in range(3):
                v.tensor_tensor(sel(VB, j), grp3(filled(("vt", j)), j), sel(B9, j).unsqueeze(2).to_broadcast([P, len(probs(j)), P]),
                                ALU.mult).then_inc(s_ge, 1)
            for j in range(5):
                n = min(2, NPROB - 2 * j)
                b = filled(("gram", j))[:, 0:2 * P * n].rearrange("p (x i t) -> p x i t", x=n, i=2)
                v.tensor_tensor(AN[:, 2 * j:2 * j + n], b, DT[:, 2 * j:2 * j + n, :].unsqueeze(2).to_broadcast([P, n, 2, P]),
                                ALU.mult).then_inc(s_ge, 1)
            dve.wait_ge(*copied(("gram", 4)))

            def level_mask(l):
                for g in range(3 if l < 2 else 2):
                    n = len(probs(g))
                    v.tensor_tensor(sel(NTl, g), sel(AN, g)[:, :, 1, :], lev[:, l, :].unsqueeze(1).to_broadcast([P, n, P]),
                                    ALU.mult).then_inc(s_ntl, 1)

            level_mask(0)
            v.tensor_tensor(QD[:, 4:8, :], QK[:, 0:4, P:SEQ], EG[:, 4:8, :], ALU.mult)
            v.tensor_tensor(WQ[:, :, 4:8], smp[:, 0, :].rearrange("p (x t) -> p x t", t=NT),
                            EG[:, 8, :].rearrange("p (x t) -> p x t", t=NT), ALU.mult)
            for l in range(7):
                groups = range(3 if l < 2 else 2)
                for g in groups:
                    v.tensor_tensor(sel(Pv, g), grp3(filled(("P", l, g)), g),
                                    sel(B9, g).unsqueeze(2).to_broadcast([P, len(probs(g)), P]), ALU.mult).then_inc(s_ge, 1)
                if l < 6:
                    level_mask(l + 1)
                for g in groups:
                    if l == 0:
                        idb = ident.unsqueeze(1).to_broadcast([P, len(probs(g)), P])
                        dve.wait_ge(*copied(("P", 0, g)))
                        v.tensor_tensor(sel(X, g), idb, sel(Pv, g), ALU.subtract)
                        v.tensor_tensor(sel(XT, g), idb, grp3(filled(("PX", 0, g)), g), ALU.subtract).then_inc(s_ge, 1)
                        continue
                    if l < 6:
                        v.tensor_tensor(sel(X, g), sel(X, g), grp3(filled(("XP", l, g)), g), ALU.subtract).then_inc(s_ge, 1)
                    v.tensor_tensor(sel(XT, g), sel(XT, g), grp3(filled(("PX", l, g)), g), ALU.subtract).then_inc(s_ge, 1)
            v.tensor_scalar(WT[:, 4:8, :], grp3(filled(("W", 1)), 1), -1.0, None, ALU.mult).then_inc(s_ge, 1)
            v.tensor_copy(WQ[:, :, 0:4], filled(("W", 2))[:, 0:P].rearrange("p (x t) -> p x t", t=NT)).then_inc(s_ge, 1)
            v.tensor_copy(VN[:, 0:4, :], grp3(filled(("U0",)), 0)).then_inc(s_ge, 1)
            v.tensor_copy(S1, grp3(filled(("S1",)), 0)).then_inc(s_ge, 1)
            v.tensor_copy(VN[:, 4:8, :], grp3(filled(("V1",)), 0)).then_inc(s_ge, 1)
            v.tensor_copy(goT[:, :, 0:P], grp3(filled(("o0",)), 0)).then_inc(s_ge, 1)
            v.tensor_copy(goT[:, :, P:SEQ], grp3(filled(("o1",)), 0)).then_inc(s_ge, 1)
            b = filled(("S2",))
            for x in range(HG):
                ins = v.scalar_tensor_tensor(S1[:, x, :], S1[:, x, :], EG[:, 4 + x, P - 1:P], b[:, x * P:(x + 1) * P],
                                             ALU.mult, ALU.add)
            ins.then_inc(s_ge, 1)
            v.tensor_copy(VX[:, 0, :], filled(("us",))[:, 0:P]).then_inc(s_ge, 1)
            b = filled(("ws",))[:, 0:8 * HG * NB].rearrange("p (x t) -> p x t", t=8)
            dve.wait_ge(*copied(("us",)))
            vx0 = VX[:, 0, :].rearrange("p (x t) -> p x t", t=NT)
            v.tensor_copy(VX[:, 1, :].rearrange("p (x t) -> p x t", t=NT), b[:, :, 4:8])
            v.tensor_tensor(vx0, vx0, b[:, :, 0:4], ALU.subtract).then_inc(s_ge, 1)
            v.tensor_copy(VN[:, 8, :], filled(("vs",))[:, 0:P]).then_inc(s_ge, 1)
            heads = "p (h n) -> p h n"
            v.tensor_tensor(goT[:, :, SEQ:TOK], VX[:, 1, :].rearrange(heads, h=HG), filled(("os",))[:, 0:P].rearrange(heads, h=HG),
                            ALU.add).then_inc(s_ge, 1)
            dve.wait_ge(*copied(("os",)))
            v.tensor_tensor(VX[:, 0:NB, :], VN[:, 8, :].unsqueeze(1).to_broadcast([P, NB, P]),
                            cst("bdm").unsqueeze(2).to_broadcast([P, NB, P]), ALU.mult).then_inc(s_vx, 1)
            for k in range(8):
                b = filled(("up", k))
                for x in range(4):
                    hh, s = k // 2, 4 * (k % 2) + x
                    last = NT * (NB * hh + s) + NT - 1
                    ins = v.scalar_tensor_tensor(st[:, hh, s, :], st[:, hh, s, :], EG[:, 8, last:last + 1], b[:, x * P:(x + 1) * P],
                                                 ALU.mult, ALU.add)
                ins.then_inc(s_ge, 1)
            for hh in range(HG):
                v.tensor_scalar(sqg[:, HG + hh, :], filled(("rms", hh))[:, 0:TOK], 1.0 / P, EPS, ALU.mult, ALU.add).then_inc(s_ge, 1)
            dve.wait_ge(s_gr, 1)
            own(v.scalar_tensor_tensor(goT, goT, gnw, sqg[:, HG:8, :], ALU.mult, ALU.mult))
            v.tensor_tensor(mix[:, 0:HG, :], goT, zs, ALU.mult).then_inc(s_gdn, 1)

            dve.wait_ge(s_out, 16 * HG)
            v.sem_inc(s_ktD, 2)
            v.sem_inc(s_lev, 2)
            for g in range(2):
                with dve.Fori(0, 4) as i:
                    for m in range(8):
                        dve.wait_ge(s_kt, i * 16 + (64 * g + 2 * m + 2))
                        dve.wait_ge(s_qk, i * 8 + (32 * g + m + 1))
                        v.tensor_copy(ktb[:, m % 2, 1, :], ps[2 * (m % 2) + 1][:, :]).then_inc(s_ktD, 1)
                        if m % 4 == 3:
                            odd = m // 4
                            dve.wait_ge(s_qk, i * 8 + (32 * g + 4 * odd + 6))
                            b = ps[4 + odd][:, 0:BLK]
                            at, one = bass.ds(i * (2 * BLK) + BLK * odd, BLK), bass.ds(i * 2 + odd, 1)
                            v.tensor_reduce(gts[:, g, one], b, AX_X, ALU.add)
                            v.tensor_tensor(S[:, g, at], b, cst("biasS")[:, at], ALU.add).then_inc(s_lev, 1)
                            dve.wait_ge(s_lev, i * 2 + (8 * g + odd + 3))
                            v.tensor_reduce(bmx[:, g, one], S[:, g, at], AX_X, ALU.max).then_inc(s_bmx, 1)
                dve.wait_ge(s_bmx, NBLK * (g + 1))
                other = gts[:, g, :].unsqueeze(1).to_broadcast([P, NBLK, NBLK])
                mine = gts[:, g, :].unsqueeze(2).to_broadcast([P, NBLK, NBLK])
                A8 = cmpA.rearrange("p (n m) -> p n m", n=NBLK)
                B8 = cmpB.rearrange("p (n m) -> p n m", n=NBLK)
                v.tensor_tensor(A8, other, mine, ALU.is_gt)
                own(v.tensor_tensor(B8, other, mine, ALU.is_equal))
                own(v.tensor_tensor(cmpB, cmpB, cst("lower8"), ALU.mult))
                own(v.tensor_tensor(cmpA, cmpA, cmpB, ALU.add))
                own(v.tensor_reduce(cnt, A8, AX_X, ALU.add))
                own(v.tensor_scalar(pen[:, g, 0:NBLK], cnt, TOPK - 0.5, NEG, ALU.is_ge, ALU.mult))
                v.tensor_tensor(bmx[:, g, 0:NBLK], bmx[:, g, 0:NBLK], pen[:, g, 0:NBLK], ALU.add)
                dve.wait_ge(s_own, 1)
                own(v.tensor_tensor(sown[:, g, :], ps[6][:, 32 * g:32 * g + 32], cst("biasO")[:, 32 * g:32 * g + 32], ALU.add))
                own(v.tensor_reduce(bmx[:, g, NBLK:NBLK + 1], sown[:, g, :], AX_X, ALU.max))
                own(v.tensor_reduce(negm[:, g:g + 1], bmx[:, g, :], AX_X, ALU.max, negate=True))
                v.tensor_copy(pen[:, g, NBLK:NBLK + 1], negm[:, g:g + 1])
                v.tensor_scalar(pen[:, g, 0:NBLK], pen[:, g, 0:NBLK], negm[:, g:g + 1], None, ALU.add).then_inc(s_pen, 1)

            for n in range(2 * NBLK):
                g, blk = n // NBLK, n % NBLK
                if blk == 0:
                    dve.wait_ge(s_oT, g + 1)
                    v.tensor_copy(ownT[0:32, g, :], ps[g][0:32, 0:P]).then_inc(s_oTs, 1)
                dve.wait_ge(s_PT, n + 1)
                if n >= 2:
                    dve.wait_ge(s_PV, n - 1)
                v.tensor_copy(pT[:, n % 2].rearrange("p a b -> p (a b)"), ps[4 + n % 2][:, 0:BLK]).then_inc(s_pTs, 1)
                if blk == NBLK - 1:
                    dve.wait_ge(s_pe, n + 1)
                    dve.wait_ge(s_po, g + 1)
                    own(v.tensor_reduce(rin[:, 2 * g:2 * g + 1], rsum[:, g, :], AX_X, ALU.add))
                    own(v.reciprocal(rin[:, 2 * g + 1:2 * g + 2], rin[:, 2 * g:2 * g + 1]))
                    dve.wait_ge(s_O, g + 1)
                    if g:
                        dve.wait_ge(s_AT, g)
                    v.scalar_tensor_tensor(Om, ps[7][:, :], rin[:, 2 * g + 1:2 * g + 2], cst("hmask"), ALU.mult, ALU.mult).then_inc(s_om, 1)
                    dve.wait_ge(s_AT, g + 1)
                    v.tensor_copy(mix[:, 4:8, SEQ + 16 * g:SEQ + 16 * g + 16],
                                  ps[6][:, 64 * g:64 * g + 64].rearrange("p (c n) -> p c n", c=4)).then_inc(s_mixa, 1)
            residual(1)

            norm(2)
            for f in range(6):
                hidden(1, f, f % 2)
            with dve.Fori(0, 2) as i:
                for k in range(8):
                    hidden(1, i * 8 + (6 + k), k % 2)
            residual(2)
            norm(3)
            for q in range(1, 6, 2):
                dve.wait_ge(s_yT, q + 1)
                n = P if q < 4 else NS
                v.tensor_copy(ytok[0:n, q // 2, 512:D], ps[1 + q][0:n, :]).then_inc(s_y, 1)


OUT_SHAPES = [("y_prompt", (1, SEQ, D)), ("y_sample", (NB, NT, D)), ("k_prompt", (1, 1, SEQ, HM, HD)), ("v_prompt", (1, 1, SEQ, HM, HD)),
              ("gdn_prompt", (1, 1, HG, P, P)), ("conv_prompt", (1, 1, 3, CC * P)), ("k_sample", (1, NB, NT, HM, HD)),
              ("v_sample", (1, NB, NT, HM, HD)), ("gdn_sample", (1, NB, HG, P, P)), ("conv_sample", (1, NB, 3, CC * P))]


def kernel(**inputs):
    import concourse.bacc as bacc
    from concourse.bass_utils import run_bass_kernel_spmd

    nc = bacc.Bacc("TRN2", target_bir_lowering=False, num_devices=1)
    arrays = {n: np.ascontiguousarray(x) for n, x in inputs.items() if n != "page_table"}
    table = np.asarray(inputs["page_table"]).reshape(2, NB // 2, NBLK, 2).transpose(0, 2, 1, 3)
    arrays["ptab"] = np.ascontiguousarray(table.reshape(1, 2 * PHASE))
    arrays["consts"] = make_consts()
    a = {n: nc.dram_tensor("in_" + n, x.shape, I32 if n == "ptab" else F32, kind="ExternalInput").ap() for n, x in arrays.items()}
    o = {n: nc.dram_tensor("out_" + n, shape, F32, kind="ExternalOutput").ap() for n, shape in OUT_SHAPES}
    build_program(nc, a, o)
    r = run_bass_kernel_spmd(nc, [{"in_" + n: x for n, x in arrays.items()}], core_ids=[0])
    return tuple(r.results[0]["out_" + n] for n, _ in OUT_SHAPES)
```

```python
from contextlib import ExitStack

import numpy as np

import concourse.bass as bass
from concourse import mybir

F32 = mybir.dt.float32
I32 = mybir.dt.int32
ALU = mybir.AluOpType
ACT = mybir.ActivationFunctionType
AX_X = mybir.AxisListType.X

P = 128
D = 1024
KD = D // P
SEQ = 256
NB = 8
NT = 4
NS = NB * NT
TOK = SEQ + NS
F = 2816
FC = F // P
NMOD = 9
NR = 1 + NB
HG = 4
HM = 8
HD = 64
CONV = 4
CC = 12
XW = 3 + SEQ + NB * 7
YW = XW - 3
NPROB = 9
PAGE = 128
NPAGE = 16
NPHYS = 160
PAST = 2048
BLK = 256
NBLK = PAST // BLK
TOPK = 3
EPS = 1e-6
NEG = -1e30
RING = 4
KVR = 8
KU = 12
PHASE = NB * NBLK

UP_TILES = FC // 2
ADA_FIRST = 4
ADA_TILES = NMOD * D // 512


def const_layout():
    names = [("ident", P), ("ones", P), ("tri", P), ("later", P), ("triS", P), ("laterS", P),
             ("lev", 7 * P), ("mh8", P), ("lower8", 64), ("biasS", PAST), ("biasO", 64),
             ("dist", 3 * P), ("hmask", 512), ("selbt", 16), ("bdm", NB)]
    at, out = 0, {}
    for n, w in names:
        out[n] = (at, at + w)
        at += w
    return out, at


def make_consts():
    lay, width = const_layout()
    c = np.zeros((P, width), np.float32)
    i = np.arange(P)

    def put(name, value):
        a, b = lay[name]
        c[:, a:b] = value

    put("ident", np.eye(P))
    put("ones", 1.0)
    put("tri", i[:, None] <= i[None, :])
    put("later", i[:, None] > i[None, :])
    same = i[:, None] // NT == i[None, :] // NT
    put("triS", same & (i[:, None] <= i[None, :]))
    put("laterS", same & (i[:, None] > i[None, :]))
    lev = np.zeros((P, 7, P))
    for l in range(7):
        s, t = i[:, None], i[None, :]
        lev[:, l, :] = (s >> (l + 1) == t >> (l + 1)) & ((s >> l) % 2 == 0) & ((t >> l) % 2 == 1)
    put("lev", lev.reshape(P, -1))
    put("mh8", (i[:, None] % 4 == i[None, :] // NS) & (i[:, None] < 8))
    n, m = np.arange(64) // 8, np.arange(64) % 8
    put("lower8", np.broadcast_to(m < n, (P, 64)))
    h, t = (i % 32) // NT, i % NT
    slope = 2.0 ** -(h + 1.0)
    put("biasS", slope[:, None] * (np.arange(PAST)[None, :] - PAST - t[:, None]))
    own = np.zeros((P, 2, 32))
    for g in range(2):
        j = np.arange(32)
        ok = (j[None, :] // NT == 4 * g + i[:, None] // 32) & (j[None, :] % NT <= t[:, None])
        own[:, g, :] = np.where(ok, slope[:, None] * (j[None, :] % NT - t[:, None]), NEG)
    put("biasO", own.reshape(P, -1))
    d0 = np.where(i[None, :] <= i[:, None], i[None, :] - i[:, None], NEG)
    k = np.arange(SEQ)
    d1 = np.where(k[None, :] <= P + i[:, None], k[None, :] - P - i[:, None], NEG)
    put("dist", np.concatenate([d0, d1], 1))
    put("hmask", h[:, None] == np.arange(512)[None, :] // HD)
    put("selbt", (i[:, None] // 32) * NT + t[:, None] == np.arange(16)[None, :])
    put("bdm", ((i % NS) // NT)[:, None] == np.arange(NB)[None, :])
    return c


def build_program(nc, a, o):
    lay, cwidth = const_layout()
    with ExitStack() as ctx:
        def sb(name, shape, dt=F32):
            return ctx.enter_context(nc.sbuf_tensor(name, shape, dt))

        def sem(name):
            return ctx.enter_context(nc.semaphore(name))

        ps = [ctx.enter_context(nc.psum_tensor(f"bank{i}", [P, 512], F32)) for i in range(8)]

        const = sb("const", [P, cwidth])

        def cst(name):
            return const[:, lay[name][0]:lay[name][1]]

        def shaped(v, *shape):
            n = int(np.prod(shape))
            v = v[:, 0:n]
            if len(shape) == 2:
                v = v.rearrange("p (a b) -> p a b", a=shape[0])
            if len(shape) == 3:
                v = v.rearrange("p (a b c) -> p a b c", a=shape[0], b=shape[1])
            return v

        def carver(flat):
            at = [0]

            def take(*shape):
                n = int(np.prod(shape))
                assert at[0] + n <= flat.shape[1], (at, n)
                v = shaped(flat[:, at[0]:at[0] + n], *shape)
                at[0] += n
                return v
            return take

        wflat = sb("wring", [P, RING * 4096])
        wring = wflat[:, :].rearrange("p (s k n) -> p s k n", s=RING, k=8)
        kv = sb("kv", [P, KVR, 2, 512])
        h = sb("h", [P, KD, TOK])
        hn = sb("hn", [P, KD, TOK])
        mix = hn
        xsf = sb("xs", [P, KD * TOK])
        xs = shaped(xsf, KD, TOK)
        rstd = sb("rstd", [P, TOK])
        modT = sb("modT", [P, NMOD * KD, NR])
        coef = sb("coef", [P, KD, NR])
        gate = sb("gate", [P, KD, NR])
        samp = sb("samp", [P, 2, NB, NT])
        pvec = sb("pvec", [P, 153])
        eps = sb("eps", [P, 1])
        cT = sb("cT", [P, KD, 32])
        adaf = sb("adasb", [P, 1024])
        adasb = shaped(adaf, 2, 512)
        sgf = sb("sgate", [P, 2 * TOK])
        sgate = shaped(sgf, 2, TOK)
        region = sb("region", [P, 11952])
        ytok = shaped(region, 3, D)
        hid = shaped(region, FC, TOK)
        vown = sb("vown", [NS, 512])
        ptab = sb("ptab", [1, 2 * PHASE], I32)

        pro = carver(region)
        xin = pro(3, D)
        cin = pro(D)
        csil = pro(D)
        prow = pro(P)
        crow = pro(P)
        srow = pro(CC * P)

        reg = carver(region)
        XC = reg(CC, XW)
        Yb = reg(4, XW)
        Cv = reg(CC, TOK)
        mqT = reg(4, TOK)
        mkT = reg(4, TOK)
        mvT = reg(4, TOK)
        cst3 = sb("cst3", [P, CC, 24])
        z4 = carver(xsf)
        zs = z4(HG, TOK)
        goT = z4(HG, TOK)
        pa = carver(wflat)
        ktok = pa(3, 512)
        vtok = pa(3, 512)
        psS = pa(2, 384)
        psP = pa(2, 384)
        psT = pa(2, 384)
        cgat = pa(CC, 27)
        cout = pa(CC * P)
        patt = pa(32)
        go4 = carver(xsf[:, HG * TOK:])
        sc8 = go4(3, TOK)
        gE = go4(2, P)
        gd = carver(wflat)
        SQ_AT = 3 * NPROB * P + 8 * TOK + 2 * NPROB * P
        RS_AT = SQ_AT + 3 * NPROB * P
        gR = gd(NPROB, P)
        EG = gd(NPROB, P)
        DT = gd(NPROB, P)
        QK = gd(8, TOK)
        AN = gd(NPROB, 2, P)
        KB = gd(NPROB, P)
        KDc = gd(NPROB, P)
        VB = gd(NPROB, P)
        X = gd(NPROB, P)
        XT = gd(NPROB, P)
        Pv = gd(NPROB, P)
        S1 = gd(HG, P)
        smp = gd(3, P)
        sq8 = shaped(wflat[:, SQ_AT:SQ_AT + 8 * TOK], 8, TOK)
        RS = shaped(wflat[:, RS_AT:RS_AT + 8 * TOK], 8, TOK)
        WQ = gd(HG * NB, 8)
        VN, WT, NTl = X, Pv, gR
        VX = shaped(QK.rearrange("p a b -> p (a b)"), NB, P)
        QD = shaped(DT.rearrange("p a b -> p (a b)"), NPROB, P)
        sqg = shaped(QK.rearrange("p a b -> p (a b)"), 8, TOK)
        dead = const[:, lay["biasS"][0]:lay["biasS"][1]]
        mq_at = CC * XW + 4 * XW + CC * TOK
        st = [shaped(region[:, mq_at + NB * P * x:mq_at + NB * P * (x + 1)], NB, P) for x in range(3)]
        st.append(shaped(dead[:, NB * P:2 * NB * P], NB, P))
        gb = sb("gb", [P, 400])
        gsm = carver(gb)
        abT = sb("abT", [8, TOK])
        wab = sb("wab", [P, KD, 8])
        pab = sb("pab", [8, 4])
        GB = gsm(6, 8)
        G9 = gsm(NPROB)
        B9 = gsm(NPROB)
        cum = gsm(18)
        ecum = gsm(18)
        bek = gsm(NPROB)
        at_ = carver(region)
        S = at_(2, PAST)
        ktb = shaped(wflat[:, 8964:8964 + 2048], 2, 2, 512)
        extra = wring[:, 3]
        pT = shaped(dead[:, 0:512], 2, 2, P)
        Om = dead[:, 512:1024]
        pex = shaped(sgf, 2, BLK)
        Qbd = shaped(adaf, 4, NB, 32)
        gts = at_(2, NBLK)
        bmx = at_(2, NBLK + 1)
        pen = at_(2, NBLK + 1)
        cmpA = at_(64)
        cmpB = at_(64)
        cnt = at_(NBLK)
        negm = at_(2)
        sown = at_(2, 32)
        pown = at_(2, 32)
        rsum = at_(2, NBLK + 1)
        rin = at_(8)
        ownT = at_(2, P)

        ident, ones, tri, later = cst("ident"), cst("ones"), cst("tri"), cst("later")
        triS, laterS = cst("triS"), cst("laterS")
        lev = shaped(cst("lev"), 7, P)
        bw = pvec[:, 0:NMOD * KD]
        nw = pvec[:, 72:104]
        gnw = pvec[:, 104:105]
        cw = pvec[:, 105:153]

        s_cst = sem("s_first_consts_landed")
        s_cst2 = sem("s_consts_landed")
        s_x = sem("s_x_landed")
        s_c = sem("s_c_landed")
        s_par = sem("s_params_landed")
        s_pab = sem("s_decay_params_landed")
        s_ini = sem("s_memsets")
        s_cs = sem("s_csilu")
        s_xT = sem("s_xT_psum")
        s_pT0 = sem("s_params_psum")
        s_cT = sem("s_cT_ready")
        s_w = [sem(f"s_w{i}_landed") for i in range(RING)]
        s_adamm = sem("s_ada_psum")
        s_adaev = sem("s_ada_copied")
        s_adaT = sem("s_ada_transposed")
        s_modr = sem("s_mod_reduced")
        s_mod = sem("s_mod_ready")
        s_h = sem("s_h_chunks")
        s_sq = sem("s_squares")
        s_ss = sem("s_sumsq_psum")
        s_ln = sem("s_ln")
        s_rstd = sem("s_rstd")
        s_xs = sem("s_xs_chunks")
        s_hs = sem("s_hn_sample_ready")
        s_hn = sem("s_hn_chunks")
        s_gate = sem("s_gate_psum")
        s_up = sem("s_up_psum")
        s_silu = sem("s_silu")
        s_hid = sem("s_hidden")
        s_dpart = sem("s_down_tile_read")
        s_sub = sem("s_sublayer_psum")
        s_dve = sem("s_dve_chain")
        s_act = sem("s_act_chain")
        s_wab = sem("s_wab_landed")
        s_win = sem("s_win_psum")
        s_xc = sem("s_xc_copied")
        s_zm = sem("s_zqkv_copied")
        s_ab = sem("s_ab_copied")
        s_conv = sem("s_conv_taps")
        s_csil = sem("s_conv_silu")
        s_cg = sem("s_conv_rows")
        s_kvT = sem("s_kv_transposed")
        s_kvt = sem("s_k_tokens")
        s_kvd = sem("s_v_tokens")
        s_cvT = sem("s_convrows_transposed")
        s_cvo = sem("s_convrows_copied")
        s_sc = sem("s_scores_psum")
        s_paS = sem("s_scores_biased")
        s_nm = sem("s_row_max")
        s_pexp = sem("s_probs")
        s_pn = sem("s_probs_scaled")
        s_paT = sem("s_probsT_psum")
        s_pTe = sem("s_probsT_copied")
        s_pav = sem("s_attn_psum")
        s_pao = sem("s_attn_copied")
        s_out = sem("s_outputs")
        s_okv = sem("s_kv_outputs_done")
        s_g8 = sem("s_decay_rows")
        s_gT = sem("s_decay_psum")
        s_gp = sem("s_delta_psum")
        s_ge = sem("s_delta_copied")
        s_gbc = sem("s_decay_spread")
        s_ecum = sem("s_exp_cum")
        s_eg = sem("s_exp_rows")
        s_df = sem("s_decay_diff")
        s_dt = sem("s_decay_exp")
        s_qks = sem("s_qk_squares")
        s_rse = sem("s_qk_rstd")
        s_qkn = sem("s_qk_normalised")
        s_ntl = sem("s_level_masked")
        s_vx = sem("s_vnew_spread")
        s_st = sem("s_states_landed")
        s_go = sem("s_go_sq")
        s_gr = sem("s_go_rstd")
        s_gdn = sem("s_gdn_done")
        s_absx = sem("s_softplus_input")
        s_sp = sem("s_softplus_log")
        s_bmx = sem("s_block_max")
        s_qz = sem("s_qbd_zero")
        s_qbd = sem("s_qbd_ready")
        s_kv = [[sem(f"s_kv{i}_page{y}_landed") for i in range(KU)] for y in range(2)]
        s_vq = [[sem(f"s_vquad{i}_half{y}_landed") for i in range(4)] for y in range(2)]
        s_wo = [sem(f"s_wout{i}_landed") for i in range(2)]
        s_pt = sem("s_page_table")
        s_own = sem("s_own_psum")
        s_owns = sem("s_own_logits_copied")
        s_kt = sem("s_kt_psum")
        s_ktA = sem("s_kt_copied_act")
        s_ktD = sem("s_kt_copied_dve")
        s_qk = sem("s_logits_psum")
        s_lev = sem("s_logits_copied")
        s_pen = sem("s_selection")
        s_po = sem("s_own_probs")
        s_pe = sem("s_sel_probs")
        s_PT = sem("s_sel_probsT_psum")
        s_oT = sem("s_own_probsT_psum")
        s_pTs = sem("s_sel_probsT_copied")
        s_oTs = sem("s_own_probsT_copied")
        s_PV = sem("s_values_read")
        s_O = sem("s_sel_attn_psum")
        s_om = sem("s_sel_attn_scaled")
        s_AT = sem("s_sel_attnT_psum")
        s_mixa = sem("s_sel_attn_ready")
        s_yT = sem("s_y_transposed")
        s_y = sem("s_y_copied")
        block = ctx.enter_context(nc.Block())

        XCs = XC[:, :, 3 + SEQ:XW].rearrange("p c (b j) -> p c b j", b=NB)

        wada = a["w_ada"][0].rearrange("(k p) n -> p k n", p=P)
        wup = [a["ffn_up"][0, l].rearrange("(k p) (g n) -> p k g n", p=P, g=2) for l in range(2)]
        wdown = [a["ffn_down"][0, l].rearrange("(f p) n -> p f n", p=P) for l in range(2)]
        win = a["w_in"][0].rearrange("(k p) n -> p k n", p=P)
        wout = a["w_out"][0].rearrange("(k p) n -> p k n", p=P)
        WIN_COL = [0, 512, 1024, 1544, 2056, 2568, 3080]

        tiles = [("ada", j) for j in range(ADA_FIRST)] + [("up", 0, 0), ("ada", 4), ("ada", 5)]
        LOOP = len(tiles)
        for i in range(5):
            tiles += [("up", 0, 1 + 2 * i), ("ada", 6 + 2 * i), ("up", 0, 2 + 2 * i), ("ada", 7 + 2 * i)]
        tiles += [("down", 0, 0, 0), ("ada", 16), ("down", 0, 0, 1), ("ada", 17), ("down", 0, 0, 2)]
        tiles += [("down", 0, 1, t) for t in range(3)]
        tiles += [("in", j) for j in range(7)]
        tiles += [("up", 1, j) for j in range(UP_TILES)]
        tiles += [("down", 1, g, t) for g in range(2) for t in range(3)]
        number = {t: n for n, t in enumerate(tiles)}

        def released(t):
            if t[0] == "ada":
                return s_adamm, t[1] + 1
            if t[0] == "up":
                return s_up, FC * t[1] + 2 * t[2] + 2
            if t[0] == "down":
                if t[3] < 2:
                    return s_dpart, 4 * t[1] + 2 * t[2] + t[3] + 1
                return s_sub, 16 * t[1] + 4 * t[2] + 4
            return s_win, 4 * t[1] + 4 + (t[1] >= 4)

        def halves(t, slot, j=None):
            w = wring[:, slot]
            if t[0] == "up":
                j = t[2] if j is None else j
                return [(w[:, :, 256 * g:256 * g + 256], wup[t[1]][:, :, g, bass.ds(j * 256, 256)]) for g in range(2)]
            if t[0] == "ada":
                j = t[1] if j is None else j
                return [(w[:, 4 * k:4 * k + 4, :], wada[:, 4 * k:4 * k + 4, bass.ds(j * 512, 512)]) for k in range(2)]
            if t[0] == "down":
                n = min(8, FC - 8 * t[3]) // 2
                return [(w[:, n * k:n * k + n, :], wdown[t[1]][:, 8 * t[3] + n * k:8 * t[3] + n * k + n, 512 * t[2]:512 * t[2] + 512]) for k in range(2)]
            c0 = WIN_COL[t[1]]
            return [(w[:, 4 * k:4 * k + 4, :], win[:, 4 * k:4 * k + 4, c0:c0 + 512]) for k in range(2)]

        wo = [kv[:, 4 * (1 - g):4 * (1 - g) + 4].rearrange("p a b n -> p (a b) n") for g in range(2)]

        def k_unit(n, x):
            slot = n % 3
            return kv[:, 4 * slot + x] if slot < 2 else shaped(extra[:, 2 * x:2 * x + 2, :].rearrange("p a b -> p (a b)"), 2, 512)

        def v_quad(q):
            return (q + 2) % 4

        def v_page(q, x):
            at = 4 * v_quad(q) + x
            return kv[:, at // 2, at % 2, :]

        cache = [a["cache_k"][0].rearrange("n p h d -> n p (h d)"), a["cache_v"][0].rearrange("n p h d -> n p (h d)")]

        def sample_steps(l):
            return {1: [("W", 2)], 2: [("us",), ("ws",)], 3: [("vs",), ("os",)],
                    4: [("up", k) for k in range(4)], 5: [("up", k) for k in range(4, 8)]}.get(l, [])

        def steps():
            out = [("cum",)] + [("row", j) for j in range(3)] + [("l2", c) for c in range(8)]
            out += [("kt", j) for j in range(3)] + [("vt", j) for j in range(3)] + [("gram", j) for j in range(5)]
            for l in range(7):
                groups = range(3 if l < 2 else 2)
                out += [("P", l, g) for g in groups]
                for g in groups:
                    out += ([("XP", l, g)] if 0 < l < 6 else []) + [("PX", l, g)]
                out += sample_steps(l)
            out += [("W", 1), ("U0",), ("S1",), ("V1",), ("o0",), ("o1",), ("S2",)] + [("rms", hh) for hh in range(HG)]
            return out

        STEPS = {t: k for k, t in enumerate(steps())}

        GBANKS = 5

        def copied(step):
            return s_ge, STEPS[step] + 1

        def page(eng, table, dst, which, landed):
            p = eng.value_load(ptab[0:1, bass.ds(table, 1)], min_val=0, max_val=NPHYS - 1)
            eng.dma_start(dst, cache[which][bass.ds(p, 1), :, :].rearrange("a p n -> (a p) n")).then_inc(landed, 16)

        def k_step(eng, y, k, table):
            for x in range(4):
                page(eng, table + 2 * x + y, k_unit(k % 3, x)[:, y, :], 0, s_kv[y][4 * (k % 3) + x])

        def v_step(eng, half, q, table):
            for x in (2 * half, 2 * half + 1):
                page(eng, table + 2 * x + q % 2, v_page(q, x), 1, s_vq[half][v_quad(q)])

        def stream_rest(eng, half):
            with eng.Fori(1, 5) as i:
                for k in range(3):
                    eng.wait_ge(s_kt, i * 24 + (8 * k - 16))
                    k_step(eng, half, k, i * 24 + 8 * k)
            eng.wait_ge(s_kt, 8 * 13)
            k_step(eng, half, 15, 8 * 15)
            for q in range(4):
                eng.wait_ge(s_kt, 8 * 14 if q < 2 else 8 * 16)
                v_step(eng, half, q, 8 * (q // 2))
            with eng.Fori(1, 8) as i:
                for k in range(4):
                    eng.wait_ge(s_PV, i * 4 + (k - 3))
                    v_step(eng, half, k, i * 16 + 8 * (k // 2))

        @block.sync
        def _(sp):
            sp.dma_start(const[:, 0:lay["tri"][0]], a["consts"][:, 0:lay["tri"][0]]).then_inc(s_cst, 16)

            def load(n):
                t = tiles[n]
                if n >= RING:
                    sp.wait_ge(*released(tiles[n - RING]))
                for dst, src in halves(t, n % RING):
                    sp.dma_start(dst, src).then_inc(s_w[n % RING], 16)

            load(0)
            sp.wait_ge(s_par, 16 * 6)
            for n in range(1, LOOP + 4):
                load(n)
            sp.dma_start(const[:, lay["tri"][0]:cwidth], a["consts"][:, lay["tri"][0]:cwidth]).then_inc(s_cst2, 16)
            with sp.Fori(1, 5) as i:
                for k in range(4):
                    kind, slot = ("up", "ada", "up", "ada")[k], (LOOP + k) % RING
                    if kind == "up":
                        j = i * 2 + 1 + k // 2
                        sp.wait_ge(s_up, j * 2 - 2)
                        t = ("up", 0, 0)
                    else:
                        j = i * 2 + 6 + k // 2
                        sp.wait_ge(s_adamm, j - 1)
                        t = ("ada", 0)
                    for dst, src in halves(t, slot, j):
                        sp.dma_start(dst, src).then_inc(s_w[slot], 16)
            first_in = number[("in", 0)]
            for n in range(LOOP + 20, first_in):
                load(n)
            sp.wait_ge(s_pt, 16)
            for n in range(2):
                k_step(sp, 0, n, 8 * n)
            for n in range(first_in, first_in + 7):
                load(n)
            sp.wait_ge(*released(("in", 4)))
            k_step(sp, 0, 2, 16)
            stream_rest(sp, 0)
            for g in range(2):
                sp.wait_ge(s_PV, 30 + 2 * g)
                for k in range(2):
                    sp.dma_start(wo[g][:, 4 * k:4 * k + 4, :], wout[:, 4 * k:4 * k + 4, 512 * g:512 * g + 512]).then_inc(s_wo[g], 16)
            sp.wait_ge(s_gdn, 1)
            sp.wait_ge(s_okv, 16 * 7)
            for n in range(first_in + 7, len(tiles)):
                load(n)

        @block.gpsimd
        def _(pool):
            pool.dma_start(xin[:, 0:2, :], a["x_prompt"][0].rearrange("(t p) d -> p t d", p=P)).then_inc(s_x, 16)
            pool.dma_start(xin[0:NS, 2, :], a["x_sample"].rearrange("b t d -> (b t) d")).then_inc(s_x, 16)
            pool.memset(cT[:], 0.0).then_inc(s_ini, 1)
            pool.memset(pab[:], 0.0).then_inc(s_ini, 1)
            pool.memset(eps[:], EPS).then_inc(s_ini, 1)

            def square(ni):
                for c in range(KD):
                    pool.wait_ge(s_h, KD * ni + c + 1)
                    nc.gpsimd.tensor_tensor(xs[:, c, :], h[:, c, :], h[:, c, :], ALU.mult).then_inc(s_sq, 1)

            square(0)
            pool.wait_ge(s_adaT, ADA_TILES)
            pool.memset(adaf[:], 0.0).then_inc(s_qz, 1)
            pool.wait_ge(s_pt, 16)
            for n in range(2):
                k_step(pool, 1, n, 8 * n)
            square(1)
            pool.wait_ge(*released(("in", 4)))
            k_step(pool, 1, 2, 16)
            pool.wait_ge(s_kvt, 3)
            pool.wait_ge(s_kvd, 3)
            for name, buf in (("k", ktok), ("v", vtok)):
                pool.dma_start(o[name + "_prompt"][0, 0].rearrange("(t p) h d -> p t (h d)", p=P), buf[:, 0:2, :]).then_inc(s_okv, 16)
                pool.dma_start(o[name + "_sample"][0].rearrange("b t h d -> (b t) (h d)"), buf[0:NS, 2, :]).then_inc(s_okv, 16)
            pool.wait_ge(s_cvo, 3)
            pool.dma_start(o["conv_prompt"][0, 0], cout[0:3, :]).then_inc(s_okv, 16)
            pool.dma_start(o["conv_sample"][0].rearrange("b i n -> (b i) n"), cout[3:27, :]).then_inc(s_okv, 16)
            stream_rest(pool, 1)
            pool.wait_ge(*copied(("S2",)))
            pool.dma_start(o["gdn_prompt"][0, 0].rearrange("h k v -> k h v"), S1).then_inc(s_okv, 16)
            pool.wait_ge(*copied(("up", 7)))
            for hh in range(HG):
                pool.dma_start(o["gdn_sample"][0, :, hh].rearrange("b k v -> k b v"), st[hh]).then_inc(s_out, 16)
            square(2)
            square(3)
            pool.wait_ge(s_y, 6)
            pool.dma_start(o["y_prompt"][0].rearrange("(t p) n -> p t n", p=P), ytok[:, 0:2, :]).then_inc(s_out, 16)
            pool.dma_start(o["y_sample"].rearrange("b t n -> (b t) n"), ytok[0:NS, 2, :]).then_inc(s_out, 16)
            pool.wait_ge(s_out, 16 * 6)
            pool.wait_ge(s_okv, 16 * 7)



        AB_TURN = 16

        def win_turn(q):
            return q + (q >= AB_TURN)

        def left_bank(turn):
            if turn < CC:
                return s_xc, turn + 1
            if turn == AB_TURN:
                return s_ab, 1
            return s_zm, turn - CC + (turn < AB_TURN)

        def sum_bank(ni):
            return 4 if ni else 0

        def probs(g):
            return [range(0, 4), range(4, 8), range(8, 9)][g]

        @block.tensor
        def _(pe):
            def T(out, in_, n):
                return nc.tensor.transpose(out, in_, ident[0:n, 0:n])

            def landed(n):
                pe.wait_ge(s_w[n % RING], 32 * (n // RING + 1))

            pe.wait_ge(s_cst, 16)
            pe.wait_ge(s_cs, 1)
            for k in range(KD):
                m = T(ps[4][:, 16 * k:16 * k + NR], csil[0:NR, k * P:(k + 1) * P], NR)
            m.then_inc(s_pT0, 1)
            def ada_mm(j, slot, wait, bank=None):
                pe.wait_ge(*wait)
                if not isinstance(j, int) or j >= 2:
                    pe.wait_ge(s_adaev, j - 1)
                for k in range(KD):
                    q = 32 * (k % 4)
                    m = nc.tensor.matmul(ps[ada_bank(j) if bank is None else bank][q:q + 32, :], cT[:, k, :], wring[:, slot, k, :],
                                         start=(k < 4), stop=(k >= 4), tile_position=(0, q))
                m.then_inc(s_adamm, 1)

            par = [0]

            def ada_bank(j):
                return 4 + (j if isinstance(j, int) else par[0]) % 2

            def ada_T(j, odd, bank=None):
                pe.wait_ge(s_adaev, j + 1)
                if not isinstance(j, int) or j >= 2:
                    pe.wait_ge(s_modr, j - 1)
                for i in range(4):
                    m = T(ps[6 + odd if bank is None else bank][:, i * P:(i + 1) * P], adasb[:, odd, i * P:(i + 1) * P], P)
                m.then_inc(s_adaT, 1)

            def up_tile(l, j, slot, wait, first=False):
                pe.wait_ge(*wait)
                for s in range(2):
                    if not first:
                        pe.wait_ge(s_hid, j * 2 + (FC * l + s - 1))
                    for half, done in ((0, s_gate), (1, s_up)):
                        for k in range(KD):
                            if first and s == 0 and half == 0:
                                normed(2 * l, k)
                            m = nc.tensor.matmul(ps[2 * s + half][:, 0:TOK], wring[:, slot, k, 256 * half + P * s:256 * half + P * s + P],
                                                 hn[:, k, :], start=(k == 0), stop=(k == KD - 1))
                        m.then_inc(done, 1)

            def normed(ni, k):
                if k == 0:
                    pe.wait_ge(s_hs, ni + 1)
                pe.wait_ge(s_hn, KD * ni + k + 1)

            def sumsq(ni):
                for k in range(KD):
                    pe.wait_ge(s_sq, KD * ni + k + 1)
                    m = nc.tensor.matmul(ps[sum_bank(ni)][:, 0:TOK], ones, xs[:, k, :], start=(k == 0), stop=(k == KD - 1))
                m.then_inc(s_ss, 1)

            def down(l):
                pe.wait_ge(s_hid, FC * (l + 1))
                for g in range(2):
                    for t in range(3):
                        landed(number[("down", l, g, t)])
                        slot = number[("down", l, g, t)] % RING
                        n = min(8, FC - 8 * t)
                        for i in range(4):
                            if l == 0 and g == 0 and t == 0 and i == 3:
                                pe.wait_ge(s_modr, 16)
                            for f in range(n):
                                m = nc.tensor.matmul(ps[4 * (1 - g) + i][:, 0:TOK], wring[:, slot, f, i * P:(i + 1) * P],
                                                     hid[:, 8 * t + f, :], start=(t == 0 and f == 0), stop=(t == 2 and f == n - 1))
                            if t == 2:
                                m.then_inc(s_sub, 1)
                        if t < 2:
                            m.then_inc(s_dpart, 1)
                        if l == 0 and g == 0 and t == 0:
                            ada_mm(16, *tile(("ada", 16)), bank=0)
                        elif l == 0 and g == 0 and t == 1:
                            ada_T(16, 0, bank=2)
                            ada_mm(17, *tile(("ada", 17)), bank=1)
                        elif l == 0 and g == 0:
                            ada_T(17, 1, bank=3)
                            pe.wait_ge(s_modr, ADA_TILES)

            def tile(t):
                n = number[t]
                return n % RING, (s_w[n % RING], 32 * (n // RING + 1))

            def features():
                pe.wait_ge(s_par, 16 * 6)
                T(ps[5][:, 0:105], prow[0:105, :], 105)
                T(ps[5][:, 105:153], crow[0:48, :], 48)
                for c in range(CC):
                    m = T(ps[6][:, 24 * c:24 * c + 24], srow[0:24, c * P:(c + 1) * P], 24)
                m.then_inc(s_pT0, 1)
                pe.wait_ge(s_x, 32)
                for c in range(KD):
                    if c >= 4:
                        pe.wait_ge(s_h, c - 3)
                    for t in range(3):
                        n = P if t < 2 else NS
                        m = T(ps[c % 4][:, t * P:t * P + n], xin[0:n, t, c * P:(c + 1) * P], n)
                    m.then_inc(s_xT, 1)

            pe.wait_ge(s_cT, 1)
            for j in range(ADA_FIRST):
                ada_mm(j, *tile(("ada", j)))
                if j == 0:
                    features()
                if j:
                    ada_T(j - 1, (j - 1) % 2)
            sumsq(0)
            ada_T(3, 1)
            up_tile(0, 0, *tile(("up", 0, 0)), first=True)
            ada_mm(4, *tile(("ada", 4)))
            ada_mm(5, *tile(("ada", 5)))
            ada_T(4, 0)
            with pe.Fori(0, 5) as i:
                for k in range(2):
                    slot = (LOOP + 2 * k) % RING
                    up_tile(0, i * 2 + 1 + k, slot, (s_w[slot], i * 32 + 32 * ((LOOP + 2 * k) // RING + 1)))
                    ada_T(i * 2 + 5 + k, (5 + k) % 2)
                    slot = (LOOP + 1 + 2 * k) % RING
                    par[0] = 6 + k
                    ada_mm(i * 2 + 6 + k, slot, (s_w[slot], i * 32 + 32 * ((LOOP + 1 + 2 * k) // RING + 1)))
            ada_T(15, 1)
            pe.wait_ge(s_modr, 15)
            down(0)

            sumsq(1)
            for turn in range(29):
                q = None if turn == AB_TURN else turn - (turn > AB_TURN)
                if turn >= 8:
                    pe.wait_ge(*left_bank(turn - 8))
                if q is None:
                    pe.wait_ge(s_wab, 16)
                elif q % 4 == 0:
                    landed(number[("in", q // 4)])
                for k in range(KD):
                    if turn == 0:
                        normed(1, k)
                    w = wab[:, k, :] if q is None else wring[:, number[("in", q // 4)] % RING, k, (q % 4) * P:(q % 4 + 1) * P]
                    m = nc.tensor.matmul(ps[turn % 8][0:w.shape[1], 0:TOK], w, hn[:, k, :], start=(k == 0), stop=(k == KD - 1))
                m.then_inc(s_win, 1)

            pe.wait_ge(s_g8, 1)
            pe.wait_ge(*left_bank(23))
            for i in range(6):
                src = sc8[0:8, 2 * (i // 3), :]
                spread = gE[0:8, i // 3, :]
                m = T(ps[7][:, 8 * i:8 * i + 8], src[:, (i % 3) * P:(i % 3) * P + P] if i % 3 < 2 else spread, 8)
            m.then_inc(s_gT, 1)

            pe.wait_ge(s_zm, 16)
            pe.wait_ge(s_ab, 1)
            for q in range(6):
                src, t = (mkT, mvT)[q % 2], q // 2
                n = P if t < 2 else NS
                for c in range(4):
                    m = T(ps[q][0:n, c * P:(c + 1) * P], src[:, c, t * P:t * P + n], P)
                m.then_inc(s_kvT, 1)
            pe.wait_ge(s_cg, 1)
            for r in range(3):
                if r == 1:
                    pe.wait_ge(s_gbc, 1)
                if r == 2:
                    pe.wait_ge(s_kvt, 1)
                bank = ps[(6, 7, 0)[r]]
                for c in range(4):
                    m = T(bank[0:27, c * P:(c + 1) * P], cgat[:, 4 * r + c, :], P)
                m.then_inc(s_cvT, 1)

            mm = nc.tensor.matmul
            pe.wait_ge(s_kvt, 3)
            pe.wait_ge(s_cvo, 3)
            pe.wait_ge(s_qbd, 8)
            for g in range(2):
                for b4 in range(4):
                    for c in range(4):
                        m = mm(ps[6][32 * b4:32 * b4 + 32, 384 + 32 * g:416 + 32 * g], Qbd[:, c, 4 * g + b4, :], mkT[:, c, SEQ:TOK],
                               start=(c == 0), stop=(c == 3), tile_position=(0, 32 * b4))
                m.then_inc((s_qk, s_own)[g], 2 - g)

            def attention(s):
                if s < HM:
                    c, r = s // 2, HD * (s % 2)
                    if s:
                        pe.wait_ge(s_paS, s)
                    mm(ps[5][:, 0:P], mqT[r:r + HD, c, 0:P], mkT[r:r + HD, c, 0:P], start=True, stop=True)
                    mm(ps[5][:, P:3 * P], mqT[r:r + HD, c, P:SEQ], mkT[r:r + HD, c, 0:SEQ], start=True, stop=True).then_inc(s_sc, 1)
                if 1 <= s <= HM:
                    x = s - 1
                    pe.wait_ge(s_pn, x + 1)
                    if x:
                        pe.wait_ge(s_pTe, x)
                    else:
                        pe.wait_ge(s_owns, 1)
                    for i in range(3):
                        m = T(ps[6][:, i * P:(i + 1) * P], psP[:, x % 2, i * P:(i + 1) * P], P)
                    m.then_inc(s_paT, 1)
                if 2 <= s < HM + 2:
                    x = s - 2
                    c, r = x // 2, HD * (x % 2)
                    pe.wait_ge(s_pTe, x + 1)
                    if x == 0:
                        pe.wait_ge(s_gbc, 1)
                    if x % 2 == 0 and c:
                        pe.wait_ge(s_pao, c)
                    out = ps[7][r:r + HD, 0:SEQ]
                    mm(out, vtok[:, 0, x * HD:(x + 1) * HD], psT[:, x % 2, 0:SEQ], start=True, stop=False)
                    mm(out[:, P:SEQ], vtok[:, 1, x * HD:(x + 1) * HD], psT[:, x % 2, SEQ:3 * P], start=False, stop=True).then_inc(s_pav, 1)

            def logits(m):
                n, c = m // 4, m % 4
                pe.wait_ge(s_ktA, m + 3)
                pe.wait_ge(s_ktD, m + 3)
                if c == 0:
                    pe.wait_ge(s_lev, n + 1)
                for b4 in range(4):
                    ins = mm(ps[4][32 * b4:32 * b4 + 32, 0:BLK], Qbd[:, c, 4 * (n // NBLK) + b4, :],
                             ktb[:, c % 2, b4 // 2, (b4 % 2) * BLK:(b4 % 2 + 1) * BLK],
                             start=(c == 0), stop=(c == 3), tile_position=(0, 32 * b4))
                ins.then_inc(s_qk, 1)

            for m in range(4 * 2 * NBLK):
                n, c = m // 4, m % 4
                for pair in range(2):
                    pe.wait_ge((s_ktA, s_ktD)[pair], m + 1)
                    for x in range(2):
                        if c == 0:
                            for y in range(2):
                                pe.wait_ge(s_kv[y][4 * (n % 3) + 2 * pair + x], 16 * (n // 3 + 1))
                        for y in range(2):
                            ins = T(ps[2 * (c % 2) + pair][:, x * BLK + y * PAGE:x * BLK + (y + 1) * PAGE],
                                    k_unit(n, 2 * pair + x)[:, y, c * P:(c + 1) * P], P)
                    ins.then_inc(s_kt, 1)
                if c == 2:
                    attention(n)
                if m:
                    logits(m - 1)
            logits(4 * 2 * NBLK - 1)

            def values(n):
                if n < 2 * NBLK:
                    if n % NBLK == 0:
                        g = n // NBLK
                        pe.wait_ge(s_po, g + 1)
                        T(ps[6][0:32, BLK + P * g:BLK + P * g + P], pown[:, g, :], P).then_inc(s_oT, 1)
                    pe.wait_ge(s_pe, n + 1)
                    if n:
                        pe.wait_ge(s_pTs, n)
                    for y in range(2):
                        m = T(ps[5][:, y * P:(y + 1) * P], pex[:, n % 2, y * P:(y + 1) * P], P)
                    m.then_inc(s_PT, 1)
                if n == NBLK + 1:
                    gathered(0)
                n -= 1
                if n < 0:
                    return
                g, blk = n // NBLK, n % NBLK
                pe.wait_ge(s_pTs, n + 1)
                for y in range(2):
                    q = 2 * n + y
                    for half in range(2):
                        pe.wait_ge(s_vq[half][v_quad(q)], 32 * (q // 4 + 1))
                    for b4 in range(4):
                        m = mm(ps[7][32 * b4:32 * b4 + 32, :], pT[:, n % 2, y, 32 * b4:32 * b4 + 32], v_page(q, b4),
                               start=(blk == 0 and y == 0), stop=False, tile_position=(0, 32 * b4))
                    m.then_inc(s_PV, 1)
                if blk == NBLK - 1:
                    pe.wait_ge(s_oTs, g + 1)
                    for b4 in range(4):
                        m = mm(ps[7][32 * b4:32 * b4 + 32, :], ownT[0:32, g, 32 * b4:32 * b4 + 32], vown[0:32, :],
                               start=False, stop=True, tile_position=(0, 32 * b4))
                    m.then_inc(s_O, 1)

            def gathered(g):
                pe.wait_ge(s_om, g + 1)
                for c in range(4):
                    m = mm(ps[6][:, 64 * g + 16 * c:64 * g + 16 * c + 16], Om[:, c * P:(c + 1) * P], cst("selbt"), start=True, stop=True)
                m.then_inc(s_AT, 1)

            def bank(step):
                k = STEPS[step]
                if k >= GBANKS:
                    pe.wait_ge(s_ge, k - GBANKS + 1)
                return ps[k % GBANKS]

            pe.wait_ge(s_gbc, 2)
            pe.wait_ge(s_pao, 4)
            pe.wait_ge(s_lev, 2 * NBLK + 1)
            b = bank(("cum",))
            mm(b[:, 0:8], tri, G9[:, 0:8], start=True, stop=True)
            mm(b[:, 8:9], triS, G9[:, 8:9], start=True, stop=True)
            mm(b[:, 9:17], later, G9[:, 0:8], start=True, stop=True)
            mm(b[:, 17:18], laterS, G9[:, 8:9], start=True, stop=True).then_inc(s_gp, 1)
            for j in range(3):
                b = bank(("row", j))
                for x, p in enumerate(probs(j)):
                    m = mm(b[:, x * P:(x + 1) * P], Pv[:, p, :], tri if p < 8 else triS, start=True, stop=True)
                m.then_inc(s_gp, 1)
            values(0)
            pe.wait_ge(s_qks, 1)
            for c in range(8):
                mm(bank(("l2", c))[:, 0:TOK], ones, sq8[:, c, :], start=True, stop=True).then_inc(s_gp, 1)
            values(1)
            pe.wait_ge(s_qkn, 1)
            for kind, base in (("kt", 4), ("vt", 8)):
                for j in range(3):
                    b = bank((kind, j))
                    for x, p in enumerate(probs(j)):
                        if p == 8:
                            src = smp[:, 1 if kind == "kt" else 2, :]
                        else:
                            src = (QK if kind == "kt" else Cv)[:, base + p % 4, (p // 4) * P:(p // 4 + 1) * P]
                        m = T(b[:, x * P:(x + 1) * P], src, P)
                    m.then_inc(s_gp, 1)
            values(2)
            QKh = QK.rearrange("p (two hh) n -> p hh two n", two=2)
            for j in range(5):
                b = bank(("gram", j))
                for x, p in enumerate(range(2 * j, min(2 * j + 2, NPROB))):
                    if p == 8:
                        k_, qk_ = smp[:, 1, :], smp[:, 0:2, :]
                    else:
                        cols = slice((p // 4) * P, (p // 4 + 1) * P)
                        k_, qk_ = QK[:, 4 + p % 4, cols], QKh[:, p % 4, :, cols]
                    m = mm(b[:, 2 * P * x:2 * P * (x + 1)], k_, qk_, start=True, stop=True)
                m.then_inc(s_gp, 1)
            values(3)

            def w_rows(g):
                b = bank(("W", g))
                for x, p in enumerate(probs(g)):
                    m = mm(b[:, x * P:(x + 1) * P], KB[:, p, :], XT[:, p, :], start=True, stop=True)
                m.then_inc(s_gp, 1)

            def sample(l):
                if l == 1:
                    pe.wait_ge(*copied(("PX", 1, 2)))
                    w_rows(2)
                elif l == 2:
                    mm(bank(("us",))[:, 0:P], VB[:, 8, :], XT[:, 8, :], start=True, stop=True).then_inc(s_gp, 1)
                    pe.wait_ge(*copied(("W", 2)))
                    pe.wait_ge(s_st, 64)
                    b = bank(("ws",))
                    for x in range(HG * NB):
                        m = mm(b[:, 8 * x:8 * x + 8], st[x // NB][:, x % NB, :], WQ[:, x, :], start=True, stop=True)
                    m.then_inc(s_gp, 1)
                elif l == 3:
                    pe.wait_ge(*copied(("ws",)))
                    T(bank(("vs",))[:, 0:P], VX[:, 0, :], P).then_inc(s_gp, 1)
                    pe.wait_ge(*copied(("vs",)))
                    mm(bank(("os",))[:, 0:P], VN[:, 8, :], AN[:, 8, 0, :], start=True, stop=True).then_inc(s_gp, 1)
                elif l in (4, 5):
                    pe.wait_ge(s_vx, 1)
                    for x in range(4 * l - 16, 4 * l - 12):
                        hh, half = x // 2, x % 2
                        rows = slice(NS * hh, NS * hh + NS)
                        mm(bank(("up", x))[:, :], KDc[rows, 8, :], VX[rows, 4 * half:4 * half + 4, :].rearrange("p a b -> p (a b)"),
                           start=True, stop=True).then_inc(s_gp, 1)

            nt = 0
            for l in range(7):
                groups = range(3 if l < 2 else 2)
                for g in groups:
                    b = bank(("P", l, g))
                    nt += 1
                    pe.wait_ge(s_ntl, nt)
                    if l:
                        pe.wait_ge(*copied(("PX", l - 1, g)))
                    for x, p in enumerate(probs(g)):
                        m = mm(b[:, x * P:(x + 1) * P], NTl[:, p, :], X[:, p, :] if l else ident, start=True, stop=True)
                    m.then_inc(s_gp, 1)
                values(4 + 2 * l)
                for g in groups:
                    pe.wait_ge(*copied(("P", l, g)))
                    if 0 < l < 6:
                        b = bank(("XP", l, g))
                        for x, p in enumerate(probs(g)):
                            m = mm(b[:, x * P:(x + 1) * P], XT[:, p, :], Pv[:, p, :], start=True, stop=True)
                        m.then_inc(s_gp, 1)
                    b = bank(("PX", l, g))
                    for x, p in enumerate(probs(g)):
                        m = mm(b[:, x * P:(x + 1) * P], Pv[:, p, :], XT[:, p, :] if l else ident, start=True, stop=True)
                    m.then_inc(s_gp, 1)
                if l < 6:
                    values(5 + 2 * l)
                sample(l)
            pe.wait_ge(*copied(("PX", 6, 1)))
            w_rows(1)
            b = bank(("U0",))
            for x in range(4):
                m = mm(b[:, x * P:(x + 1) * P], XT[:, x, :], VB[:, x, :], start=True, stop=True)
            m.then_inc(s_gp, 1)
            pe.wait_ge(*copied(("U0",)))
            b = bank(("S1",))
            for x in range(4):
                m = mm(b[:, x * P:(x + 1) * P], KDc[:, x, :], VN[:, x, :], start=True, stop=True)
            m.then_inc(s_gp, 1)
            pe.wait_ge(*copied(("S1",)))
            b = bank(("V1",))
            for x in range(4):
                mm(b[:, x * P:(x + 1) * P], XT[:, 4 + x, :], VB[:, 4 + x, :], start=True, stop=False)
                m = mm(b[:, x * P:(x + 1) * P], WT[:, 4 + x, :], S1[:, x, :], start=False, stop=True)
            m.then_inc(s_gp, 1)
            b = bank(("o0",))
            for x in range(4):
                m = mm(b[:, x * P:(x + 1) * P], VN[:, x, :], AN[:, x, 0, :], start=True, stop=True)
            m.then_inc(s_gp, 1)
            pe.wait_ge(*copied(("V1",)))
            b = bank(("o1",))
            for x in range(4):
                mm(b[:, x * P:(x + 1) * P], VN[:, 4 + x, :], AN[:, 4 + x, 0, :], start=True, stop=False)
                m = mm(b[:, x * P:(x + 1) * P], S1[:, x, :], QD[:, 4 + x, :], start=False, stop=True)
            m.then_inc(s_gp, 1)
            b = bank(("S2",))
            for x in range(4):
                m = mm(b[:, x * P:(x + 1) * P], KDc[:, 4 + x, :], VN[:, 4 + x, :], start=True, stop=True)
            m.then_inc(s_gp, 1)
            gathered(1)
            pe.wait_ge(s_go, 1)
            for hh in range(HG):
                mm(bank(("rms", hh))[:, 0:TOK], ones, sqg[:, hh, :], start=True, stop=True).then_inc(s_gp, 1)

            pe.wait_ge(s_mixa, 2)
            pe.wait_ge(s_ge, len(STEPS))
            for g in range(2):
                pe.wait_ge(s_wo[g], 32)
                for part in (range(4, 8), range(4)):
                    if part[0] == 0 and g == 0:
                        pe.wait_ge(s_gdn, 1)
                    for i in range(4):
                        for k in part:
                            m = mm(ps[4 * (1 - g) + i][:, 0:TOK], wo[g][:, k, i * P:(i + 1) * P], mix[:, k, :],
                                   start=(k == 4), stop=(k == 3))
                        if part[0] == 0:
                            m.then_inc(s_sub, 1)

            sumsq(2)
            for j in range(3):
                up_tile(1, j, *tile(("up", 1, j)), first=(j == 0))
            with pe.Fori(0, 2) as i:
                for k in range(4):
                    n = number[("up", 1, 3)] + k
                    up_tile(1, i * 4 + 3 + k, n % RING, (s_w[n % RING], i * 32 + 32 * (n // RING + 1)))
            down(1)

            sumsq(3)
            pe.wait_ge(s_hn, KD * 3 + KD)
            for q in range(6):
                t, half = q // 2, q % 2
                n = P if t < 2 else NS
                for c in range(4):
                    m = T(ps[1 + q][0:n, c * P:(c + 1) * P], hn[:, 4 * half + c, t * P:t * P + n], P)
                m.then_inc(s_yT, 1)

        @block.scalar
        def _(act):
            def fn(out, in_, func, **kw):
                return nc.scalar.activation(out, in_, func, **kw)

            def own(ins, s=s_act, count=[0]):
                count[0] += 1
                ins.then_inc(s, 1)
                act.wait_ge(s, count[0])

            act.dma_start(cin[0:1, :], a["c_prompt"]).then_inc(s_c, 16)
            act.dma_start(cin[1:NR, :], a["c_sample"]).then_inc(s_c, 16)
            act.dma_start(prow[0:72, :], a["b_ada"][0].rearrange("(r p) -> r p", p=P)).then_inc(s_par, 16)
            act.dma_start(prow[72:96, :], a["norm_w"][0].rearrange("i (r p) -> (i r) p", p=P)).then_inc(s_par, 16)
            act.dma_start(prow[96:104, :], a["final_norm_w"].rearrange("(r p) -> r p", p=P)).then_inc(s_par, 16)
            act.dma_start(prow[104:105, :], a["gdn_norm_w"]).then_inc(s_par, 16)
            act.dma_start(crow[0:48, :], a["conv_w"][0].rearrange("i (c p) -> (i c) p", p=P)).then_inc(s_par, 16)
            act.dma_start(srow[0:24, :], a["state_conv"][0].rearrange("b i n -> (b i) n")).then_inc(s_par, 16)
            act.wait_ge(s_c, 32)
            fn(csil[0:NR, :], cin[0:NR, :], ACT.Silu).then_inc(s_cs, 1)
            def norm(ni):
                fn(pab[:, 3:4], eps[0:8, :], ACT.Ln)
                act.wait_ge(s_ss, ni + 1)
                fn(rstd[:, :], ps[sum_bank(ni)][:, 0:TOK], ACT.Ln, scale=1.0 / D, bias=eps[:, 0:1]).then_inc(s_ln, 1)
                act.wait_ge(s_ln, ni + 1)
                fn(rstd[:, :], rstd[:, :], ACT.Exp, scale=-0.5).then_inc(s_rstd, 1)
                if ni < 3:
                    sh = modT[:, 3 * ni * KD:(3 * ni + 1) * KD, :]
                    for c in range(KD):
                        act.wait_ge(s_xs, KD * ni + c + 1)
                        fn(hn[:, c, 0:SEQ], xs[:, c, 0:SEQ], ACT.Identity, bias=sh[:, c, 0:1]).then_inc(s_hn, 1)

            def ada_copy(j, odd):
                act.wait_ge(s_adamm, j + 1)
                if not isinstance(j, int) or j >= 2:
                    act.wait_ge(s_adaT, j - 1)
                nc.scalar.copy(adasb[:, odd, :], ps[4 + odd][:, :]).then_inc(s_adaev, 1)

            def gate_silu(l, f, odd):
                act.wait_ge(s_gate, f + (FC * l + 1))
                if l or not isinstance(f, int) or f >= 2:
                    act.wait_ge(s_hid, f + (FC * l - 1))
                fn(sgate[:, odd, :], ps[2 * odd][:, 0:TOK], ACT.Silu).then_inc(s_silu, 1)

            for j in range(ADA_FIRST):
                ada_copy(j, j % 2)
                if j == 0:
                    act.dma_start(wab[:, :, :], win[:, :, 1536:1544]).then_inc(s_wab, 16)
                    act.dma_start(ptab[:, :], a["ptab"]).then_inc(s_pt, 16)
                    act.wait_ge(s_ini, 3)
                    act.dma_start(pab[0:HG, 0:1], a["dt_bias"].rearrange("o h -> h o")).then_inc(s_pab, 16)
                    act.dma_start(pab[0:HG, 1:2], a["a_log"].rearrange("o h -> h o")).then_inc(s_pab, 16)
            norm(0)
            gate_silu(0, 0, 0)
            gate_silu(0, 1, 1)
            ada_copy(4, 0)
            ada_copy(5, 1)
            with act.Fori(0, 5) as i:
                for k in range(2):
                    gate_silu(0, i * 4 + (2 + 2 * k), 0)
                    gate_silu(0, i * 4 + (3 + 2 * k), 1)
                    ada_copy(i * 2 + (6 + k), k)
            for j in (16, 17):
                act.wait_ge(s_adamm, j + 1)
                act.wait_ge(s_adaT, j - 1)
                nc.scalar.copy(adasb[:, j % 2, :], ps[j % 2][:, :]).then_inc(s_adaev, 1)

            norm(1)

            def zqkv(q):
                act.wait_ge(s_win, win_turn(q) + 1)
                src, kind, c = ps[win_turn(q) % 8][:, 0:TOK], (q - 12) // 4, q % 4
                if kind == 0:
                    ins = fn(zs[:, c, :], src, ACT.Silu)
                elif kind == 1:
                    ins = nc.scalar.mul(mqT[:, c, :], src, HD ** -0.5)
                else:
                    ins = nc.scalar.copy((mkT, mvT)[kind - 2][:, c, :], src)
                ins.then_inc(s_zm, 1)

            def conv_silu(grp):
                for j in range(4):
                    cc = 4 * grp + j
                    act.wait_ge(s_conv, 16 * grp + 12 + j + 1)
                    fn(Cv[:, cc, 0:SEQ], Yb[:, j, 0:SEQ], ACT.Silu)
                    fn(Cv[:, cc, SEQ:TOK].rearrange("p (b t) -> p b t", b=NB),
                       Yb[:, j, 3 + SEQ:XW].rearrange("p (b s) -> p b s", b=NB)[:, :, 0:NT], ACT.Silu).then_inc(s_csil, 1)

            for q in range(12, 16):
                zqkv(q)
            conv_silu(0)
            act.wait_ge(s_win, AB_TURN + 1)
            nc.scalar.copy(abT[:, :], ps[AB_TURN % 8][0:8, 0:TOK]).then_inc(s_ab, 1)
            for q in range(16, 20):
                zqkv(q)
            conv_silu(1)
            conv_silu(2)
            act.wait_ge(s_absx, 1)
            act.wait_ge(s_pab, 32)
            act.wait_ge(s_ab, 1)
            fn(sc8[0:8, 2, :], abT[:, :], ACT.Sigmoid)
            fn(pab[:, 2:3], pab[:, 1:2], ACT.Exp)
            own(fn(sc8[0:8, 1, :], sc8[0:8, 1, :], ACT.Exp))
            fn(sc8[0:8, 1, :], sc8[0:8, 1, :], ACT.Ln, bias=1.0).then_inc(s_sp, 1)
            for q in range(20, 28):
                zqkv(q)
            for q in range(0, 6, 2):
                act.wait_ge(s_kvT, q + 1)
                n = P if q < 4 else NS
                nc.scalar.copy(ktok[0:n, q // 2, :], ps[q][0:n, :]).then_inc(s_kvt, 1)
            act.wait_ge(s_qz, 1)
            act.wait_ge(s_zm, 16)
            for c in range(4):
                for hh in range(2):
                    rows, head = slice(HD * hh, HD * hh + HD), 2 * c + hh
                    nc.scalar.copy(Qbd[rows, c, :, NT * head:NT * head + NT],
                                   mqT[rows, c, SEQ:TOK].rearrange("p (b t) -> p b t", b=NB)).then_inc(s_qbd, 1)
            act.sem_inc(s_ktA, 2)

            for m in range(4 * 2 * NBLK):
                act.wait_ge(s_kt, 2 * m + 1)
                act.wait_ge(s_qk, m + 1)
                nc.scalar.copy(ktb[:, m % 2, 0, :], ps[2 * (m % 2)][:, :]).then_inc(s_ktA, 1)
                s = m // 4
                if m % 4 < 3:
                    continue
                if 1 <= s <= HM:
                    x = s - 1
                    act.wait_ge(s_paT, x + 1)
                    if x >= 2:
                        act.wait_ge(s_pav, x - 1)
                    nc.scalar.copy(psT[:, x % 2, :], ps[6][:, 0:3 * P]).then_inc(s_pTe, 1)
                if s < HM:
                    act.wait_ge(s_nm, s + 1)
                    if s >= 2:
                        act.wait_ge(s_paT, s - 1)
                    fn(psP[:, s % 2, 0:P], psS[:, s % 2, 0:P], ACT.Exp, bias=patt[:, 2 * s:2 * s + 1],
                       accum_out=patt[:, 16 + 2 * s:17 + 2 * s])
                    fn(psP[:, s % 2, P:3 * P], psS[:, s % 2, P:3 * P], ACT.Exp, bias=patt[:, 2 * s + 1:2 * s + 2],
                       accum_out=patt[:, 17 + 2 * s:18 + 2 * s]).then_inc(s_pexp, 1)

            act.wait_ge(s_lev, 2 * NBLK + 1)
            act.wait_ge(s_own, 1)
            for hh in range(HG):
                act.dma_start(st[hh], a["state_gdn"][0, :, hh].rearrange("b k v -> k b v")).then_inc(s_st, 16)

            def probabilities(n):
                if n >= 2 * NBLK:
                    return
                g, blk = n // NBLK, n % NBLK
                act.wait_ge(s_pen, g + 1)
                if blk == 0:
                    fn(pown[:, g, :], sown[:, g, :], ACT.Exp, bias=pen[:, g, NBLK:NBLK + 1],
                       accum_out=rsum[:, g, NBLK:NBLK + 1]).then_inc(s_po, 1)
                if n >= 2:
                    act.wait_ge(s_PT, n - 1)
                fn(pex[:, n % 2, :], S[:, g, blk * BLK:(blk + 1) * BLK], ACT.Exp, bias=pen[:, g, blk:blk + 1],
                   accum_out=rsum[:, g, blk:blk + 1]).then_inc(s_pe, 1)

            act.wait_ge(s_gT, 1)
            probabilities(0)
            fn(sq8, Cv[:, 0:8, :], ACT.Square).then_inc(s_qks, 1)
            act.wait_ge(*copied(("cum",)))
            fn(ecum, cum, ACT.Exp).then_inc(s_ecum, 1)
            for j in range(3):
                act.wait_ge(*copied(("row", j)))
                pr = probs(j)
                fn(EG[:, pr[0]:pr[-1] + 1, :], gR[:, pr[0]:pr[-1] + 1, :], ACT.Exp).then_inc(s_eg, 1)
            act.wait_ge(s_df, 1)
            fn(DT, DT, ACT.Exp).then_inc(s_dt, 1)
            probabilities(1)
            act.wait_ge(*copied(("l2", 7)))
            own(fn(RS, RS, ACT.Ln))
            fn(RS, RS, ACT.Exp, scale=-0.5).then_inc(s_rse, 1)
            for n in range(2, 2 * NBLK):
                probabilities(n)
            act.wait_ge(*copied(("o1",)))
            fn(sqg[:, 0:HG, :], goT, ACT.Square).then_inc(s_go, 1)
            act.wait_ge(*copied(("rms", HG - 1)))
            own(fn(sqg[:, HG:8, :], sqg[:, HG:8, :], ACT.Ln))
            fn(sqg[:, HG:8, :], sqg[:, HG:8, :], ACT.Exp, scale=-0.5).then_inc(s_gr, 1)

            norm(2)
            for f in range(6):
                gate_silu(1, f, f % 2)
            with act.Fori(0, 2) as i:
                for k in range(8):
                    gate_silu(1, i * 8 + (6 + k), k % 2)
            norm(3)
            for q in range(0, 6, 2):
                act.wait_ge(s_yT, q + 1)
                n = P if q < 4 else NS
                nc.scalar.copy(ytok[0:n, q // 2, 0:512], ps[1 + q][0:n, :]).then_inc(s_y, 1)

        @block.vector
        def _(dve):
            v = nc.vector

            def own(ins, count=[0]):
                count[0] += 1
                ins.then_inc(s_dve, 1)
                dve.wait_ge(s_dve, count[0])

            def bt(x):
                return x.rearrange("p (b t) -> p b t", b=NB)

            dve.wait_ge(s_ini, 3)
            dve.wait_ge(s_pT0, 1)
            v.tensor_copy(cT[:, :, 0:NR], ps[4][:, 0:P].rearrange("p (k r) -> p k r", k=KD)[:, :, 0:NR]).then_inc(s_cT, 1)
            dve.wait_ge(s_pT0, 2)
            v.tensor_copy(pvec[:, :], ps[5][:, 0:153])
            own(v.tensor_copy(cst3[:, :, :], ps[6][:, 0:CC * 24].rearrange("p (c x) -> p c x", c=CC)))
            for c in range(KD):
                dve.wait_ge(s_xT, c + 1)
                v.tensor_copy(h[:, c, :], ps[c % 4][:, 0:TOK]).then_inc(s_h, 1)

            def mod_tile(j, odd, bank=None):
                dve.wait_ge(s_adaT, j + 1)
                part = ps[6 + odd if bank is None else bank][:, :].rearrange("p (c g r) -> p c r g", c=4, g=4)[:, :, 0:NR, :]
                at = bass.ds(j * 4, 4)
                v.tensor_reduce(modT[:, at, :], part, AX_X, ALU.add).then_inc(s_modr, 1)
                dve.wait_ge(s_modr, j + 1)
                v.tensor_tensor(modT[:, at, :], modT[:, at, :], bw[:, at].unsqueeze(2).to_broadcast([P, 4, NR]),
                                ALU.add).then_inc(s_mod, 1)

            def norm(ni):
                if ni < 3:
                    dve.wait_ge(s_mod, ADA_FIRST if ni == 0 else ADA_TILES)
                    sh = modT[:, 3 * ni * KD:(3 * ni + 1) * KD, :]
                    own(v.scalar_tensor_tensor(coef[:, :, :], modT[:, (3 * ni + 1) * KD:(3 * ni + 2) * KD, :], 1.0,
                                           nw[:, KD * ni:KD * ni + KD].unsqueeze(2).to_broadcast([P, KD, NR]), ALU.add, ALU.mult))
                dve.wait_ge(s_rstd, ni + 1)
                if ni == 3:
                    for c in range(KD):
                        v.scalar_tensor_tensor(hn[:, c, :], h[:, c, :], nw[:, 24 + c:25 + c], rstd[:, :], ALU.mult, ALU.mult).then_inc(s_hn, 1)
                    return

                def smp4(x):
                    return x[:, :, SEQ:TOK].rearrange("p c (b t) -> p c b t", b=NB)

                def spread(x):
                    return x[:, :, 1:NR].unsqueeze(3).to_broadcast([P, KD, NB, NT])

                for c in range(KD):
                    v.scalar_tensor_tensor(xs[:, c, 0:SEQ], h[:, c, 0:SEQ], coef[:, c, 0:1], rstd[:, 0:SEQ], ALU.mult, ALU.mult).then_inc(s_xs, 1)
                    if c:
                        continue
                    own(v.tensor_tensor(xs[:, :, SEQ:TOK], h[:, :, SEQ:TOK], rstd[:, SEQ:TOK].unsqueeze(1).to_broadcast([P, KD, NS]), ALU.mult))
                    own(v.tensor_tensor(smp4(hn), smp4(xs), spread(coef), ALU.mult))
                    v.tensor_tensor(smp4(hn), smp4(hn), spread(sh), ALU.add).then_inc(s_hs, 1)

            def hidden(l, f, odd):
                dve.wait_ge(s_silu, f + (FC * l + 1))
                dve.wait_ge(s_up, f + (FC * l + 1))
                at = bass.ds(f, 1)
                v.tensor_tensor(hid[:, at, :].rearrange("p o n -> p (o n)"), sgate[:, odd, :], ps[2 * odd + 1][:, 0:TOK],
                                ALU.mult).then_inc(s_hid, 1)

            def residual(si):
                mod = modT[:, (3 * si + 2) * KD:(3 * si + 3) * KD, :]
                gt = mod
                if si != 1:
                    own(v.tensor_scalar(gate[:, :, :], mod, 0.5, None, ALU.mult))
                    gt = gate
                for m in range(KD):
                    dve.wait_ge(s_sub, KD * si + m + 1)
                    b = ps[4 + m] if m < 4 else ps[m - 4]
                    own(v.tensor_tensor(samp[:, m % 2], bt(b[:, SEQ:TOK]), gt[:, m, 1:NR].unsqueeze(2).to_broadcast([P, NB, NT]), ALU.mult))
                    v.scalar_tensor_tensor(h[:, m, 0:SEQ], b[:, 0:SEQ], gt[:, m, 0:1], h[:, m, 0:SEQ], ALU.mult, ALU.add)
                    v.tensor_tensor(bt(h[:, m, SEQ:TOK]), bt(h[:, m, SEQ:TOK]), samp[:, m % 2], ALU.add).then_inc(s_h, 1)

            for j in range(ADA_FIRST):
                mod_tile(j, j % 2)
            norm(0)
            hidden(0, 0, 0)
            hidden(0, 1, 1)
            mod_tile(4, 0)
            with dve.Fori(0, 5) as i:
                for k in range(2):
                    hidden(0, i * 4 + (2 + 2 * k), 0)
                    hidden(0, i * 4 + (3 + 2 * k), 1)
                    mod_tile(i * 2 + (5 + k), 1 - k)
            mod_tile(15, 1)
            mod_tile(16, 0, bank=2)
            mod_tile(17, 1, bank=3)
            dve.wait_ge(s_mod, ADA_TILES)
            residual(0)

            norm(1)
            v.memset(XC[:, :, 0:3], 0.0)
            v.tensor_copy(XCs[:, :, :, 0:3], cst3[:, :, :].rearrange("p c (b i) -> p c b i", b=NB))
            for q in range(CC):
                dve.wait_ge(s_win, q + 1)
                v.tensor_copy(XC[:, q, 3:3 + SEQ], ps[q % 8][:, 0:SEQ])
                v.tensor_copy(XCs[:, q, :, 3:7], bt(ps[q % 8][:, SEQ:TOK])).then_inc(s_xc, 1)
            for grp in range(3):
                dve.wait_ge(s_xc, 4 * grp + 4)
                for tap in range(CONV):
                    for j in range(4):
                        cc, op = 4 * grp + j, 16 * grp + 4 * tap + j
                        src, w = XC[:, cc, tap:tap + YW], cw[:, CC * tap + cc:CC * tap + cc + 1]
                        if tap == 0:
                            if grp:
                                dve.wait_ge(s_csil, cc - 3)
                            ins = v.tensor_scalar(Yb[:, j, 0:YW], src, w, None, ALU.mult)
                        else:
                            dve.wait_ge(s_conv, op - 3)
                            ins = v.scalar_tensor_tensor(Yb[:, j, 0:YW], src, w, Yb[:, j, 0:YW], ALU.mult, ALU.add)
                        ins.then_inc(s_conv, 1)
            dve.wait_ge(s_cst2, 16)
            dve.wait_ge(s_ab, 1)
            dve.wait_ge(s_pab, 32)
            own(v.tensor_scalar(sc8[0:8, 0, :], abT[:, :], pab[:, 0:1], None, ALU.add))
            v.scalar_tensor_tensor(sc8[0:8, 1, :], sc8[0:8, 0, :], -1.0, sc8[0:8, 0, :], ALU.mult, ALU.min).then_inc(s_absx, 1)

            dve.wait_ge(s_sp, 1)
            own(v.scalar_tensor_tensor(sc8[0:8, 0, :], sc8[0:8, 0, :], 0.0, sc8[0:8, 1, :], ALU.max, ALU.add))
            own(v.tensor_scalar(sc8[0:8, 0, :], sc8[0:8, 0, :], pab[:, 2:3], -1.0, ALU.mult, ALU.mult))
            for i in range(2):
                ins = v.tensor_tensor(gE[0:8, i, :].rearrange("p (h n) -> p h n", h=HG),
                                      sc8[0:8, 2 * i, SEQ:TOK].unsqueeze(1).to_broadcast([8, HG, NS]),
                                      cst("mh8")[0:8, :].rearrange("p (h n) -> p h n", h=HG), ALU.mult)
            ins.then_inc(s_g8, 1)
            dve.wait_ge(s_win, 29)
            v.tensor_copy(cgat[:, :, 0:3], XC[:, :, SEQ:SEQ + 3])
            v.tensor_copy(cgat[:, :, 3:27].rearrange("p c (b i) -> p c b i", b=NB), XCs[:, :, :, 4:7]).then_inc(s_cg, 1)

            dve.wait_ge(s_gT, 1)
            own(v.tensor_copy(GB, ps[7][:, 0:48].rearrange("p (a b) -> p a b", a=6)))
            for dst, i, r in ((G9, 0, 0), (B9, 3, 4)):
                v.tensor_copy(dst[:, 0:4], GB[:, i, r:r + 4])
                v.tensor_copy(dst[:, 4:8], GB[:, i + 1, r:r + 4])
                ins = v.tensor_reduce(dst[:, 8:9], GB[:, i + 2, r:r + 4], AX_X, ALU.add)
            ins.then_inc(s_gbc, 1)
            for q in range(1, 6, 2):
                dve.wait_ge(s_kvT, q + 1)
                n = P if q < 4 else NS
                if q == 5:
                    v.tensor_copy(vown[:, :], ps[q][0:n, :])
                v.tensor_copy(vtok[0:n, q // 2, :], ps[q][0:n, :]).then_inc(s_kvd, 1)
            for r in range(3):
                dve.wait_ge(s_cvT, r + 1)
                v.tensor_copy(cout[0:27, 512 * r:512 * r + 512], ps[(6, 7, 0)[r]][0:27, :]).then_inc(s_cvo, 1)

            v.sem_inc(s_ktD, 2)
            v.sem_inc(s_lev, 1)

            def normalise(s):
                if 1 <= s <= HM:
                    x = s - 1
                    dve.wait_ge(s_pexp, x + 1)
                    sums = patt[:, 16 + 2 * x:18 + 2 * x]
                    own(v.reciprocal(sums, sums))
                    v.tensor_scalar(psP[:, x % 2, 0:P], psP[:, x % 2, 0:P], sums[:, 0:1], None, ALU.mult)
                    v.tensor_scalar(psP[:, x % 2, P:3 * P], psP[:, x % 2, P:3 * P], sums[:, 1:2], None, ALU.mult).then_inc(s_pn, 1)

            def biased(s):
                if s < HM:
                    dve.wait_ge(s_sc, s + 1)
                    if s >= 2:
                        dve.wait_ge(s_pexp, s - 1)
                    v.scalar_tensor_tensor(psS[:, s % 2, :], cst("dist"), 2.0 ** -(s + 1), ps[5][:, 0:3 * P],
                                           ALU.mult, ALU.add).then_inc(s_paS, 1)
                    dve.wait_ge(s_paS, s + 1)
                    v.tensor_reduce(patt[:, 2 * s:2 * s + 1], psS[:, s % 2, 0:P], AX_X, ALU.max, negate=True)
                    v.tensor_reduce(patt[:, 2 * s + 1:2 * s + 2], psS[:, s % 2, P:3 * P], AX_X, ALU.max, negate=True).then_inc(s_nm, 1)
                if 2 < s < HM + 2 and s % 2:
                    c = (s - 2) // 2
                    dve.wait_ge(s_pav, 2 * c + 2)
                    v.tensor_copy(mix[:, 4 + c, 0:SEQ], ps[7][:, 0:SEQ]).then_inc(s_pao, 1)

            def block_logits(n):
                g, blk = n // NBLK, n % NBLK
                dve.wait_ge(s_qk, 4 * n + 6)
                b = ps[4][:, 0:BLK]
                at, one = slice(blk * BLK, (blk + 1) * BLK), slice(blk, blk + 1)
                v.tensor_reduce(gts[:, g, one], b, AX_X, ALU.add)
                v.tensor_tensor(S[:, g, at], b, cst("biasS")[:, at], ALU.add).then_inc(s_lev, 1)
                dve.wait_ge(s_lev, n + 2)
                v.tensor_reduce(bmx[:, g, one], S[:, g, at], AX_X, ALU.max).then_inc(s_bmx, 1)

            def selection(g):
                dve.wait_ge(s_bmx, NBLK * (g + 1))
                other = gts[:, g, :].unsqueeze(1).to_broadcast([P, NBLK, NBLK])
                mine = gts[:, g, :].unsqueeze(2).to_broadcast([P, NBLK, NBLK])
                A8 = cmpA.rearrange("p (n m) -> p n m", n=NBLK)
                B8 = cmpB.rearrange("p (n m) -> p n m", n=NBLK)
                v.tensor_tensor(A8, other, mine, ALU.is_gt)
                own(v.tensor_tensor(B8, other, mine, ALU.is_equal))
                own(v.tensor_tensor(cmpB, cmpB, cst("lower8"), ALU.mult))
                own(v.tensor_tensor(cmpA, cmpA, cmpB, ALU.add))
                own(v.tensor_reduce(cnt, A8, AX_X, ALU.add))
                own(v.tensor_scalar(pen[:, g, 0:NBLK], cnt, TOPK - 0.5, NEG, ALU.is_ge, ALU.mult))
                v.tensor_tensor(bmx[:, g, 0:NBLK], bmx[:, g, 0:NBLK], pen[:, g, 0:NBLK], ALU.add)
                dve.wait_ge(s_owns, 1)
                own(v.tensor_reduce(bmx[:, g, NBLK:NBLK + 1], sown[:, g, :], AX_X, ALU.max))
                own(v.tensor_reduce(negm[:, g:g + 1], bmx[:, g, :], AX_X, ALU.max, negate=True))
                v.tensor_copy(pen[:, g, NBLK:NBLK + 1], negm[:, g:g + 1])
                v.tensor_scalar(pen[:, g, 0:NBLK], pen[:, g, 0:NBLK], negm[:, g:g + 1], None, ALU.add).then_inc(s_pen, 1)

            dve.wait_ge(s_csil, CC)
            dve.wait_ge(s_own, 1)
            v.tensor_tensor(sown.rearrange("p g n -> p (g n)"), ps[6][:, 384:448], cst("biasO"), ALU.add).then_inc(s_owns, 1)
            for m in range(4 * 2 * NBLK):
                dve.wait_ge(s_kt, 2 * m + 2)
                dve.wait_ge(s_qk, m + 1)
                v.tensor_copy(ktb[:, m % 2, 1, :], ps[2 * (m % 2) + 1][:, :]).then_inc(s_ktD, 1)
                n = m // 4
                if m % 4 == 0 and n:
                    block_logits(n - 1)
                    if n == NBLK:
                        selection(0)
                elif m % 4 == 1:
                    normalise(n)
                elif m % 4 == 2:
                    biased(n)
                elif n == 2 * NBLK - 1:
                    v.tensor_copy(Pv, G9.unsqueeze(2).to_broadcast([P, NPROB, P])).then_inc(s_gbc, 1)
            block_logits(2 * NBLK - 1)

            def scaled(g):
                own(v.tensor_reduce(rin[:, 2 * g:2 * g + 1], rsum[:, g, :], AX_X, ALU.add))
                own(v.reciprocal(rin[:, 2 * g + 1:2 * g + 2], rin[:, 2 * g:2 * g + 1]))
                dve.wait_ge(s_O, g + 1)
                v.scalar_tensor_tensor(Om, ps[7][:, :], rin[:, 2 * g + 1:2 * g + 2], cst("hmask"), ALU.mult, ALU.mult).then_inc(s_om, 1)

            def into_mix(g):
                dve.wait_ge(s_AT, g + 1)
                v.tensor_copy(mix[:, 4:8, SEQ + 16 * g:SEQ + 16 * g + 16],
                              ps[6][:, 64 * g:64 * g + 64].rearrange("p (c n) -> p c n", c=4)).then_inc(s_mixa, 1)

            def values(n):
                if n == NBLK + 1:
                    scaled(0)
                if n == NBLK + 2:
                    into_mix(0)
                if n == 2 * NBLK:
                    scaled(1)
                    return
                g, blk = n // NBLK, n % NBLK
                if blk == 0:
                    dve.wait_ge(s_oT, g + 1)
                    v.tensor_copy(ownT[0:32, g, :], ps[6][0:32, BLK + P * g:BLK + P * g + P]).then_inc(s_oTs, 1)
                dve.wait_ge(s_PT, n + 1)
                if n >= 2:
                    dve.wait_ge(s_PV, 2 * n - 2)
                v.tensor_copy(pT[:, n % 2].rearrange("p a b -> p (a b)"), ps[5][:, 0:BLK]).then_inc(s_pTs, 1)

            def filled(step):
                k = STEPS[step]
                dve.wait_ge(s_gp, k + 1)
                return ps[k % GBANKS]

            def grp3(b, g):
                n = len(probs(g))
                return b[:, 0:n * P].rearrange("p (a b) -> p a b", a=n)

            def sel(x, g):
                return x[:, probs(g)[0]:probs(g)[-1] + 1]

            v.tensor_copy(cum, filled(("cum",))[:, 0:18]).then_inc(s_ge, 1)
            dve.wait_ge(s_okv, 96)
            for g in range(3):
                v.tensor_copy(sel(gR, g), grp3(filled(("row", g)), g)).then_inc(s_ge, 1)
            dve.wait_ge(*copied(("row", 2)))
            for p in range(NPROB):
                ins = v.tensor_scalar(DT[:, p, :], gR[:, p, :], cum[:, p:p + 1], 0.0, ALU.subtract, ALU.min)
            ins.then_inc(s_df, 1)
            dve.wait_ge(s_ecum, 1)
            v.tensor_tensor(bek, B9, ecum[:, 0:NPROB], ALU.mult)
            values(0)
            for c in range(8):
                v.tensor_scalar(RS[:, c, :], filled(("l2", c))[:, 0:TOK], EPS, None, ALU.add).then_inc(s_ge, 1)
            values(1)
            dve.wait_ge(s_dt, 1)
            v.tensor_tensor(DT[:, 0:8, :], DT[:, 0:8, :], tri.unsqueeze(1).to_broadcast([P, 8, P]), ALU.mult)
            v.tensor_tensor(DT[:, 8, :], DT[:, 8, :], triS, ALU.mult)
            dve.wait_ge(s_rse, 1)
            v.scalar_tensor_tensor(QK[:, 0:4, :], Cv[:, 0:4, :], P ** -0.5, RS[:, 0:4, :], ALU.mult, ALU.mult)
            own(v.tensor_tensor(QK[:, 4:8, :], Cv[:, 4:8, :], RS[:, 4:8, :], ALU.mult))
            for i, src in enumerate((QK[:, 0:4], QK[:, 4:8], Cv[:, 8:12])):
                ins = v.tensor_copy(smp[:, i, :].rearrange("p (h n) -> p h n", h=HG), src[:, :, SEQ:TOK])
            ins.then_inc(s_qkn, 1)
            dve.wait_ge(s_qkn, 1)
            for j in range(3):
                b = filled(("kt", j))
                for x, p in enumerate(probs(j)):
                    v.tensor_scalar(KB[:, p, :], b[:, x * P:(x + 1) * P], bek[:, p:p + 1], None, ALU.mult)
                    ins = v.tensor_scalar(KDc[:, p, :], b[:, x * P:(x + 1) * P], ecum[:, 9 + p:10 + p], None, ALU.mult)
                ins.then_inc(s_ge, 1)
            for j in range(3):
                v.tensor_tensor(sel(VB, j), grp3(filled(("vt", j)), j), sel(B9, j).unsqueeze(2).to_broadcast([P, len(probs(j)), P]),
                                ALU.mult).then_inc(s_ge, 1)
            values(2)
            for j in range(5):
                n = min(2, NPROB - 2 * j)
                b = filled(("gram", j))[:, 0:2 * P * n].rearrange("p (x i t) -> p x i t", x=n, i=2)
                v.tensor_tensor(AN[:, 2 * j:2 * j + n], b, DT[:, 2 * j:2 * j + n, :].unsqueeze(2).to_broadcast([P, n, 2, P]),
                                ALU.mult).then_inc(s_ge, 1)
            dve.wait_ge(*copied(("gram", 4)))

            def level_mask(l):
                for g in range(3 if l < 2 else 2):
                    n = len(probs(g))
                    v.tensor_tensor(sel(NTl, g), sel(AN, g)[:, :, 1, :], lev[:, l, :].unsqueeze(1).to_broadcast([P, n, P]),
                                    ALU.mult).then_inc(s_ntl, 1)

            level_mask(0)
            values(3)
            selection(1)
            v.tensor_tensor(QD[:, 4:8, :], QK[:, 0:4, P:SEQ], EG[:, 4:8, :], ALU.mult)
            v.tensor_tensor(WQ[:, :, 4:8], smp[:, 0, :].rearrange("p (x t) -> p x t", t=NT),
                            EG[:, 8, :].rearrange("p (x t) -> p x t", t=NT), ALU.mult)

            def sample(l):
                if l == 1:
                    v.tensor_copy(WQ[:, :, 0:4], filled(("W", 2))[:, 0:P].rearrange("p (x t) -> p x t", t=NT)).then_inc(s_ge, 1)
                elif l == 2:
                    v.tensor_copy(VX[:, 0, :], filled(("us",))[:, 0:P]).then_inc(s_ge, 1)
                    b = filled(("ws",))[:, 0:8 * HG * NB].rearrange("p (x t) -> p x t", t=8)
                    dve.wait_ge(*copied(("us",)))
                    vx0 = VX[:, 0, :].rearrange("p (x t) -> p x t", t=NT)
                    v.tensor_copy(VX[:, 1, :].rearrange("p (x t) -> p x t", t=NT), b[:, :, 4:8])
                    v.tensor_tensor(vx0, vx0, b[:, :, 0:4], ALU.subtract).then_inc(s_ge, 1)
                elif l == 3:
                    v.tensor_copy(VN[:, 8, :], filled(("vs",))[:, 0:P]).then_inc(s_ge, 1)
                    heads = "p (h n) -> p h n"
                    v.tensor_tensor(goT[:, :, SEQ:TOK], VX[:, 1, :].rearrange(heads, h=HG), filled(("os",))[:, 0:P].rearrange(heads, h=HG),
                                    ALU.add).then_inc(s_ge, 1)
                    dve.wait_ge(*copied(("os",)))
                    v.tensor_tensor(VX[:, 0:NB, :], VN[:, 8, :].unsqueeze(1).to_broadcast([P, NB, P]),
                                    cst("bdm").unsqueeze(2).to_broadcast([P, NB, P]), ALU.mult).then_inc(s_vx, 1)
                elif l in (4, 5):
                    for k in range(4 * l - 16, 4 * l - 12):
                        b = filled(("up", k))
                        for x in range(4):
                            hh, s = k // 2, 4 * (k % 2) + x
                            last = NT * (NB * hh + s) + NT - 1
                            ins = v.scalar_tensor_tensor(st[hh][:, s, :], st[hh][:, s, :], EG[:, 8, last:last + 1], b[:, x * P:(x + 1) * P],
                                                         ALU.mult, ALU.add)
                        ins.then_inc(s_ge, 1)

            for l in range(7):
                groups = range(3 if l < 2 else 2)
                for g in groups:
                    v.tensor_tensor(sel(Pv, g), grp3(filled(("P", l, g)), g),
                                    sel(B9, g).unsqueeze(2).to_broadcast([P, len(probs(g)), P]), ALU.mult).then_inc(s_ge, 1)
                if l < 6:
                    level_mask(l + 1)
                values(4 + 2 * l)
                for g in groups:
                    if l == 0:
                        idb = ident.unsqueeze(1).to_broadcast([P, len(probs(g)), P])
                        dve.wait_ge(*copied(("P", 0, g)))
                        v.tensor_tensor(sel(X, g), idb, sel(Pv, g), ALU.subtract)
                        v.tensor_tensor(sel(XT, g), idb, grp3(filled(("PX", 0, g)), g), ALU.subtract).then_inc(s_ge, 1)
                        continue
                    if l < 6:
                        v.tensor_tensor(sel(X, g), sel(X, g), grp3(filled(("XP", l, g)), g), ALU.subtract).then_inc(s_ge, 1)
                    v.tensor_tensor(sel(XT, g), sel(XT, g), grp3(filled(("PX", l, g)), g), ALU.subtract).then_inc(s_ge, 1)
                if l < 6:
                    values(5 + 2 * l)
                sample(l)
            v.tensor_scalar(WT[:, 4:8, :], grp3(filled(("W", 1)), 1), -1.0, None, ALU.mult).then_inc(s_ge, 1)
            v.tensor_copy(VN[:, 0:4, :], grp3(filled(("U0",)), 0)).then_inc(s_ge, 1)
            v.tensor_copy(S1, grp3(filled(("S1",)), 0)).then_inc(s_ge, 1)
            v.tensor_copy(VN[:, 4:8, :], grp3(filled(("V1",)), 0)).then_inc(s_ge, 1)
            v.tensor_copy(goT[:, :, 0:P], grp3(filled(("o0",)), 0)).then_inc(s_ge, 1)
            v.tensor_copy(goT[:, :, P:SEQ], grp3(filled(("o1",)), 0)).then_inc(s_ge, 1)
            b = filled(("S2",))
            for x in range(HG):
                ins = v.scalar_tensor_tensor(S1[:, x, :], S1[:, x, :], EG[:, 4 + x, P - 1:P], b[:, x * P:(x + 1) * P],
                                             ALU.mult, ALU.add)
            ins.then_inc(s_ge, 1)
            into_mix(1)
            for hh in range(HG):
                v.tensor_scalar(sqg[:, HG + hh, :], filled(("rms", hh))[:, 0:TOK], 1.0 / P, EPS, ALU.mult, ALU.add).then_inc(s_ge, 1)
            dve.wait_ge(s_gr, 1)
            own(v.scalar_tensor_tensor(goT, goT, gnw, sqg[:, HG:8, :], ALU.mult, ALU.mult))
            v.tensor_tensor(mix[:, 0:HG, :], goT, zs, ALU.mult).then_inc(s_gdn, 1)

            residual(1)

            norm(2)
            for f in range(6):
                hidden(1, f, f % 2)
            with dve.Fori(0, 2) as i:
                for k in range(8):
                    hidden(1, i * 8 + (6 + k), k % 2)
            residual(2)
            norm(3)
            for q in range(1, 6, 2):
                dve.wait_ge(s_yT, q + 1)
                n = P if q < 4 else NS
                v.tensor_copy(ytok[0:n, q // 2, 512:D], ps[1 + q][0:n, :]).then_inc(s_y, 1)


OUT_SHAPES = [("y_prompt", (1, SEQ, D)), ("y_sample", (NB, NT, D)), ("k_prompt", (1, 1, SEQ, HM, HD)), ("v_prompt", (1, 1, SEQ, HM, HD)),
              ("gdn_prompt", (1, 1, HG, P, P)), ("conv_prompt", (1, 1, 3, CC * P)), ("k_sample", (1, NB, NT, HM, HD)),
              ("v_sample", (1, NB, NT, HM, HD)), ("gdn_sample", (1, NB, HG, P, P)), ("conv_sample", (1, NB, 3, CC * P))]


def kernel(**inputs):
    import concourse.bacc as bacc
    from concourse.bass_utils import run_bass_kernel_spmd

    nc = bacc.Bacc("TRN2", target_bir_lowering=False, num_devices=1)
    arrays = {n: np.ascontiguousarray(x) for n, x in inputs.items() if n != "page_table"}
    table = np.asarray(inputs["page_table"]).reshape(2, NB // 2, NBLK, 2).transpose(0, 2, 1, 3)
    arrays["ptab"] = np.ascontiguousarray(table.reshape(1, 2 * PHASE))
    arrays["consts"] = make_consts()
    a = {n: nc.dram_tensor("in_" + n, x.shape, I32 if n == "ptab" else F32, kind="ExternalInput").ap() for n, x in arrays.items()}
    o = {n: nc.dram_tensor("out_" + n, shape, F32, kind="ExternalOutput").ap() for n, shape in OUT_SHAPES}
    build_program(nc, a, o)
    r = run_bass_kernel_spmd(nc, [{"in_" + n: x for n, x in arrays.items()}], core_ids=[0])
    return tuple(r.results[0]["out_" + n] for n, _ in OUT_SHAPES)
```

```python
from contextlib import ExitStack

import numpy as np

import concourse.bass as bass
from concourse import mybir

F32 = mybir.dt.float32
F32R = mybir.dt.float32r
I32 = mybir.dt.int32
ALU = mybir.AluOpType
ACT = mybir.ActivationFunctionType
AX_X = mybir.AxisListType.X

P = 128
D = 1024
KD = D // P
SEQ = 256
NB = 8
NT = 4
NS = NB * NT
TOK = SEQ + NS
F = 2816
FC = F // P
NMOD = 9
NR = 1 + NB
HG = 4
HM = 8
HD = 64
CONV = 4
CC = 12
XW = 3 + SEQ + NB * 7
YW = XW - 3
NPROB = 9
PAGE = 128
NPAGE = 16
NPHYS = 160
PAST = 2048
BLK = 256
NBLK = PAST // BLK
TOPK = 3
EPS = 1e-6
NEG = -1e30
RING = 4
KVR = 8
KU = 12
PHASE = NB * NBLK

UP_TILES = FC // 2
ADA_FIRST = 4
ADA_TILES = NMOD * D // 512


def const_layout():
    names = [("ident", P), ("ones", P), ("tri", P), ("later", P), ("triS", P), ("laterS", P),
             ("lev", 7 * P), ("mh8", P), ("lower8", 64), ("biasS", PAST), ("biasO", 64),
             ("dist", 3 * P), ("hmask", 512), ("selbt", 16), ("bdm", NB)]
    at, out = 0, {}
    for n, w in names:
        out[n] = (at, at + w)
        at += w
    return out, at


def make_consts():
    lay, width = const_layout()
    c = np.zeros((P, width), np.float32)
    i = np.arange(P)

    def put(name, value):
        a, b = lay[name]
        c[:, a:b] = value

    put("ident", np.eye(P))
    put("ones", 1.0)
    put("tri", i[:, None] <= i[None, :])
    put("later", i[:, None] > i[None, :])
    same = i[:, None] // NT == i[None, :] // NT
    put("triS", same & (i[:, None] <= i[None, :]))
    put("laterS", same & (i[:, None] > i[None, :]))
    lev = np.zeros((P, 7, P))
    for l in range(7):
        s, t = i[:, None], i[None, :]
        lev[:, l, :] = (s >> (l + 1) == t >> (l + 1)) & ((s >> l) % 2 == 0) & ((t >> l) % 2 == 1)
    put("lev", lev.reshape(P, -1))
    put("mh8", (i[:, None] % 4 == i[None, :] // NS) & (i[:, None] < 8))
    n, m = np.arange(64) // 8, np.arange(64) % 8
    put("lower8", np.broadcast_to(m < n, (P, 64)))
    h, t = (i % 32) // NT, i % NT
    slope = 2.0 ** -(h + 1.0)
    put("biasS", slope[:, None] * (np.arange(PAST)[None, :] - PAST - t[:, None]))
    own = np.zeros((P, 2, 32))
    for g in range(2):
        j = np.arange(32)
        ok = (j[None, :] // NT == 4 * g + i[:, None] // 32) & (j[None, :] % NT <= t[:, None])
        own[:, g, :] = np.where(ok, slope[:, None] * (j[None, :] % NT - t[:, None]), NEG)
    put("biasO", own.reshape(P, -1))
    d0 = np.where(i[None, :] <= i[:, None], i[None, :] - i[:, None], NEG)
    k = np.arange(SEQ)
    d1 = np.where(k[None, :] <= P + i[:, None], k[None, :] - P - i[:, None], NEG)
    put("dist", np.concatenate([d0, d1], 1))
    put("hmask", h[:, None] == np.arange(512)[None, :] // HD)
    put("selbt", (i[:, None] // 32) * NT + t[:, None] == np.arange(16)[None, :])
    put("bdm", ((i % NS) // NT)[:, None] == np.arange(NB)[None, :])
    return c


def build_program(nc, a, o):
    lay, cwidth = const_layout()
    with ExitStack() as ctx:
        def sb(name, shape, dt=F32):
            return ctx.enter_context(nc.sbuf_tensor(name, shape, dt))

        def sem(name):
            return ctx.enter_context(nc.semaphore(name))

        ps = [ctx.enter_context(nc.psum_tensor(f"bank{i}", [P, 512], F32)) for i in range(8)]

        sizes = [("wring", RING * 4096), ("kv", KVR * 1024), ("hn", KD * TOK), ("xs", KD * TOK), ("region", 12864)]
        plain, rounded = [], []
        for made, dt, suffix in ((plain, F32, ""), (rounded, F32R, "_rounded")):
            with ExitStack() as overlay:
                for name, n in sizes:
                    made.append(overlay.enter_context(nc.sbuf_tensor(name + suffix, [P, n], dt)))
        for name, n in sizes:
            sb(name + "_space", [P, n])
        wflat, kvf, hnf, xsf, region = plain
        wflatR, kvfR, hnfR, xsfR, regionR = rounded
        const = sb("const", [P, cwidth])

        def cst(name):
            return const[:, lay[name][0]:lay[name][1]]

        def shaped(v, *shape):
            n = int(np.prod(shape))
            v = v[:, 0:n]
            if len(shape) == 2:
                v = v.rearrange("p (a b) -> p a b", a=shape[0])
            if len(shape) == 3:
                v = v.rearrange("p (a b c) -> p a b c", a=shape[0], b=shape[1])
            return v

        def carver(flat):
            at = [0]

            def take(*shape):
                n = int(np.prod(shape))
                assert at[0] + n <= flat.shape[1], (at, n)
                v = shaped(flat[:, at[0]:at[0] + n], *shape)
                at[0] += n
                return v
            return take

        wring = wflat[:, :].rearrange("p (s k n) -> p s k n", s=RING, k=8)
        kv = shaped(kvf, KVR, 2, 512)
        h = sb("h", [P, KD, TOK])
        hn = shaped(hnf, KD, TOK)
        mix = hn
        xs = shaped(xsf, KD, TOK)
        rstd = sb("rstd", [P, TOK])
        modT = sb("modT", [P, NMOD * KD, NR])
        coef = sb("coef", [P, KD, NR])
        gate = sb("gate", [P, KD, NR])
        samp = sb("samp", [P, 2, NB, NT])
        pvec = sb("pvec", [P, 153])
        eps = sb("eps", [P, 1])
        cT = sb("cT", [P, KD, 32])
        adaf = sb("adasb", [P, 1024])
        adasb = shaped(adaf, 2, 512)
        sgf = sb("sgate", [P, 2 * TOK])
        sgate = shaped(sgf, 2, TOK)
        ytok = shaped(region, 3, D)
        hidR = shaped(regionR, 2 * FC, TOK)
        hnR, xsR = shaped(hnfR, KD, TOK), shaped(xsfR, KD, TOK)
        wringR = wflatR[:, :].rearrange("p (s k n) -> p s k n", s=RING, k=8)
        whiR = shaped(kvfR, 2, 8, 512)
        tail = region[:, 11952:12864]
        vown = tail[0:NS, 0:512]
        ptab = sb("ptab", [1, 2 * PHASE], I32)

        pro = carver(region)
        xin = pro(3, D)
        cin = pro(D)
        csil = pro(D)
        prow = pro(P)
        crow = pro(P)
        srow = pro(CC * P)

        reg = carver(region)
        XC = reg(CC, XW)
        Yb = reg(4, XW)
        Cv = reg(CC, TOK)
        mqT = reg(4, TOK)
        mkT = reg(4, TOK)
        mvT = reg(4, TOK)
        cst3 = sb("cst3", [P, CC, 24])
        z4 = carver(xsf)
        zs = z4(HG, TOK)
        goT = z4(HG, TOK)
        pa = carver(wflat)
        ktok = pa(3, 512)
        vtok = pa(3, 512)
        psS = pa(2, 384)
        psP = pa(2, 384)
        psT = pa(2, 384)
        cgat = pa(CC, 27)
        cout = pa(CC * P)
        patt = pa(32)
        sc8 = shaped(tail, 3, TOK)
        gE = shaped(sgf, 2, P)
        mq_at = CC * XW + 4 * XW + CC * TOK
        gd = carver(wflat)
        gR = gd(NPROB, P)
        EG = gd(NPROB, P)
        DT = gd(NPROB, P)
        QK = gd(8, TOK)
        AN = gd(NPROB, 2, P)
        KB = gd(NPROB, P)
        KDc = gd(NPROB, P)
        VB = gd(NPROB, P)
        X = gd(NPROB, P)
        XT = gd(NPROB, P)
        Pv = gd(NPROB, P)
        S1 = gd(HG, P)
        smp = gd(3, P)
        RS = shaped(region[:, mq_at:mq_at + 8 * TOK], 8, TOK)
        VN, WT, NTl = X, Pv, gR
        QKf = QK.rearrange("p a b -> p (a b)")
        VX = shaped(QKf, NB, P)
        WX = [shaped(QKf[:, 1152 * i:1152 * i + 1152], HG, 36 * NB) for i in range(2)]
        WXd = [w.rearrange("p h (b x) -> p h b x", x=36)[:, :, :, 0:NT] for w in WX]
        QD = shaped(DT.rearrange("p a b -> p (a b)"), NPROB, P)
        sqg = shaped(QK.rearrange("p a b -> p (a b)"), 8, TOK)
        dead = const[:, lay["biasS"][0]:lay["biasS"][1]]
        st = [shaped(region[:, mq_at + NB * P * x:mq_at + NB * P * (x + 1)], NB, P) for x in range(3)]
        st.append(shaped(dead[:, NB * P:2 * NB * P], NB, P))
        gsm = carver(tail[:, 512:912])
        abT = sb("abT", [8, TOK])
        wab = sb("wab", [P, KD, 8])
        pab = sb("pab", [8, 4])
        GB = gsm(6, 8)
        G9 = gsm(NPROB)
        B9 = gsm(NPROB)
        cum = gsm(18)
        ecum = gsm(18)
        bek = gsm(NPROB)
        at_ = carver(region)
        S = at_(2, PAST)
        ktb = shaped(wflat[:, 8964:8964 + 2048], 2, 2, 512)
        extra = wring[:, 3]
        pT = shaped(dead[:, 0:512], 2, 2, P)
        Om = dead[:, 512:1024]
        pex = shaped(sgf, 2, BLK)
        Qbd = shaped(adaf, 4, NB, 32)
        gts = at_(2, NBLK)
        bmx = at_(2, NBLK + 1)
        pen = at_(2, NBLK + 1)
        cmpA = at_(64)
        cmpB = at_(64)
        cnt = at_(NBLK)
        negm = at_(2)
        sown = at_(2, 32)
        pown = at_(2, 32)
        rsum = at_(2, NBLK + 1)
        rin = at_(8)
        ownT = at_(2, P)

        ident, ones, tri, later = cst("ident"), cst("ones"), cst("tri"), cst("later")
        triS, laterS = cst("triS"), cst("laterS")
        lev = shaped(cst("lev"), 7, P)
        bw = pvec[:, 0:NMOD * KD]
        nw = pvec[:, 72:104]
        gnw = pvec[:, 104:105]
        cw = pvec[:, 105:153]

        s_cst = sem("s_first_consts_landed")
        s_cst2 = sem("s_consts_landed")
        s_x = sem("s_x_landed")
        s_c = sem("s_c_landed")
        s_par = sem("s_params_landed")
        s_pab = sem("s_decay_params_landed")
        s_ini = sem("s_memsets")
        s_cs = sem("s_csilu")
        s_xT = sem("s_xT_psum")
        s_pT0 = sem("s_params_psum")
        s_cT = sem("s_cT_ready")
        s_w = [sem(f"s_w{i}_landed") for i in range(RING)]
        s_adamm = sem("s_ada_psum")
        s_adaev = sem("s_ada_copied")
        s_adaT = sem("s_ada_transposed")
        s_modr = sem("s_mod_reduced")
        s_mod = sem("s_mod_ready")
        s_h = sem("s_h_chunks")
        s_sq = sem("s_squares")
        s_ss = sem("s_sumsq_psum")
        s_ln = sem("s_ln")
        s_rstd = sem("s_rstd")
        s_xs = sem("s_xs_chunks")
        s_smp = sem("s_hn_sample_steps")
        s_hs = sem("s_hn_sample_ready")
        s_hn = sem("s_hn_chunks")
        s_xl = sem("s_hn_rests")
        s_whi = sem("s_tile_rounded")
        s_wlo = sem("s_tile_rest")
        s_hm = sem("s_hidden_product")
        s_hh = sem("s_hidden_rounded")
        s_gate = sem("s_gate_psum")
        s_up = sem("s_up_psum")
        s_silu = sem("s_silu")
        s_hid = sem("s_hidden")
        s_dpart = sem("s_down_tile_read")
        s_sub = sem("s_sublayer_psum")
        s_dve = sem("s_dve_chain")
        s_act = sem("s_act_chain")
        s_wab = sem("s_wab_landed")
        s_win = sem("s_win_psum")
        s_xc = sem("s_xc_copied")
        s_zm = sem("s_zqkv_copied")
        s_ab = sem("s_ab_copied")
        s_conv = sem("s_conv_taps")
        s_csil = sem("s_conv_silu")
        s_cg = sem("s_conv_rows")
        s_kvT = sem("s_kv_transposed")
        s_kvt = sem("s_k_tokens")
        s_kvd = sem("s_v_tokens")
        s_cvT = sem("s_convrows_transposed")
        s_cvo = sem("s_convrows_copied")
        s_sc = sem("s_scores_psum")
        s_paS = sem("s_scores_biased")
        s_nm = sem("s_row_max")
        s_pexp = sem("s_probs")
        s_pn = sem("s_probs_scaled")
        s_paT = sem("s_probsT_psum")
        s_pTe = sem("s_probsT_copied")
        s_pav = sem("s_attn_psum")
        s_pao = sem("s_attn_copied")
        s_out = sem("s_outputs")
        s_okv = sem("s_kv_outputs_done")
        s_g8 = sem("s_decay_rows")
        s_gT = sem("s_decay_psum")
        s_gp = sem("s_delta_psum")
        s_ge = sem("s_delta_copied")
        s_gbc = sem("s_decay_spread")
        s_ecum = sem("s_exp_cum")
        s_bek = sem("s_beta_exp_cum")
        s_eg = sem("s_exp_rows")
        s_df = sem("s_decay_diff")
        s_dt = sem("s_decay_exp")
        s_qks = sem("s_qk_squares")
        s_l2 = sem("s_qk_sums_psum")
        s_l2e = sem("s_qk_sums_copied")
        s_rln = sem("s_qk_ln")
        s_rse = sem("s_qk_rstd")
        s_qkn = sem("s_qk_normalised")
        s_ntl = sem("s_level_masked")
        s_vx = sem("s_vnew_spread")
        s_st = sem("s_states_landed")
        s_go = sem("s_go_sq")
        s_gr = sem("s_go_rstd")
        s_gdn = sem("s_gdn_done")
        s_absx = sem("s_softplus_input")
        s_sp = sem("s_softplus_log")
        s_bmx = sem("s_block_max")
        s_qz = sem("s_qbd_zero")
        s_qbd = sem("s_qbd_ready")
        s_kv = [[sem(f"s_kv{i}_page{y}_landed") for i in range(KU)] for y in range(2)]
        s_vq = [[sem(f"s_vquad{i}_half{y}_landed") for i in range(4)] for y in range(2)]
        s_wo = [sem(f"s_wout{i}_landed") for i in range(2)]
        s_pt = sem("s_page_table")
        s_own = sem("s_own_psum")
        s_owns = sem("s_own_logits_copied")
        s_kt = sem("s_kt_psum")
        s_ktA = sem("s_kt_copied_act")
        s_ktD = sem("s_kt_copied_dve")
        s_qk = sem("s_logits_psum")
        s_lev = sem("s_logits_copied")
        s_pen = sem("s_selection")
        s_po = sem("s_own_probs")
        s_pe = sem("s_sel_probs")
        s_PT = sem("s_sel_probsT_psum")
        s_oT = sem("s_own_probsT_psum")
        s_pTs = sem("s_sel_probsT_copied")
        s_oTs = sem("s_own_probsT_copied")
        s_PV = sem("s_values_read")
        s_O = sem("s_sel_attn_psum")
        s_om = sem("s_sel_attn_scaled")
        s_AT = sem("s_sel_attnT_psum")
        s_mixa = sem("s_sel_attn_ready")
        s_yT = sem("s_y_transposed")
        s_y = [sem(f"s_y_half{i}_copied") for i in range(2)]
        s_yout = sem("s_y_stored")
        block = ctx.enter_context(nc.Block())

        XCs = XC[:, :, 3 + SEQ:XW].rearrange("p c (b j) -> p c b j", b=NB)

        wada = a["w_ada"][0].rearrange("(k p) n -> p k n", p=P)
        wup = [a["ffn_up"][0, l].rearrange("(k p) (g n) -> p k g n", p=P, g=2) for l in range(2)]
        wdown = [a["ffn_down"][0, l].rearrange("(f p) n -> p f n", p=P) for l in range(2)]
        win = a["w_in"][0].rearrange("(k p) n -> p k n", p=P)
        wout = a["w_out"][0].rearrange("(k p) n -> p k n", p=P)
        WIN_COL = [0, 512, 1024, 2056, 2568, 3080, 1544]

        tiles = [("ada", j) for j in range(ADA_FIRST)] + [("up", 0, 0), ("ada", 4), ("ada", 5)]
        LOOP = len(tiles)
        for i in range(5):
            tiles += [("up", 0, 1 + 2 * i), ("ada", 6 + 2 * i), ("up", 0, 2 + 2 * i), ("ada", 7 + 2 * i)]
        tiles += [("down", 0, 0, 0), ("ada", 16), ("down", 0, 0, 1), ("ada", 17), ("down", 0, 0, 2)]
        tiles += [("down", 0, 1, t) for t in range(3)]
        tiles += [("in", j) for j in range(7)]
        tiles += [("up", 1, j) for j in range(UP_TILES)]
        tiles += [("down", 1, g, t) for g in range(2) for t in range(3)]
        number = {t: n for n, t in enumerate(tiles)}

        def released(t):
            if t[0] == "ada":
                return s_adamm, t[1] + 1
            if t[0] == "up":
                return s_up, FC * t[1] + 2 * t[2] + 2
            if t[0] == "down":
                if t[3] < 2:
                    return s_dpart, 4 * t[1] + 2 * t[2] + t[3] + 1
                return s_sub, 16 * t[1] + 4 * t[2] + 4
            return s_win, 4 * t[1] + 4 + (t[1] >= 5)

        split = []
        for l in range(2):
            split += [("up", l, j) for j in range(UP_TILES)] + [("down", l, g, t) for g in range(2) for t in range(3)]
            if l == 0:
                split += [("in", j) for j in range(7)]
        IN0 = split.index(("in", 0))
        S1ST = split.index(("up", 1, 0))

        def quarter(t, q):
            if t[0] == "down" and t[3] == 2:
                return [slice(0, 2), slice(2, 4), slice(4, 5), slice(5, 6)][q]
            return slice(2 * q, 2 * q + 2)

        def halves(t, slot, j=None):
            w = wring[:, slot]
            if t[0] == "up":
                j = t[2] if j is None else j
                return [(w[:, :, 256 * g:256 * g + 256], wup[t[1]][:, :, g, bass.ds(j * 256, 256)]) for g in range(2)]
            if t[0] == "ada":
                j = t[1] if j is None else j
                return [(w[:, 4 * k:4 * k + 4, :], wada[:, 4 * k:4 * k + 4, bass.ds(j * 512, 512)]) for k in range(2)]
            if t[0] == "down":
                n = min(8, FC - 8 * t[3]) // 2
                return [(w[:, n * k:n * k + n, :], wdown[t[1]][:, 8 * t[3] + n * k:8 * t[3] + n * k + n, 512 * t[2]:512 * t[2] + 512]) for k in range(2)]
            c0 = WIN_COL[t[1]]
            return [(w[:, 4 * k:4 * k + 4, :], win[:, 4 * k:4 * k + 4, c0:c0 + 512]) for k in range(2)]

        wo = [kv[:, 4 * g:4 * g + 4].rearrange("p a b n -> p (a b) n") for g in range(2)]

        def k_unit(n, x):
            slot = (0, 2, 1)[n % 3]
            return kv[:, 4 * slot + x] if slot < 2 else shaped(extra[:, 2 * x:2 * x + 2, :].rearrange("p a b -> p (a b)"), 2, 512)

        def v_quad(q):
            return (q + 2) % 4

        def v_page(q, x):
            at = 4 * v_quad(q) + x
            return kv[:, at // 2, at % 2, :]

        cache = [a["cache_k"][0].rearrange("n p h d -> n p (h d)"), a["cache_v"][0].rearrange("n p h d -> n p (h d)")]

        def sample_steps(l):
            return {1: [("W", 2)], 2: [("us",), ("ws",)], 3: [("os",)],
                    4: [("up", k) for k in range(4)], 5: [("up", k) for k in range(4, 8)]}.get(l, [])

        def steps():
            out = [("cum",)] + [("row", j) for j in range(3)]
            out += [("kt", j) for j in range(3)] + [("vt", j) for j in range(3)] + [("gram", j) for j in range(5)]
            for l in range(7):
                groups = range(3 if l < 2 else 2)
                out += [("P", l, g) for g in groups]
                for g in groups:
                    out += ([("XP", l, g)] if 0 < l < 6 else []) + [("PX", l, g)]
                out += sample_steps(l)
            out += [("W", 1), ("U0",), ("S1",), ("V1",), ("o0",), ("o1",), ("S2",)] + [("rms", hh) for hh in range(HG)]
            return out

        STEPS = {t: k for k, t in enumerate(steps())}

        GBANKS = 5

        def copied(step):
            return s_ge, STEPS[step] + 1

        def page(eng, table, dst, which, landed):
            p = eng.value_load(ptab[0:1, bass.ds(table, 1)], min_val=0, max_val=NPHYS - 1)
            eng.dma_start(dst, cache[which][bass.ds(p, 1), :, :].rearrange("a p n -> (a p) n")).then_inc(landed, 16)

        def k_step(eng, y, k, table):
            for x in range(4):
                page(eng, table + 2 * x + y, k_unit(k % 3, x)[:, y, :], 0, s_kv[y][4 * (k % 3) + x])

        def v_step(eng, half, q, table):
            for x in (2 * half, 2 * half + 1):
                page(eng, table + 2 * x + q % 2, v_page(q, x), 1, s_vq[half][v_quad(q)])

        def first_k_steps(eng, half):
            for n, t in ((1, 4), (0, 5), (2, 6)):
                eng.wait_ge(*released(("in", t)))
                k_step(eng, half, n, 8 * n)

        def stream_rest(eng, half):
            with eng.Fori(1, 5) as i:
                for k in range(3):
                    eng.wait_ge(s_kt, i * 24 + (8 * k - 16))
                    k_step(eng, half, k, i * 24 + 8 * k)
            eng.wait_ge(s_kt, 8 * 13)
            k_step(eng, half, 15, 8 * 15)
            for q in range(4):
                eng.wait_ge(s_kt, 8 * 15 if q < 2 else 8 * 16)
                v_step(eng, half, q, 8 * (q // 2))
            with eng.Fori(1, 8) as i:
                for k in range(4):
                    eng.wait_ge(s_PV, i * 4 + (k - 3))
                    v_step(eng, half, k, i * 16 + 8 * (k // 2))

        @block.sync
        def _(sp):
            sp.dma_start(const[:, 0:lay["tri"][0]], a["consts"][:, 0:lay["tri"][0]]).then_inc(s_cst, 16)

            def load(n):
                t = tiles[n]
                if n >= RING:
                    sp.wait_ge(*released(tiles[n - RING]))
                for dst, src in halves(t, n % RING):
                    sp.dma_start(dst, src).then_inc(s_w[n % RING], 16)

            load(0)
            sp.wait_ge(s_par, 16 * 6)
            for n in range(1, LOOP + 4):
                load(n)
            sp.dma_start(const[:, lay["tri"][0]:cwidth], a["consts"][:, lay["tri"][0]:cwidth]).then_inc(s_cst2, 16)
            with sp.Fori(1, 5) as i:
                for k in range(4):
                    kind, slot = ("up", "ada", "up", "ada")[k], (LOOP + k) % RING
                    if kind == "up":
                        j = i * 2 + 1 + k // 2
                        sp.wait_ge(s_up, j * 2 - 2)
                        t = ("up", 0, 0)
                    else:
                        j = i * 2 + 6 + k // 2
                        sp.wait_ge(s_adamm, j - 1)
                        t = ("ada", 0)
                    for dst, src in halves(t, slot, j):
                        sp.dma_start(dst, src).then_inc(s_w[slot], 16)
            first_in = number[("in", 0)]
            for n in range(LOOP + 20, first_in):
                load(n)
            sp.wait_ge(s_pt, 16)
            for n in range(first_in, first_in + 7):
                load(n)
            first_k_steps(sp, 0)
            stream_rest(sp, 0)
            for g in (1, 0):
                sp.wait_ge(s_PV, 32 - 2 * g)
                for k in range(2):
                    sp.dma_start(wo[g][:, 4 * k:4 * k + 4, :], wout[:, 4 * k:4 * k + 4, 512 * g:512 * g + 512]).then_inc(s_wo[g], 16)
            sp.wait_ge(s_gdn, 1)
            sp.wait_ge(s_okv, 16 * 7)
            for n in range(first_in + 7, len(tiles)):
                load(n)
            for i in range(2):
                cols = slice(512 * i, 512 * i + 512)
                sp.wait_ge(s_y[i], 3)
                sp.dma_start(o["y_prompt"][0].rearrange("(t p) n -> p t n", p=P)[:, :, cols], ytok[:, 0:2, cols]).then_inc(s_yout, 16)
                sp.dma_start(o["y_sample"].rearrange("b t n -> (b t) n")[:, cols], ytok[0:NS, 2, cols]).then_inc(s_yout, 16)
            sp.wait_ge(s_yout, 64)

        @block.gpsimd
        def _(pool):
            pool.dma_start(xin[:, 0:2, :], a["x_prompt"][0].rearrange("(t p) d -> p t d", p=P)).then_inc(s_x, 16)
            pool.dma_start(xin[0:NS, 2, :], a["x_sample"].rearrange("b t d -> (b t) d")).then_inc(s_x, 16)
            pool.memset(cT[:], 0.0).then_inc(s_ini, 1)
            pool.memset(pab[:], 0.0).then_inc(s_ini, 1)
            pool.memset(eps[:], EPS).then_inc(s_ini, 1)

            def square(ni):
                for c in range(KD):
                    pool.wait_ge(s_h, KD * ni + c + 1)
                    nc.gpsimd.tensor_tensor(xs[:, c, :], h[:, c, :], h[:, c, :], ALU.mult).then_inc(s_sq, 1)

            square(0)
            pool.wait_ge(s_adaT, ADA_TILES)
            pool.memset(adaf[:], 0.0).then_inc(s_qz, 1)
            pool.wait_ge(s_pt, 16)
            square(1)
            first_k_steps(pool, 1)
            pool.wait_ge(s_kvt, 3)
            pool.wait_ge(s_kvd, 3)
            for name, buf in (("k", ktok), ("v", vtok)):
                pool.dma_start(o[name + "_prompt"][0, 0].rearrange("(t p) h d -> p t (h d)", p=P), buf[:, 0:2, :]).then_inc(s_okv, 16)
                pool.dma_start(o[name + "_sample"][0].rearrange("b t h d -> (b t) (h d)"), buf[0:NS, 2, :]).then_inc(s_okv, 16)
            pool.wait_ge(s_cvo, 3)
            pool.dma_start(o["conv_prompt"][0, 0], cout[0:3, :]).then_inc(s_okv, 16)
            pool.dma_start(o["conv_sample"][0].rearrange("b i n -> (b i) n"), cout[3:27, :]).then_inc(s_okv, 16)
            stream_rest(pool, 1)
            pool.wait_ge(*copied(("S2",)))
            pool.dma_start(o["gdn_prompt"][0, 0].rearrange("h k v -> k h v"), S1).then_inc(s_okv, 16)
            pool.wait_ge(*copied(("up", 7)))
            for hh in range(HG):
                pool.dma_start(o["gdn_sample"][0, :, hh].rearrange("b k v -> k b v"), st[hh]).then_inc(s_out, 16)
            square(2)
            square(3)
            pool.wait_ge(s_out, 16 * HG)
            pool.wait_ge(s_okv, 16 * 7)



        AB_TURN = 20

        def win_turn(q):
            return q + (q >= AB_TURN)

        def left_bank(turn):
            if turn < CC:
                return s_xc, turn + 1
            if turn == AB_TURN:
                return s_ab, 1
            return s_zm, turn - CC + (turn < AB_TURN)

        def sum_bank(ni):
            return 4 if ni else 0

        def probs(g):
            return [range(0, 4), range(4, 8), range(8, 9)][g]

        @block.tensor
        def _(pe):
            mm = nc.tensor.matmul

            def T(out, in_, n):
                return nc.tensor.transpose(out, in_, ident[0:n, 0:n])

            def landed(n):
                pe.wait_ge(s_w[n % RING], 32 * (n // RING + 1))

            pe.wait_ge(s_cst, 16)
            pe.wait_ge(s_cs, 1)
            for k in range(KD):
                m = T(ps[4][:, 16 * k:16 * k + NR], csil[0:NR, k * P:(k + 1) * P], NR)
            m.then_inc(s_pT0, 1)
            def ada_mm(j, slot, wait, bank=None):
                pe.wait_ge(*wait)
                if not isinstance(j, int) or j >= 2:
                    pe.wait_ge(s_adaev, j - 1)
                for k in range(KD):
                    q = 32 * (k % 4)
                    m = nc.tensor.matmul(ps[ada_bank(j) if bank is None else bank][q:q + 32, :], cT[:, k, :], wring[:, slot, k, :],
                                         start=(k < 4), stop=(k >= 4), tile_position=(0, q))
                m.then_inc(s_adamm, 1)

            par = [0]

            def ada_bank(j):
                return 4 + (j if isinstance(j, int) else par[0]) % 2

            def ada_T(j, odd, bank=None):
                pe.wait_ge(s_adaev, j + 1)
                if not isinstance(j, int) or j >= 2:
                    pe.wait_ge(s_modr, j - 1)
                for i in range(4):
                    m = T(ps[6 + odd if bank is None else bank][:, i * P:(i + 1) * P], adasb[:, odd, i * P:(i + 1) * P], P)
                m.then_inc(s_adaT, 1)

            def split_products(out, hi, lo, rhs_hi, rhs_lo, start, stop):
                nc.tensor.matmul(out, hi, rhs_hi, start=start, stop=False)
                nc.tensor.matmul(out, hi, rhs_lo, start=False, stop=False)
                return nc.tensor.matmul(out, lo, rhs_hi, start=False, stop=stop)

            def up_tile(l, j, slot, side, first=False):
                for s in range(2):
                    if not first:
                        pe.wait_ge(s_hid, j * 2 + (FC * l + s - 1))
                    for half, done in ((0, s_gate), (1, s_up)):
                        for k in range(KD):
                            if s == 0 and half == 0 and k % 2 == 0:
                                pe.wait_ge(s_wlo, j * 4 + (4 * S1ST * l + k // 2 + 1))
                            if first and s == 0 and half == 0:
                                normed(2 * l, k)
                            cols = slice(256 * half + P * s, 256 * half + P * s + P)
                            m = split_products(ps[2 * s + half][:, 0:TOK], whiR[:, side, k, cols], wringR[:, slot, k, cols],
                                               hnR[:, k, :], xsR[:, k, :], k == 0, k == KD - 1)
                        m.then_inc(done, 1)

            def normed(ni, k):
                if k == 0:
                    pe.wait_ge(s_hs, ni + 1)
                pe.wait_ge(s_hn, KD * ni + k + 1)
                pe.wait_ge(s_xl, KD * ni + k + 1)

            def sumsq(ni):
                for k in range(KD):
                    pe.wait_ge(s_sq, KD * ni + k + 1)
                    m = nc.tensor.matmul(ps[sum_bank(ni)][:, 0:TOK], ones, xs[:, k, :], start=(k == 0), stop=(k == KD - 1))
                m.then_inc(s_ss, 1)

            def down(l):
                for g in range(2):
                    for t in range(3):
                        u = split.index(("down", l, g, t))
                        slot = number[("down", l, g, t)] % RING
                        n = min(8, FC - 8 * t)
                        pe.wait_ge(s_wlo, 4 * u + 4)
                        pe.wait_ge(s_hid, FC * l + 8 * t + n)
                        for i in range(4):
                            if l == 0 and g == 0 and t == 0 and i == 3:
                                pe.wait_ge(s_modr, 16)
                            for f in range(n):
                                cols = slice(i * P, (i + 1) * P)
                                m = split_products(ps[4 * (1 - g) + i][:, 0:TOK], whiR[:, u % 2, f, cols], wringR[:, slot, f, cols],
                                                   hidR[:, 8 * t + f, :], hidR[:, FC + 8 * t + f, :],
                                                   t == 0 and f == 0, t == 2 and f == n - 1)
                            if t == 2:
                                m.then_inc(s_sub, 1)
                        if t < 2:
                            m.then_inc(s_dpart, 1)
                        if l == 0 and g == 0 and t == 0:
                            ada_mm(16, *tile(("ada", 16)), bank=0)
                        elif l == 0 and g == 0 and t == 1:
                            ada_T(16, 0, bank=2)
                            ada_mm(17, *tile(("ada", 17)), bank=1)
                        elif l == 0 and g == 0:
                            ada_T(17, 1, bank=3)
                            pe.wait_ge(s_modr, ADA_TILES)

            def tile(t):
                n = number[t]
                return n % RING, (s_w[n % RING], 32 * (n // RING + 1))

            def features():
                pe.wait_ge(s_par, 16 * 6)
                T(ps[5][:, 0:105], prow[0:105, :], 105)
                T(ps[5][:, 105:153], crow[0:48, :], 48)
                for c in range(CC):
                    m = T(ps[6][:, 24 * c:24 * c + 24], srow[0:24, c * P:(c + 1) * P], 24)
                m.then_inc(s_pT0, 1)
                pe.wait_ge(s_x, 32)
                for c in range(KD):
                    if c >= 4:
                        pe.wait_ge(s_h, c - 3)
                    for t in range(3):
                        n = P if t < 2 else NS
                        m = T(ps[c % 4][:, t * P:t * P + n], xin[0:n, t, c * P:(c + 1) * P], n)
                    m.then_inc(s_xT, 1)

            pe.wait_ge(s_cT, 1)
            for j in range(ADA_FIRST):
                ada_mm(j, *tile(("ada", j)))
                if j == 0:
                    features()
                if j:
                    ada_T(j - 1, (j - 1) % 2)
            sumsq(0)
            ada_T(3, 1)
            up_tile(0, 0, number[("up", 0, 0)] % RING, 0, first=True)
            ada_mm(4, *tile(("ada", 4)))
            ada_mm(5, *tile(("ada", 5)))
            ada_T(4, 0)
            with pe.Fori(0, 5) as i:
                for k in range(2):
                    slot = (LOOP + 2 * k) % RING
                    up_tile(0, i * 2 + 1 + k, slot, (1 + k) % 2)
                    ada_T(i * 2 + 5 + k, (5 + k) % 2)
                    slot = (LOOP + 1 + 2 * k) % RING
                    par[0] = 6 + k
                    ada_mm(i * 2 + 6 + k, slot, (s_w[slot], i * 32 + 32 * ((LOOP + 1 + 2 * k) // RING + 1)))
            ada_T(15, 1)
            pe.wait_ge(s_modr, 15)
            down(0)

            sumsq(1)
            for turn in range(29):
                q = None if turn == AB_TURN else turn - (turn > AB_TURN)
                if turn >= 8:
                    pe.wait_ge(*left_bank(turn - 8))
                if q is None:
                    pe.wait_ge(s_wab, 16)
                for k in range(KD):
                    if turn == 0:
                        normed(1, k)
                    start, stop = k == 0, k == KD - 1
                    if q is None:
                        out = ps[turn % 8][0:8, 0:TOK]
                        mm(out, wab[:, k, :], hnR[:, k, :].bitcast(F32), start=start, stop=False)
                        m = mm(out, wab[:, k, :], xsR[:, k, :].bitcast(F32), start=False, stop=stop)
                        continue
                    u, slot, cols = IN0 + q // 4, number[("in", q // 4)] % RING, slice((q % 4) * P, (q % 4 + 1) * P)
                    if q % 4 == 0:
                        pe.wait_ge(s_wlo, 4 * u + k // 2 + 1)
                    m = split_products(ps[turn % 8][:, 0:TOK], whiR[:, u % 2, k, cols], wringR[:, slot, k, cols],
                                       hnR[:, k, :], xsR[:, k, :], start, stop)
                m.then_inc(s_win, 1)

            pe.wait_ge(s_g8, 1)
            pe.wait_ge(*left_bank(23))
            for i in range(6):
                src = sc8[0:8, 2 * (i // 3), :]
                spread = gE[0:8, i // 3, :]
                m = T(ps[7][:, 8 * i:8 * i + 8], src[:, (i % 3) * P:(i % 3) * P + P] if i % 3 < 2 else spread, 8)
            m.then_inc(s_gT, 1)

            pe.wait_ge(s_zm, 16)
            pe.wait_ge(s_ab, 1)
            for q in range(6):
                src, t = (mkT, mvT)[q % 2], q // 2
                n = P if t < 2 else NS
                for c in range(4):
                    m = T(ps[q][0:n, c * P:(c + 1) * P], src[:, c, t * P:t * P + n], P)
                m.then_inc(s_kvT, 1)
            pe.wait_ge(s_cg, 1)
            for r in range(3):
                if r == 1:
                    pe.wait_ge(s_gbc, 1)
                if r == 2:
                    pe.wait_ge(s_kvt, 1)
                bank = ps[(6, 7, 0)[r]]
                for c in range(4):
                    m = T(bank[0:27, c * P:(c + 1) * P], cgat[:, 4 * r + c, :], P)
                m.then_inc(s_cvT, 1)

            pe.wait_ge(s_kvt, 3)
            pe.wait_ge(s_cvo, 3)
            pe.wait_ge(s_qbd, 8)
            for g in range(2):
                for b4 in range(4):
                    for c in range(4):
                        m = mm(ps[6][32 * b4:32 * b4 + 32, 384 + 32 * g:416 + 32 * g], Qbd[:, c, 4 * g + b4, :], mkT[:, c, SEQ:TOK],
                               start=(c == 0), stop=(c == 3), tile_position=(0, 32 * b4))
                m.then_inc((s_qk, s_own)[g], 2 - g)

            def attention(s):
                if s < HM:
                    c, r = s // 2, HD * (s % 2)
                    if s:
                        pe.wait_ge(s_paS, s)
                    mm(ps[5][:, 0:P], mqT[r:r + HD, c, 0:P], mkT[r:r + HD, c, 0:P], start=True, stop=True)
                    mm(ps[5][:, P:3 * P], mqT[r:r + HD, c, P:SEQ], mkT[r:r + HD, c, 0:SEQ], start=True, stop=True).then_inc(s_sc, 1)
                if 1 <= s <= HM:
                    x = s - 1
                    pe.wait_ge(s_pn, x + 1)
                    if x:
                        pe.wait_ge(s_pTe, x)
                    else:
                        pe.wait_ge(s_owns, 1)
                    for i in range(3):
                        m = T(ps[6][:, i * P:(i + 1) * P], psP[:, x % 2, i * P:(i + 1) * P], P)
                    m.then_inc(s_paT, 1)
                if 2 <= s < HM + 2:
                    x = s - 2
                    c, r = x // 2, HD * (x % 2)
                    pe.wait_ge(s_pTe, x + 1)
                    if x == 0:
                        pe.wait_ge(s_gbc, 1)
                    if x % 2 == 0 and c:
                        pe.wait_ge(s_pao, c)
                    out = ps[7][r:r + HD, 0:SEQ]
                    mm(out, vtok[:, 0, x * HD:(x + 1) * HD], psT[:, x % 2, 0:SEQ], start=True, stop=False)
                    mm(out[:, P:SEQ], vtok[:, 1, x * HD:(x + 1) * HD], psT[:, x % 2, SEQ:3 * P], start=False, stop=True).then_inc(s_pav, 1)

            def logits(m):
                n, c = m // 4, m % 4
                pe.wait_ge(s_ktA, m + 3)
                pe.wait_ge(s_ktD, m + 3)
                if c == 0:
                    pe.wait_ge(s_lev, n + 1)
                for b4 in range(4):
                    ins = mm(ps[4][32 * b4:32 * b4 + 32, 0:BLK], Qbd[:, c, 4 * (n // NBLK) + b4, :],
                             ktb[:, c % 2, b4 // 2, (b4 % 2) * BLK:(b4 % 2 + 1) * BLK],
                             start=(c == 0), stop=(c == 3), tile_position=(0, 32 * b4))
                ins.then_inc(s_qk, 1)

            def qk_sums(n):
                for x in range(2 if n < 13 else 0):
                    c = 2 * (n - 9) + x
                    pe.wait_ge(s_qks, c + 1)
                    if c >= 2:
                        pe.wait_ge(s_l2e, c - 1)
                    mm(ps[5 + x][:, 0:TOK], ones, psS[:, x, 0:TOK], start=True, stop=True).then_inc(s_l2, 1)

            def values(n):
                if n < 2 * NBLK:
                    if n % NBLK == 0:
                        g = n // NBLK
                        pe.wait_ge(s_po, g + 1)
                        T(ps[6][0:32, BLK + P * g:BLK + P * g + P], pown[:, g, :], P).then_inc(s_oT, 1)
                    pe.wait_ge(s_pe, n + 1)
                    if n:
                        pe.wait_ge(s_pTs, n)
                    for y in range(2):
                        m = T(ps[5][:, y * P:(y + 1) * P], pex[:, n % 2, y * P:(y + 1) * P], P)
                    m.then_inc(s_PT, 1)
                if n == NBLK + 1:
                    gathered(0)
                n -= 1
                if n < 0:
                    return
                g, blk = n // NBLK, n % NBLK
                pe.wait_ge(s_pTs, n + 1)
                for y in range(2):
                    q = 2 * n + y
                    for half in range(2):
                        pe.wait_ge(s_vq[half][v_quad(q)], 32 * (q // 4 + 1))
                    for b4 in range(4):
                        m = mm(ps[7][32 * b4:32 * b4 + 32, :], pT[:, n % 2, y, 32 * b4:32 * b4 + 32], v_page(q, b4),
                               start=(blk == 0 and y == 0), stop=False, tile_position=(0, 32 * b4))
                    m.then_inc(s_PV, 1)
                if blk == NBLK - 1:
                    pe.wait_ge(s_oTs, g + 1)
                    for b4 in range(4):
                        m = mm(ps[7][32 * b4:32 * b4 + 32, :], ownT[0:32, g, 32 * b4:32 * b4 + 32], vown[0:32, :],
                               start=False, stop=True, tile_position=(0, 32 * b4))
                    m.then_inc(s_O, 1)

            def gathered(g):
                pe.wait_ge(s_om, g + 1)
                for c in range(4):
                    m = mm(ps[6][:, 64 * g + 16 * c:64 * g + 16 * c + 16], Om[:, c * P:(c + 1) * P], cst("selbt"), start=True, stop=True)
                m.then_inc(s_AT, 1)

            for m in range(4 * 2 * NBLK):
                n, c = m // 4, m % 4
                for pair in range(2):
                    pe.wait_ge((s_ktA, s_ktD)[pair], m + 1)
                    for x in range(2):
                        if c == 0:
                            for y in range(2):
                                pe.wait_ge(s_kv[y][4 * (n % 3) + 2 * pair + x], 16 * (n // 3 + 1))
                        for y in range(2):
                            ins = T(ps[2 * (c % 2) + pair][:, x * BLK + y * PAGE:x * BLK + (y + 1) * PAGE],
                                    k_unit(n, 2 * pair + x)[:, y, c * P:(c + 1) * P], P)
                    ins.then_inc(s_kt, 1)
                if c == 2:
                    attention(n)
                    if n >= 9:
                        qk_sums(n)
                    if n == 2 * NBLK - 2:
                        values(0)
                if m:
                    logits(m - 1)
            logits(4 * 2 * NBLK - 1)

            def bank(step):
                k = STEPS[step]
                if k >= GBANKS:
                    pe.wait_ge(s_ge, k - GBANKS + 1)
                return ps[k % GBANKS]

            pe.wait_ge(s_gbc, 2)
            pe.wait_ge(s_pao, 4)
            pe.wait_ge(s_lev, 2 * NBLK + 1)
            b = bank(("cum",))
            mm(b[:, 0:8], tri, G9[:, 0:8], start=True, stop=True)
            mm(b[:, 8:9], triS, G9[:, 8:9], start=True, stop=True)
            mm(b[:, 9:17], later, G9[:, 0:8], start=True, stop=True)
            mm(b[:, 17:18], laterS, G9[:, 8:9], start=True, stop=True).then_inc(s_gp, 1)
            values(1)
            for j in range(3):
                b = bank(("row", j))
                for x, p in enumerate(probs(j)):
                    m = mm(b[:, x * P:(x + 1) * P], Pv[:, p, :], tri if p < 8 else triS, start=True, stop=True)
                m.then_inc(s_gp, 1)
            values(2)
            pe.wait_ge(s_qkn, 1)
            for kind, base in (("kt", 4), ("vt", 8)):
                for j in range(3):
                    b = bank((kind, j))
                    for x, p in enumerate(probs(j)):
                        if p == 8:
                            src = smp[:, 1 if kind == "kt" else 2, :]
                        else:
                            src = (QK if kind == "kt" else Cv)[:, base + p % 4, (p // 4) * P:(p // 4 + 1) * P]
                        m = T(b[:, x * P:(x + 1) * P], src, P)
                    m.then_inc(s_gp, 1)
                if kind == "kt":
                    values(3)
            values(4)
            QKh = QK.rearrange("p (two hh) n -> p hh two n", two=2)
            for j in range(5):
                b = bank(("gram", j))
                for x, p in enumerate(range(2 * j, min(2 * j + 2, NPROB))):
                    if p == 8:
                        k_, qk_ = smp[:, 1, :], smp[:, 0:2, :]
                    else:
                        cols = slice((p // 4) * P, (p // 4 + 1) * P)
                        k_, qk_ = QK[:, 4 + p % 4, cols], QKh[:, p % 4, :, cols]
                    m = mm(b[:, 2 * P * x:2 * P * (x + 1)], k_, qk_, start=True, stop=True)
                m.then_inc(s_gp, 1)
            values(5)

            def w_rows(g):
                b = bank(("W", g))
                for x, p in enumerate(probs(g)):
                    m = mm(b[:, x * P:(x + 1) * P], KB[:, p, :], XT[:, p, :], start=True, stop=True)
                m.then_inc(s_gp, 1)

            def sample(l):
                if l == 1:
                    pe.wait_ge(*copied(("PX", 1, 2)))
                    w_rows(2)
                elif l == 2:
                    mm(bank(("us",))[:, 0:P], XT[:, 8, :], VB[:, 8, :], start=True, stop=True).then_inc(s_gp, 1)
                    pe.wait_ge(*copied(("W", 2)))
                    pe.wait_ge(s_st, 64)
                    b = bank(("ws",))
                    for side in range(2):
                        for sq in range(NB):
                            for hh in range(HG):
                                m = mm(b[NS * hh:NS * hh + NS, side * P:(side + 1) * P], WX[side][:, hh, NS * sq:NS * sq + NS],
                                       st[hh][:, sq, :], start=(sq == 0), stop=(sq == NB - 1), tile_position=(0, NS * hh))
                    m.then_inc(s_gp, 1)
                elif l == 3:
                    pe.wait_ge(*copied(("ws",)))
                    b = bank(("os",))[:, 0:P]
                    mm(b, VX[:, 1, :], ident, start=True, stop=False)
                    mm(b, VN[:, 8, :], AN[:, 8, 0, :], start=False, stop=True).then_inc(s_gp, 1)
                elif l in (4, 5):
                    pe.wait_ge(s_vx, 1)
                    for x in range(4 * l - 16, 4 * l - 12):
                        hh, half = x // 2, x % 2
                        rows = slice(NS * hh, NS * hh + NS)
                        mm(bank(("up", x))[:, :], KDc[rows, 8, :], VX[rows, 4 * half:4 * half + 4, :].rearrange("p a b -> p (a b)"),
                           start=True, stop=True).then_inc(s_gp, 1)

            nt = 0
            for l in range(7):
                groups = range(3 if l < 2 else 2)
                for g in groups:
                    b = bank(("P", l, g))
                    nt += 1
                    pe.wait_ge(s_ntl, nt)
                    if l:
                        pe.wait_ge(*copied(("PX", l - 1, g)))
                    for x, p in enumerate(probs(g)):
                        m = mm(b[:, x * P:(x + 1) * P], NTl[:, p, :], X[:, p, :] if l else ident, start=True, stop=True)
                    m.then_inc(s_gp, 1)
                if l < 6:
                    values(6 + 2 * l)
                for g in groups:
                    pe.wait_ge(*copied(("P", l, g)))
                    if 0 < l < 6:
                        b = bank(("XP", l, g))
                        for x, p in enumerate(probs(g)):
                            m = mm(b[:, x * P:(x + 1) * P], XT[:, p, :], Pv[:, p, :], start=True, stop=True)
                        m.then_inc(s_gp, 1)
                    b = bank(("PX", l, g))
                    for x, p in enumerate(probs(g)):
                        m = mm(b[:, x * P:(x + 1) * P], Pv[:, p, :], XT[:, p, :] if l else ident, start=True, stop=True)
                    m.then_inc(s_gp, 1)
                if l < 5:
                    values(7 + 2 * l)
                sample(l)
            pe.wait_ge(*copied(("PX", 6, 1)))
            w_rows(1)
            b = bank(("U0",))
            for x in range(4):
                m = mm(b[:, x * P:(x + 1) * P], XT[:, x, :], VB[:, x, :], start=True, stop=True)
            m.then_inc(s_gp, 1)
            pe.wait_ge(*copied(("U0",)))
            b = bank(("S1",))
            for x in range(4):
                m = mm(b[:, x * P:(x + 1) * P], KDc[:, x, :], VN[:, x, :], start=True, stop=True)
            m.then_inc(s_gp, 1)
            pe.wait_ge(*copied(("S1",)))
            b = bank(("V1",))
            for x in range(4):
                mm(b[:, x * P:(x + 1) * P], XT[:, 4 + x, :], VB[:, 4 + x, :], start=True, stop=False)
                m = mm(b[:, x * P:(x + 1) * P], WT[:, 4 + x, :], S1[:, x, :], start=False, stop=True)
            m.then_inc(s_gp, 1)
            b = bank(("o0",))
            for x in range(4):
                m = mm(b[:, x * P:(x + 1) * P], VN[:, x, :], AN[:, x, 0, :], start=True, stop=True)
            m.then_inc(s_gp, 1)
            pe.wait_ge(*copied(("V1",)))
            b = bank(("o1",))
            for x in range(4):
                mm(b[:, x * P:(x + 1) * P], VN[:, 4 + x, :], AN[:, 4 + x, 0, :], start=True, stop=False)
                m = mm(b[:, x * P:(x + 1) * P], S1[:, x, :], QD[:, 4 + x, :], start=False, stop=True)
            m.then_inc(s_gp, 1)
            b = bank(("S2",))
            for x in range(4):
                m = mm(b[:, x * P:(x + 1) * P], KDc[:, 4 + x, :], VN[:, 4 + x, :], start=True, stop=True)
            m.then_inc(s_gp, 1)
            gathered(1)
            pe.wait_ge(s_go, 1)
            for hh in range(HG):
                mm(bank(("rms", hh))[:, 0:TOK], ones, sqg[:, hh, :], start=True, stop=True).then_inc(s_gp, 1)

            pe.wait_ge(s_mixa, 2)
            pe.wait_ge(s_ge, len(STEPS))
            for g in range(2):
                pe.wait_ge(s_wo[g], 32)
                for part in (range(4, 8), range(4)):
                    if part[0] == 0 and g == 0:
                        pe.wait_ge(s_gdn, 1)
                    for i in range(4):
                        for k in part:
                            m = mm(ps[4 * (1 - g) + i][:, 0:TOK], wo[g][:, k, i * P:(i + 1) * P], mix[:, k, :],
                                   start=(k == 4), stop=(k == 3))
                        if part[0] == 0:
                            m.then_inc(s_sub, 1)

            sumsq(2)
            for j in range(3):
                up_tile(1, j, number[("up", 1, j)] % RING, (S1ST + j) % 2, first=(j == 0))
            with pe.Fori(0, 2) as i:
                for k in range(4):
                    n = number[("up", 1, 3)] + k
                    up_tile(1, i * 4 + 3 + k, n % RING, (S1ST + 3 + k) % 2)
            down(1)

            sumsq(3)
            for q in range(6):
                t, half = q % 3, q // 3
                pe.wait_ge(s_hn, KD * 3 + 4 * half + 4)
                n = P if t < 2 else NS
                for c in range(4):
                    m = T(ps[1 + q][0:n, c * P:(c + 1) * P], hn[:, 4 * half + c, t * P:t * P + n], P)
                m.then_inc(s_yT, 1)

        @block.scalar
        def _(act):
            def fn(out, in_, func, **kw):
                return nc.scalar.activation(out, in_, func, **kw)

            def own(ins, s=s_act, count=[0]):
                count[0] += 1
                ins.then_inc(s, 1)
                act.wait_ge(s, count[0])

            act.dma_start(cin[0:1, :], a["c_prompt"]).then_inc(s_c, 16)
            act.dma_start(cin[1:NR, :], a["c_sample"]).then_inc(s_c, 16)
            act.dma_start(prow[0:72, :], a["b_ada"][0].rearrange("(r p) -> r p", p=P)).then_inc(s_par, 16)
            act.dma_start(prow[72:96, :], a["norm_w"][0].rearrange("i (r p) -> (i r) p", p=P)).then_inc(s_par, 16)
            act.dma_start(prow[96:104, :], a["final_norm_w"].rearrange("(r p) -> r p", p=P)).then_inc(s_par, 16)
            act.dma_start(prow[104:105, :], a["gdn_norm_w"]).then_inc(s_par, 16)
            act.dma_start(crow[0:48, :], a["conv_w"][0].rearrange("i (c p) -> (i c) p", p=P)).then_inc(s_par, 16)
            act.dma_start(srow[0:24, :], a["state_conv"][0].rearrange("b i n -> (b i) n")).then_inc(s_par, 16)
            act.wait_ge(s_c, 32)
            fn(csil[0:NR, :], cin[0:NR, :], ACT.Silu).then_inc(s_cs, 1)
            def round_quarters(u, qs, i=0, step=0):
                t, n = split[u], number[split[u]]
                if 0 in qs:
                    act.wait_ge(s_w[n % RING], i * (8 * step * (1 + (u < S1ST))) + 32 * (n // RING + 1))
                    if u == S1ST:
                        act.wait_ge(s_sub, 12)
                    elif u == S1ST + 1:
                        act.wait_ge(s_sub, 16)
                    elif u >= 2:
                        free, count = released(split[u - 2])
                        act.wait_ge(free, i * (2 * step) + count)
                for q in qs:
                    c = quarter(t, q)
                    nc.scalar.copy(whiR[:, u % 2, c, :], wring[:, n % RING, c, :]).then_inc(s_whi, 1)

            def norm(ni):
                fn(pab[:, 3:4], eps[0:8, :], ACT.Ln)
                act.wait_ge(s_ss, ni + 1)
                fn(rstd[:, :], ps[sum_bank(ni)][:, 0:TOK], ACT.Ln, scale=1.0 / D, bias=eps[:, 0:1]).then_inc(s_ln, 1)
                act.wait_ge(s_ln, ni + 1)
                fn(rstd[:, :], rstd[:, :], ACT.Exp, scale=-0.5).then_inc(s_rstd, 1)
                if ni < 3:
                    sh = modT[:, 3 * ni * KD:(3 * ni + 1) * KD, :]
                    for c in range(KD):
                        if ni == 0 and c % 2 == 0:
                            round_quarters(0, (c // 2,))
                        act.wait_ge(s_xs, KD * ni + c + 1)
                        fn(hnR[:, c, 0:SEQ], xs[:, c, 0:SEQ], ACT.Identity, bias=sh[:, c, 0:1]).then_inc(s_hn, 1)

            def ada_copy(j, odd):
                act.wait_ge(s_adamm, j + 1)
                if not isinstance(j, int) or j >= 2:
                    act.wait_ge(s_adaT, j - 1)
                nc.scalar.copy(adasb[:, odd, :], ps[4 + odd][:, :]).then_inc(s_adaev, 1)

            def gate_silu(l, f, odd):
                act.wait_ge(s_gate, f + (FC * l + 1))
                if l or not isinstance(f, int) or f >= 2:
                    act.wait_ge(s_hid, f + (FC * l - 1))
                fn(sgate[:, odd, :], ps[2 * odd][:, 0:TOK], ACT.Silu).then_inc(s_silu, 1)

            for j in range(ADA_FIRST):
                ada_copy(j, j % 2)
                if j == 0:
                    act.dma_start(wab[:, :, :], win[:, :, 1536:1544]).then_inc(s_wab, 16)
                    act.dma_start(ptab[:, :], a["ptab"]).then_inc(s_pt, 16)
                    act.wait_ge(s_ini, 3)
                    act.dma_start(pab[0:HG, 0:1], a["dt_bias"].rearrange("o h -> h o")).then_inc(s_pab, 16)
                    act.dma_start(pab[0:HG, 1:2], a["a_log"].rearrange("o h -> h o")).then_inc(s_pab, 16)
            norm(0)
            gate_silu(0, 0, 0)
            gate_silu(0, 1, 1)
            ada_copy(4, 0)
            ada_copy(5, 1)
            round_quarters(1, range(4))
            with act.Fori(0, 5) as i:
                for k in range(2):
                    gate_silu(0, i * 4 + (2 + 2 * k), 0)
                    round_quarters(2 + k, (0, 1), i, 2)
                    gate_silu(0, i * 4 + (3 + 2 * k), 1)
                    round_quarters(2 + k, (2, 3), i, 2)
                    ada_copy(i * 2 + (6 + k), k)
            for u in range(UP_TILES + 1, IN0 + 1):
                round_quarters(u, range(4))
                if u < UP_TILES + 3:
                    j = 16 + u - UP_TILES - 1
                    act.wait_ge(s_adamm, j + 1)
                    act.wait_ge(s_adaT, j - 1)
                    nc.scalar.copy(adasb[:, j % 2, :], ps[j % 2][:, :]).then_inc(s_adaev, 1)

            norm(1)

            def zqkv(q):
                act.wait_ge(s_win, win_turn(q) + 1)
                src, kind, c = ps[win_turn(q) % 8][:, 0:TOK], (q - 12) // 4, q % 4
                if kind == 0:
                    ins = nc.scalar.mul(mqT[:, c, :], src, HD ** -0.5)
                elif kind < 3:
                    ins = nc.scalar.copy((mkT, mvT)[kind - 1][:, c, :], src)
                else:
                    ins = fn(zs[:, c, :], src, ACT.Silu)
                ins.then_inc(s_zm, 1)

            def conv_silu(grp):
                for j in range(4):
                    cc = 4 * grp + j
                    act.wait_ge(s_conv, 16 * grp + 12 + j + 1)
                    fn(Cv[:, cc, 0:SEQ], Yb[:, j, 0:SEQ], ACT.Silu)
                    fn(Cv[:, cc, SEQ:TOK].rearrange("p (b t) -> p b t", b=NB),
                       Yb[:, j, 3 + SEQ:XW].rearrange("p (b s) -> p b s", b=NB)[:, :, 0:NT], ACT.Silu).then_inc(s_csil, 1)

            for j in range(1, 5):
                round_quarters(IN0 + j, range(4))
            for q in range(12, 16):
                zqkv(q)
            conv_silu(0)
            round_quarters(IN0 + 5, range(4))
            for q in range(16, 20):
                zqkv(q)
            conv_silu(1)
            round_quarters(IN0 + 6, range(4))
            act.wait_ge(s_win, AB_TURN + 1)
            nc.scalar.copy(abT[:, :], ps[AB_TURN % 8][0:8, 0:TOK]).then_inc(s_ab, 1)
            conv_silu(2)
            for q in range(20, 24):
                zqkv(q)
            act.wait_ge(s_absx, 1)
            act.wait_ge(s_pab, 32)
            act.wait_ge(s_ab, 1)
            fn(sc8[0:8, 2, :], abT[:, :], ACT.Sigmoid)
            fn(pab[:, 2:3], pab[:, 1:2], ACT.Exp)
            own(fn(sc8[0:8, 1, :], sc8[0:8, 1, :], ACT.Exp))
            fn(sc8[0:8, 1, :], sc8[0:8, 1, :], ACT.Ln, bias=1.0).then_inc(s_sp, 1)
            act.wait_ge(s_win, 29)
            for q in range(24, 28):
                zqkv(q)
            for q in range(0, 6, 2):
                act.wait_ge(s_kvT, q + 1)
                n = P if q < 4 else NS
                nc.scalar.copy(ktok[0:n, q // 2, :], ps[q][0:n, :]).then_inc(s_kvt, 1)
            act.wait_ge(s_qz, 1)
            act.wait_ge(s_zm, 12)
            for c in range(4):
                for hh in range(2):
                    rows, head = slice(HD * hh, HD * hh + HD), 2 * c + hh
                    nc.scalar.copy(Qbd[rows, c, :, NT * head:NT * head + NT],
                                   mqT[rows, c, SEQ:TOK].rearrange("p (b t) -> p b t", b=NB)).then_inc(s_qbd, 1)
            act.sem_inc(s_ktA, 2)

            def probabilities(n):
                if n >= 2 * NBLK:
                    return
                g, blk = n // NBLK, n % NBLK
                act.wait_ge(s_pen, g + 1)
                if blk == 0:
                    fn(pown[:, g, :], sown[:, g, :], ACT.Exp, bias=pen[:, g, NBLK:NBLK + 1],
                       accum_out=rsum[:, g, NBLK:NBLK + 1]).then_inc(s_po, 1)
                if n >= 2:
                    act.wait_ge(s_PT, n - 1)
                fn(pex[:, n % 2, :], S[:, g, blk * BLK:(blk + 1) * BLK], ACT.Exp, bias=pen[:, g, blk:blk + 1],
                   accum_out=rsum[:, g, blk:blk + 1]).then_inc(s_pe, 1)

            for m in range(4 * 2 * NBLK):
                act.wait_ge(s_kt, 2 * m + 1)
                act.wait_ge(s_qk, m + 1)
                nc.scalar.copy(ktb[:, m % 2, 0, :], ps[2 * (m % 2)][:, :]).then_inc(s_ktA, 1)
                s = m // 4
                if 52 <= m < 56:
                    part = RS[:, 4 * (m % 2):4 * (m % 2) + 4, :]
                    act.wait_ge(s_l2e, 8)
                    if m < 54:
                        fn(part, part, ACT.Ln).then_inc(s_rln, 1)
                    else:
                        act.wait_ge(s_rln, 2)
                        fn(part, part, ACT.Exp, scale=-0.5).then_inc(s_rse, 1)
                if m in (56, 57):
                    probabilities(m - 56)
                if m % 4 < 3:
                    continue
                if 8 <= s < 12:
                    for x in range(2):
                        c = 2 * (s - 8) + x
                        if c >= 2:
                            act.wait_ge(s_l2, c - 1)
                        fn(psS[:, x, 0:TOK], Cv[:, c, :], ACT.Square).then_inc(s_qks, 1)
                if 1 <= s <= HM:
                    x = s - 1
                    act.wait_ge(s_paT, x + 1)
                    if x >= 2:
                        act.wait_ge(s_pav, x - 1)
                    nc.scalar.copy(psT[:, x % 2, :], ps[6][:, 0:3 * P]).then_inc(s_pTe, 1)
                if s < HM:
                    act.wait_ge(s_nm, s + 1)
                    if s >= 2:
                        act.wait_ge(s_paT, s - 1)
                    fn(psP[:, s % 2, 0:P], psS[:, s % 2, 0:P], ACT.Exp, bias=patt[:, 2 * s:2 * s + 1],
                       accum_out=patt[:, 16 + 2 * s:17 + 2 * s])
                    fn(psP[:, s % 2, P:3 * P], psS[:, s % 2, P:3 * P], ACT.Exp, bias=patt[:, 2 * s + 1:2 * s + 2],
                       accum_out=patt[:, 17 + 2 * s:18 + 2 * s]).then_inc(s_pexp, 1)

            probabilities(2)
            act.wait_ge(*copied(("cum",)))
            fn(ecum, cum, ACT.Exp).then_inc(s_ecum, 1)
            for j in range(3):
                act.wait_ge(*copied(("row", j)))
                pr = probs(j)
                fn(EG[:, pr[0]:pr[-1] + 1, :], gR[:, pr[0]:pr[-1] + 1, :], ACT.Exp).then_inc(s_eg, 1)
            probabilities(3)
            act.wait_ge(s_df, 1)
            fn(DT, DT, ACT.Exp).then_inc(s_dt, 1)
            act.wait_ge(s_qkn, 1)
            act.wait_ge(s_lev, 2 * NBLK + 1)
            act.wait_ge(s_own, 1)
            for hh in range(HG):
                act.dma_start(st[hh], a["state_gdn"][0, :, hh].rearrange("b k v -> k b v")).then_inc(s_st, 16)
            for n in range(4, 2 * NBLK):
                probabilities(n)
            act.wait_ge(*copied(("o1",)))
            fn(sqg[:, 0:HG, :], goT, ACT.Square).then_inc(s_go, 1)
            act.wait_ge(*copied(("rms", HG - 1)))
            own(fn(sqg[:, HG:8, :], sqg[:, HG:8, :], ACT.Ln))
            fn(sqg[:, HG:8, :], sqg[:, HG:8, :], ACT.Exp, scale=-0.5).then_inc(s_gr, 1)

            round_quarters(S1ST, range(4))
            norm(2)
            for j in range(3):
                round_quarters(S1ST + j + 1, (0, 1, 2))
                gate_silu(1, 2 * j, 0)
                round_quarters(S1ST + j + 1, (3,))
                gate_silu(1, 2 * j + 1, 1)
            with act.Fori(0, 2) as i:
                for k in range(4):
                    round_quarters(S1ST + 4 + k, (0, 1, 2), i, 4)
                    gate_silu(1, i * 8 + (6 + 2 * k), 0)
                    round_quarters(S1ST + 4 + k, (3,), i, 4)
                    gate_silu(1, i * 8 + (7 + 2 * k), 1)
            for u in range(S1ST + UP_TILES + 1, len(split)):
                round_quarters(u, range(4))
            norm(3)
            for t in range(0, 6, 2):
                act.wait_ge(s_yT, t + 1)
                n = NS if t % 3 == 2 else P
                nc.scalar.copy(ytok[0:n, t % 3, 512 * (t // 3):512 * (t // 3) + 512], ps[1 + t][0:n, :]).then_inc(s_y[t // 3], 1)

        @block.vector
        def _(dve):
            v = nc.vector

            def own(ins, count=[0]):
                count[0] += 1
                ins.then_inc(s_dve, 1)
                dve.wait_ge(s_dve, count[0])

            def bt(x):
                return x.rearrange("p (b t) -> p b t", b=NB)

            dve.wait_ge(s_ini, 3)
            dve.wait_ge(s_pT0, 1)
            v.tensor_copy(cT[:, :, 0:NR], ps[4][:, 0:P].rearrange("p (k r) -> p k r", k=KD)[:, :, 0:NR]).then_inc(s_cT, 1)
            dve.wait_ge(s_pT0, 2)
            v.tensor_copy(pvec[:, :], ps[5][:, 0:153])
            own(v.tensor_copy(cst3[:, :, :], ps[6][:, 0:CC * 24].rearrange("p (c x) -> p c x", c=CC)))
            for c in range(KD):
                dve.wait_ge(s_xT, c + 1)
                v.tensor_copy(h[:, c, :], ps[c % 4][:, 0:TOK]).then_inc(s_h, 1)

            def mod_tile(j, odd, bank=None):
                dve.wait_ge(s_adaT, j + 1)
                part = ps[6 + odd if bank is None else bank][:, :].rearrange("p (c g r) -> p c r g", c=4, g=4)[:, :, 0:NR, :]
                at = bass.ds(j * 4, 4)
                v.tensor_reduce(modT[:, at, :], part, AX_X, ALU.add).then_inc(s_modr, 1)
                dve.wait_ge(s_modr, j + 1)
                v.tensor_tensor(modT[:, at, :], modT[:, at, :], bw[:, at].unsqueeze(2).to_broadcast([P, 4, NR]),
                                ALU.add).then_inc(s_mod, 1)

            def rest_quarters(u, qs, i=0, step=0):
                t, slot = split[u], number[split[u]] % RING
                for q in qs:
                    c = quarter(t, q)
                    dve.wait_ge(s_whi, i * (4 * step) + (4 * u + q + 1))
                    v.tensor_tensor(wringR[:, slot, c, :], wring[:, slot, c, :], whiR[:, u % 2, c, :], ALU.subtract).then_inc(s_wlo, 1)

            def norm(ni):
                if ni < 3:
                    dve.wait_ge(s_mod, ADA_FIRST if ni == 0 else ADA_TILES)
                    sh = modT[:, 3 * ni * KD:(3 * ni + 1) * KD, :]
                    own(v.scalar_tensor_tensor(coef[:, :, :], modT[:, (3 * ni + 1) * KD:(3 * ni + 2) * KD, :], 1.0,
                                           nw[:, KD * ni:KD * ni + KD].unsqueeze(2).to_broadcast([P, KD, NR]), ALU.add, ALU.mult))
                    smp4_ = hn[:, :, SEQ:TOK].rearrange("p c (b t) -> p c b t", b=NB)
                    own(v.tensor_tensor(smp4_, h[:, :, SEQ:TOK].rearrange("p c (b t) -> p c b t", b=NB),
                                        coef[:, :, 1:NR].unsqueeze(3).to_broadcast([P, KD, NB, NT]), ALU.mult))
                    v.sem_inc(s_smp, 1)
                dve.wait_ge(s_rstd, ni + 1)
                if ni == 3:
                    for c in range(KD):
                        v.scalar_tensor_tensor(hn[:, c, :], h[:, c, :], nw[:, 24 + c:25 + c], rstd[:, :], ALU.mult, ALU.mult).then_inc(s_hn, 1)
                    return

                def smp4(x):
                    return x[:, :, SEQ:TOK].rearrange("p c (b t) -> p c b t", b=NB)

                def spread(x):
                    return x[:, :, 1:NR].unsqueeze(3).to_broadcast([P, KD, NB, NT])

                def scaled(c):
                    v.scalar_tensor_tensor(xs[:, c, 0:SEQ], h[:, c, 0:SEQ], coef[:, c, 0:1], rstd[:, 0:SEQ], ALU.mult, ALU.mult).then_inc(s_xs, 1)

                def rest(c):
                    dve.wait_ge(s_hn, KD * ni + c + 1)
                    v.scalar_tensor_tensor(xsR[:, c, 0:SEQ], xs[:, c, 0:SEQ], sh[:, c, 0:1], hnR[:, c, 0:SEQ], ALU.add, ALU.subtract).then_inc(s_xl, 1)

                smp = slice(SEQ, TOK)
                scaled(0)
                v.tensor_tensor(xs[:, :, smp], hn[:, :, smp], rstd[:, smp].unsqueeze(1).to_broadcast([P, KD, NS]), ALU.mult).then_inc(s_smp, 1)
                scaled(1)
                dve.wait_ge(s_smp, 4 * ni + 2)
                v.tensor_tensor(smp4(xs), smp4(xs), spread(sh), ALU.add).then_inc(s_smp, 1)
                scaled(2)
                dve.wait_ge(s_smp, 4 * ni + 3)
                v.tensor_copy(hnR[:, :, smp], xs[:, :, smp]).then_inc(s_smp, 1)
                rest(0)
                dve.wait_ge(s_smp, 4 * ni + 4)
                v.tensor_tensor(xsR[:, :, smp], xs[:, :, smp], hnR[:, :, smp], ALU.subtract).then_inc(s_hs, 1)
                if ni == 0:
                    rest_quarters(0, (0,))
                for c in range(1, KD):
                    if c + 2 < KD:
                        scaled(c + 2)
                    rest(c)
                    if ni == 0 and c % 2 == 0:
                        rest_quarters(0, (c // 2,))

            def hidden(l, f, odd):
                dve.wait_ge(s_silu, f + (FC * l + 1))
                dve.wait_ge(s_up, f + (FC * l + 1))
                both = sgate[:, odd, :]
                v.tensor_tensor(both, both, ps[2 * odd + 1][:, 0:TOK], ALU.mult).then_inc(s_hm, 1)
                dve.wait_ge(s_hm, f + (FC * l + 1))

                def chunk(x, f):
                    return x[:, bass.ds(f, 1), :].rearrange("p o n -> p (o n)")

                v.tensor_copy(chunk(hidR, f), both).then_inc(s_hh, 1)
                dve.wait_ge(s_hh, f + (FC * l + 1))
                v.tensor_tensor(chunk(hidR, f + FC), both, chunk(hidR, f), ALU.subtract).then_inc(s_hid, 1)

            def residual(si, between):
                mod = modT[:, (3 * si + 2) * KD:(3 * si + 3) * KD, :]
                gt = mod
                if si != 1:
                    own(v.tensor_scalar(gate[:, :, :], mod, 0.5, None, ALU.mult))
                    gt = gate
                for m in range(KD):
                    for u in between if m == 4 else ():
                        rest_quarters(u, range(4))
                    dve.wait_ge(s_sub, KD * si + m + 1)
                    b = ps[4 + m] if m < 4 else ps[m - 4]
                    own(v.tensor_tensor(samp[:, m % 2], bt(b[:, SEQ:TOK]), gt[:, m, 1:NR].unsqueeze(2).to_broadcast([P, NB, NT]), ALU.mult))
                    v.scalar_tensor_tensor(h[:, m, 0:SEQ], b[:, 0:SEQ], gt[:, m, 0:1], h[:, m, 0:SEQ], ALU.mult, ALU.add)
                    v.tensor_tensor(bt(h[:, m, SEQ:TOK]), bt(h[:, m, SEQ:TOK]), samp[:, m % 2], ALU.add).then_inc(s_h, 1)

            for j in range(ADA_FIRST):
                mod_tile(j, j % 2)
            norm(0)
            hidden(0, 0, 0)
            hidden(0, 1, 1)
            mod_tile(4, 0)
            rest_quarters(1, range(4))
            with dve.Fori(0, 5) as i:
                for k in range(2):
                    hidden(0, i * 4 + (2 + 2 * k), 0)
                    rest_quarters(2 + k, (0, 1), i, 2)
                    hidden(0, i * 4 + (3 + 2 * k), 1)
                    rest_quarters(2 + k, (2, 3), i, 2)
                    mod_tile(i * 2 + (5 + k), 1 - k)
            mod_tile(15, 1)
            rest_quarters(UP_TILES + 1, range(4))
            rest_quarters(UP_TILES + 2, range(4))
            mod_tile(16, 0, bank=2)
            rest_quarters(UP_TILES + 3, range(4))
            mod_tile(17, 1, bank=3)
            rest_quarters(UP_TILES + 4, range(4))
            dve.wait_ge(s_mod, ADA_TILES)
            residual(0, (UP_TILES + 5, IN0))

            norm(1)
            rest_quarters(IN0 + 1, range(4))
            v.memset(XC[:, :, 0:3], 0.0)
            v.tensor_copy(XCs[:, :, :, 0:3], cst3[:, :, :].rearrange("p c (b i) -> p c b i", b=NB))
            for q in range(CC):
                if q in (4, 8):
                    rest_quarters(IN0 + 1 + q // 4, range(4))
                dve.wait_ge(s_win, q + 1)
                v.tensor_copy(XC[:, q, 3:3 + SEQ], ps[q % 8][:, 0:SEQ])
                v.tensor_copy(XCs[:, q, :, 3:7], bt(ps[q % 8][:, SEQ:TOK])).then_inc(s_xc, 1)
            for grp in range(3):
                rest_quarters(IN0 + 4 + grp, range(4))
                dve.wait_ge(s_xc, 4 * grp + 4)
                for tap in range(CONV):
                    for j in range(4):
                        cc, op = 4 * grp + j, 16 * grp + 4 * tap + j
                        src, w = XC[:, cc, tap:tap + YW], cw[:, CC * tap + cc:CC * tap + cc + 1]
                        if tap == 0:
                            if grp:
                                dve.wait_ge(s_csil, cc - 3)
                            ins = v.tensor_scalar(Yb[:, j, 0:YW], src, w, None, ALU.mult)
                        else:
                            dve.wait_ge(s_conv, op - 3)
                            ins = v.scalar_tensor_tensor(Yb[:, j, 0:YW], src, w, Yb[:, j, 0:YW], ALU.mult, ALU.add)
                        ins.then_inc(s_conv, 1)
            dve.wait_ge(s_cst2, 16)
            dve.wait_ge(s_ab, 1)
            dve.wait_ge(s_pab, 32)
            own(v.tensor_scalar(sc8[0:8, 0, :], abT[:, :], pab[:, 0:1], None, ALU.add))
            v.scalar_tensor_tensor(sc8[0:8, 1, :], sc8[0:8, 0, :], -1.0, sc8[0:8, 0, :], ALU.mult, ALU.min).then_inc(s_absx, 1)

            dve.wait_ge(s_sp, 1)
            own(v.scalar_tensor_tensor(sc8[0:8, 0, :], sc8[0:8, 0, :], 0.0, sc8[0:8, 1, :], ALU.max, ALU.add))
            own(v.tensor_scalar(sc8[0:8, 0, :], sc8[0:8, 0, :], pab[:, 2:3], -1.0, ALU.mult, ALU.mult))
            for i in range(2):
                ins = v.tensor_tensor(gE[0:8, i, :].rearrange("p (h n) -> p h n", h=HG),
                                      sc8[0:8, 2 * i, SEQ:TOK].unsqueeze(1).to_broadcast([8, HG, NS]),
                                      cst("mh8")[0:8, :].rearrange("p (h n) -> p h n", h=HG), ALU.mult)
            ins.then_inc(s_g8, 1)
            dve.wait_ge(s_win, 29)
            v.tensor_copy(cgat[:, :, 0:3], XC[:, :, SEQ:SEQ + 3])
            v.tensor_copy(cgat[:, :, 3:27].rearrange("p c (b i) -> p c b i", b=NB), XCs[:, :, :, 4:7]).then_inc(s_cg, 1)

            dve.wait_ge(s_gT, 1)
            own(v.tensor_copy(GB, ps[7][:, 0:48].rearrange("p (a b) -> p a b", a=6)))
            for dst, i, r in ((G9, 0, 0), (B9, 3, 4)):
                v.tensor_copy(dst[:, 0:4], GB[:, i, r:r + 4])
                v.tensor_copy(dst[:, 4:8], GB[:, i + 1, r:r + 4])
                ins = v.tensor_reduce(dst[:, 8:9], GB[:, i + 2, r:r + 4], AX_X, ALU.add)
            ins.then_inc(s_gbc, 1)
            for q in range(1, 6, 2):
                dve.wait_ge(s_kvT, q + 1)
                n = P if q < 4 else NS
                if q == 5:
                    v.tensor_copy(vown[:, :], ps[q][0:n, :])
                v.tensor_copy(vtok[0:n, q // 2, :], ps[q][0:n, :]).then_inc(s_kvd, 1)
            for r in range(3):
                dve.wait_ge(s_cvT, r + 1)
                v.tensor_copy(cout[0:27, 512 * r:512 * r + 512], ps[(6, 7, 0)[r]][0:27, :]).then_inc(s_cvo, 1)

            v.sem_inc(s_ktD, 2)
            v.sem_inc(s_lev, 1)

            def normalise(s):
                if 1 <= s <= HM:
                    x = s - 1
                    dve.wait_ge(s_pexp, x + 1)
                    sums = patt[:, 16 + 2 * x:18 + 2 * x]
                    own(v.reciprocal(sums, sums))
                    v.tensor_scalar(psP[:, x % 2, 0:P], psP[:, x % 2, 0:P], sums[:, 0:1], None, ALU.mult)
                    v.tensor_scalar(psP[:, x % 2, P:3 * P], psP[:, x % 2, P:3 * P], sums[:, 1:2], None, ALU.mult).then_inc(s_pn, 1)

            def biased(s):
                if s < HM:
                    dve.wait_ge(s_sc, s + 1)
                    if s >= 2:
                        dve.wait_ge(s_pexp, s - 1)
                    v.scalar_tensor_tensor(psS[:, s % 2, :], cst("dist"), 2.0 ** -(s + 1), ps[5][:, 0:3 * P],
                                           ALU.mult, ALU.add).then_inc(s_paS, 1)
                    dve.wait_ge(s_paS, s + 1)
                    v.tensor_reduce(patt[:, 2 * s:2 * s + 1], psS[:, s % 2, 0:P], AX_X, ALU.max, negate=True)
                    v.tensor_reduce(patt[:, 2 * s + 1:2 * s + 2], psS[:, s % 2, P:3 * P], AX_X, ALU.max, negate=True).then_inc(s_nm, 1)
                if 2 < s < HM + 2 and s % 2:
                    c = (s - 2) // 2
                    dve.wait_ge(s_pav, 2 * c + 2)
                    v.tensor_copy(mix[:, 4 + c, 0:SEQ], ps[7][:, 0:SEQ]).then_inc(s_pao, 1)

            def block_logits(n):
                g, blk = n // NBLK, n % NBLK
                dve.wait_ge(s_qk, 4 * n + 6)
                b = ps[4][:, 0:BLK]
                at, one = slice(blk * BLK, (blk + 1) * BLK), slice(blk, blk + 1)
                v.tensor_reduce(gts[:, g, one], b, AX_X, ALU.add)
                v.tensor_tensor(S[:, g, at], b, cst("biasS")[:, at], ALU.add).then_inc(s_lev, 1)
                dve.wait_ge(s_lev, n + 2)
                v.tensor_reduce(bmx[:, g, one], S[:, g, at], AX_X, ALU.max).then_inc(s_bmx, 1)

            def selection(g):
                dve.wait_ge(s_bmx, NBLK * (g + 1))
                other = gts[:, g, :].unsqueeze(1).to_broadcast([P, NBLK, NBLK])
                mine = gts[:, g, :].unsqueeze(2).to_broadcast([P, NBLK, NBLK])
                A8 = cmpA.rearrange("p (n m) -> p n m", n=NBLK)
                B8 = cmpB.rearrange("p (n m) -> p n m", n=NBLK)
                v.tensor_tensor(A8, other, mine, ALU.is_gt)
                own(v.tensor_tensor(B8, other, mine, ALU.is_equal))
                own(v.tensor_tensor(cmpB, cmpB, cst("lower8"), ALU.mult))
                own(v.tensor_tensor(cmpA, cmpA, cmpB, ALU.add))
                own(v.tensor_reduce(cnt, A8, AX_X, ALU.add))
                own(v.tensor_scalar(pen[:, g, 0:NBLK], cnt, TOPK - 0.5, NEG, ALU.is_ge, ALU.mult))
                v.tensor_tensor(bmx[:, g, 0:NBLK], bmx[:, g, 0:NBLK], pen[:, g, 0:NBLK], ALU.add)
                dve.wait_ge(s_owns, 1)
                own(v.tensor_reduce(bmx[:, g, NBLK:NBLK + 1], sown[:, g, :], AX_X, ALU.max))
                own(v.tensor_reduce(negm[:, g:g + 1], bmx[:, g, :], AX_X, ALU.max, negate=True))
                v.tensor_copy(pen[:, g, NBLK:NBLK + 1], negm[:, g:g + 1])
                v.tensor_scalar(pen[:, g, 0:NBLK], pen[:, g, 0:NBLK], negm[:, g:g + 1], None, ALU.add).then_inc(s_pen, 1)

            def scaled(g):
                own(v.tensor_reduce(rin[:, 2 * g:2 * g + 1], rsum[:, g, :], AX_X, ALU.add))
                own(v.reciprocal(rin[:, 2 * g + 1:2 * g + 2], rin[:, 2 * g:2 * g + 1]))
                dve.wait_ge(s_O, g + 1)
                v.scalar_tensor_tensor(Om, ps[7][:, :], rin[:, 2 * g + 1:2 * g + 2], cst("hmask"), ALU.mult, ALU.mult).then_inc(s_om, 1)

            def into_mix(g):
                dve.wait_ge(s_AT, g + 1)
                v.tensor_copy(mix[:, 4:8, SEQ + 16 * g:SEQ + 16 * g + 16],
                              ps[6][:, 64 * g:64 * g + 64].rearrange("p (c n) -> p c n", c=4)).then_inc(s_mixa, 1)

            def values(n):
                if n == NBLK + 1:
                    scaled(0)
                if n == NBLK + 2:
                    into_mix(0)
                if n == 2 * NBLK:
                    scaled(1)
                    return
                g, blk = n // NBLK, n % NBLK
                if blk == 0:
                    dve.wait_ge(s_oT, g + 1)
                    v.tensor_copy(ownT[0:32, g, :], ps[6][0:32, BLK + P * g:BLK + P * g + P]).then_inc(s_oTs, 1)
                dve.wait_ge(s_PT, n + 1)
                if n >= 2:
                    dve.wait_ge(s_PV, 2 * n - 2)
                v.tensor_copy(pT[:, n % 2].rearrange("p a b -> p (a b)"), ps[5][:, 0:BLK]).then_inc(s_pTs, 1)

            dve.wait_ge(s_csil, CC)
            dve.wait_ge(s_own, 1)
            v.tensor_tensor(sown.rearrange("p g n -> p (g n)"), ps[6][:, 384:448], cst("biasO"), ALU.add).then_inc(s_owns, 1)
            for m in range(4 * 2 * NBLK):
                dve.wait_ge(s_kt, 2 * m + 2)
                dve.wait_ge(s_qk, m + 1)
                v.tensor_copy(ktb[:, m % 2, 1, :], ps[2 * (m % 2) + 1][:, :]).then_inc(s_ktD, 1)
                n = m // 4
                if m % 4 == 0 and n:
                    block_logits(n - 1)
                    if n == NBLK:
                        selection(0)
                elif m % 4 == 1:
                    normalise(n)
                    if n == 2 * NBLK - 1:
                        values(0)
                elif m % 4 == 2:
                    biased(n)
                elif 9 <= n < 13:
                    for x in range(2):
                        c = 2 * (n - 9) + x
                        dve.wait_ge(s_l2, c + 1)
                        v.tensor_scalar(RS[:, c, :], ps[5 + x][:, 0:TOK], EPS, None, ALU.add).then_inc(s_l2e, 1)
                elif n == 2 * NBLK - 1:
                    v.tensor_copy(Pv, G9.unsqueeze(2).to_broadcast([P, NPROB, P])).then_inc(s_gbc, 1)
            block_logits(2 * NBLK - 1)

            def filled(step):
                k = STEPS[step]
                dve.wait_ge(s_gp, k + 1)
                return ps[k % GBANKS]

            def grp3(b, g):
                n = len(probs(g))
                return b[:, 0:n * P].rearrange("p (a b) -> p a b", a=n)

            def sel(x, g):
                return x[:, probs(g)[0]:probs(g)[-1] + 1]

            v.tensor_copy(cum, filled(("cum",))[:, 0:18]).then_inc(s_ge, 1)
            values(1)
            dve.wait_ge(s_okv, 96)
            for g in range(3):
                v.tensor_copy(sel(gR, g), grp3(filled(("row", g)), g)).then_inc(s_ge, 1)
            dve.wait_ge(s_rse, 2)
            v.scalar_tensor_tensor(QK[:, 0:4, :], Cv[:, 0:4, :], P ** -0.5, RS[:, 0:4, :], ALU.mult, ALU.mult)
            own(v.tensor_tensor(QK[:, 4:8, :], Cv[:, 4:8, :], RS[:, 4:8, :], ALU.mult))
            for i, src in enumerate((QK[:, 0:4], QK[:, 4:8], Cv[:, 8:12])):
                ins = v.tensor_copy(smp[:, i, :].rearrange("p (h n) -> p h n", h=HG), src[:, :, SEQ:TOK])
            ins.then_inc(s_qkn, 1)
            values(2)
            dve.wait_ge(*copied(("row", 2)))
            for p in range(NPROB):
                ins = v.tensor_scalar(DT[:, p, :], gR[:, p, :], cum[:, p:p + 1], 0.0, ALU.subtract, ALU.min)
            ins.then_inc(s_df, 1)
            dve.wait_ge(s_ecum, 1)
            v.tensor_tensor(bek, B9, ecum[:, 0:NPROB], ALU.mult).then_inc(s_bek, 1)
            dve.wait_ge(s_bek, 1)
            for j in range(3):
                b = filled(("kt", j))
                for x, p in enumerate(probs(j)):
                    v.tensor_scalar(KB[:, p, :], b[:, x * P:(x + 1) * P], bek[:, p:p + 1], None, ALU.mult)
                    ins = v.tensor_scalar(KDc[:, p, :], b[:, x * P:(x + 1) * P], ecum[:, 9 + p:10 + p], None, ALU.mult)
                ins.then_inc(s_ge, 1)
            values(3)
            for j in range(3):
                v.tensor_tensor(sel(VB, j), grp3(filled(("vt", j)), j), sel(B9, j).unsqueeze(2).to_broadcast([P, len(probs(j)), P]),
                                ALU.mult).then_inc(s_ge, 1)
            dve.wait_ge(s_dt, 1)
            v.tensor_tensor(DT[:, 0:8, :], DT[:, 0:8, :], tri.unsqueeze(1).to_broadcast([P, 8, P]), ALU.mult)
            own(v.tensor_tensor(DT[:, 8, :], DT[:, 8, :], triS, ALU.mult))
            values(4)
            for j in range(5):
                n = min(2, NPROB - 2 * j)
                b = filled(("gram", j))[:, 0:2 * P * n].rearrange("p (x i t) -> p x i t", x=n, i=2)
                v.tensor_tensor(AN[:, 2 * j:2 * j + n], b, DT[:, 2 * j:2 * j + n, :].unsqueeze(2).to_broadcast([P, n, 2, P]),
                                ALU.mult).then_inc(s_ge, 1)
            dve.wait_ge(*copied(("gram", 4)))

            def level_mask(l):
                for g in range(3 if l < 2 else 2):
                    n = len(probs(g))
                    v.tensor_tensor(sel(NTl, g), sel(AN, g)[:, :, 1, :], lev[:, l, :].unsqueeze(1).to_broadcast([P, n, P]),
                                    ALU.mult).then_inc(s_ntl, 1)

            level_mask(0)
            values(5)
            selection(1)
            v.tensor_tensor(QD[:, 4:8, :], QK[:, 0:4, P:SEQ], EG[:, 4:8, :], ALU.mult)

            def sample(l):
                if l == 1:
                    hbt = "p (h b t) -> p h b t"
                    own(v.memset(QKf, 0.0))
                    v.tensor_tensor(WXd[1], smp[:, 0, :].rearrange(hbt, h=HG, b=NB), EG[:, 8, :].rearrange(hbt, h=HG, b=NB), ALU.mult)
                    v.tensor_copy(WXd[0], filled(("W", 2))[:, 0:P].rearrange(hbt, h=HG, b=NB)).then_inc(s_ge, 1)
                elif l == 2:
                    v.tensor_copy(VN[:, 8, :], filled(("us",))[:, 0:P]).then_inc(s_ge, 1)
                    b = filled(("ws",))
                    dve.wait_ge(*copied(("us",)))
                    v.tensor_copy(VX[:, 1, :], b[:, P:2 * P])
                    v.tensor_tensor(VN[:, 8, :], VN[:, 8, :], b[:, 0:P], ALU.subtract).then_inc(s_ge, 1)
                elif l == 3:
                    v.tensor_copy(goT[:, :, SEQ:TOK], filled(("os",))[:, 0:P].rearrange("p (h n) -> p h n", h=HG)).then_inc(s_ge, 1)
                    dve.wait_ge(*copied(("os",)))
                    v.tensor_tensor(VX[:, 0:NB, :], VN[:, 8, :].unsqueeze(1).to_broadcast([P, NB, P]),
                                    cst("bdm").unsqueeze(2).to_broadcast([P, NB, P]), ALU.mult).then_inc(s_vx, 1)
                elif l in (4, 5):
                    for k in range(4 * l - 16, 4 * l - 12):
                        b = filled(("up", k))
                        for x in range(4):
                            hh, s = k // 2, 4 * (k % 2) + x
                            last = NT * (NB * hh + s) + NT - 1
                            ins = v.scalar_tensor_tensor(st[hh][:, s, :], st[hh][:, s, :], EG[:, 8, last:last + 1], b[:, x * P:(x + 1) * P],
                                                         ALU.mult, ALU.add)
                        ins.then_inc(s_ge, 1)

            for l in range(7):
                groups = range(3 if l < 2 else 2)
                for g in groups:
                    v.tensor_tensor(sel(Pv, g), grp3(filled(("P", l, g)), g),
                                    sel(B9, g).unsqueeze(2).to_broadcast([P, len(probs(g)), P]), ALU.mult).then_inc(s_ge, 1)
                if l < 6:
                    level_mask(l + 1)
                if l < 6:
                    values(6 + 2 * l)
                for g in groups:
                    if l == 0:
                        idb = ident.unsqueeze(1).to_broadcast([P, len(probs(g)), P])
                        dve.wait_ge(*copied(("P", 0, g)))
                        v.tensor_tensor(sel(X, g), idb, sel(Pv, g), ALU.subtract)
                        v.tensor_tensor(sel(XT, g), idb, grp3(filled(("PX", 0, g)), g), ALU.subtract).then_inc(s_ge, 1)
                        continue
                    if l < 6:
                        v.tensor_tensor(sel(X, g), sel(X, g), grp3(filled(("XP", l, g)), g), ALU.subtract).then_inc(s_ge, 1)
                    v.tensor_tensor(sel(XT, g), sel(XT, g), grp3(filled(("PX", l, g)), g), ALU.subtract).then_inc(s_ge, 1)
                if l < 5:
                    values(7 + 2 * l)
                sample(l)
            v.tensor_scalar(WT[:, 4:8, :], grp3(filled(("W", 1)), 1), -1.0, None, ALU.mult).then_inc(s_ge, 1)
            v.tensor_copy(VN[:, 0:4, :], grp3(filled(("U0",)), 0)).then_inc(s_ge, 1)
            v.tensor_copy(S1, grp3(filled(("S1",)), 0)).then_inc(s_ge, 1)
            v.tensor_copy(VN[:, 4:8, :], grp3(filled(("V1",)), 0)).then_inc(s_ge, 1)
            v.tensor_copy(goT[:, :, 0:P], grp3(filled(("o0",)), 0)).then_inc(s_ge, 1)
            v.tensor_copy(goT[:, :, P:SEQ], grp3(filled(("o1",)), 0)).then_inc(s_ge, 1)
            b = filled(("S2",))
            for x in range(HG):
                ins = v.scalar_tensor_tensor(S1[:, x, :], S1[:, x, :], EG[:, 4 + x, P - 1:P], b[:, x * P:(x + 1) * P],
                                             ALU.mult, ALU.add)
            ins.then_inc(s_ge, 1)
            into_mix(1)
            for hh in range(HG):
                v.tensor_scalar(sqg[:, HG + hh, :], filled(("rms", hh))[:, 0:TOK], 1.0 / P, EPS, ALU.mult, ALU.add).then_inc(s_ge, 1)
            dve.wait_ge(s_gr, 1)
            own(v.scalar_tensor_tensor(goT, goT, gnw, sqg[:, HG:8, :], ALU.mult, ALU.mult))
            v.tensor_tensor(mix[:, 0:HG, :], goT, zs, ALU.mult).then_inc(s_gdn, 1)

            residual(1, (S1ST,))

            norm(2)
            dve.wait_ge(s_out, 16 * HG)
            for j in range(3):
                rest_quarters(S1ST + j + 1, (0, 1, 2))
                hidden(1, 2 * j, 0)
                rest_quarters(S1ST + j + 1, (3,))
                hidden(1, 2 * j + 1, 1)
            with dve.Fori(0, 2) as i:
                for k in range(4):
                    rest_quarters(S1ST + 4 + k, (0, 1, 2), i, 4)
                    hidden(1, i * 8 + (6 + 2 * k), 0)
                    rest_quarters(S1ST + 4 + k, (3,), i, 4)
                    hidden(1, i * 8 + (7 + 2 * k), 1)
            for u in range(S1ST + UP_TILES + 1, len(split) - 1):
                rest_quarters(u, range(4))
            residual(2, (len(split) - 1,))
            norm(3)
            for t in range(1, 6, 2):
                dve.wait_ge(s_yT, t + 1)
                n = NS if t % 3 == 2 else P
                v.tensor_copy(ytok[0:n, t % 3, 512 * (t // 3):512 * (t // 3) + 512], ps[1 + t][0:n, :]).then_inc(s_y[t // 3], 1)


OUT_SHAPES = [("y_prompt", (1, SEQ, D)), ("y_sample", (NB, NT, D)), ("k_prompt", (1, 1, SEQ, HM, HD)), ("v_prompt", (1, 1, SEQ, HM, HD)),
              ("gdn_prompt", (1, 1, HG, P, P)), ("conv_prompt", (1, 1, 3, CC * P)), ("k_sample", (1, NB, NT, HM, HD)),
              ("v_sample", (1, NB, NT, HM, HD)), ("gdn_sample", (1, NB, HG, P, P)), ("conv_sample", (1, NB, 3, CC * P))]


def kernel(**inputs):
    import concourse.bacc as bacc
    from concourse.bass_utils import run_bass_kernel_spmd

    nc = bacc.Bacc("TRN2", target_bir_lowering=False, num_devices=1)
    arrays = {n: np.ascontiguousarray(x) for n, x in inputs.items() if n != "page_table"}
    table = np.asarray(inputs["page_table"]).reshape(2, NB // 2, NBLK, 2).transpose(0, 2, 1, 3)
    arrays["ptab"] = np.ascontiguousarray(table.reshape(1, 2 * PHASE))
    arrays["consts"] = make_consts()
    a = {n: nc.dram_tensor("in_" + n, x.shape, I32 if n == "ptab" else F32, kind="ExternalInput").ap() for n, x in arrays.items()}
    o = {n: nc.dram_tensor("out_" + n, shape, F32, kind="ExternalOutput").ap() for n, shape in OUT_SHAPES}
    build_program(nc, a, o)
    r = run_bass_kernel_spmd(nc, [{"in_" + n: x for n, x in arrays.items()}], core_ids=[0])
    return tuple(r.results[0]["out_" + n] for n, _ in OUT_SHAPES)
```
